# Optimizing a Trainium2 kernel written in Bass

```python
import jax, jax.numpy as jnp
from jax import lax
import numpy as np

D_MODEL = 1024
BATCH = 1
SEQ = 1024
DEPTH = 1
DEC_BATCH = 8
DEC_SEQ = 1
PAST_LEN = 8192
PAGE_SIZE = 128

N_META = 16
MIX_WIDTH = D_MODEL
CONV_WIDTH = MIX_WIDTH // 2
CONV_K = 3
RWKV_WIDTH = MIX_WIDTH - CONV_WIDTH
RWKV_HEAD = 64
RWKV_HEADS = RWKV_WIDTH // RWKV_HEAD
W_LORA = 32
A_LORA = 32
G_LORA = 96
RW_COLS = 3 * RWKV_WIDTH + W_LORA + A_LORA + G_LORA
IN_COLS = 3 * CONV_WIDTH + RW_COLS
PEER_HEADS = 8
N_KEYS = 128
N_EXPERTS = N_KEYS * N_KEYS
PEER_TOPK = 16
QUERY_DIM = 256
HALF = QUERY_DIM // 2
PEER_BLOCK = 128
LN_EPS = 1e-5
GN_EPS = RWKV_HEAD * 1e-5
ALPHA = (2 * DEPTH) ** 0.25
BETA = (8 * DEPTH) ** -0.25

kernel_name = 'hymba_conv_rwkv7_peer_step'

def layer_norm(x, g, b, eps=LN_EPS):
    xf = x.astype(jnp.float32)
    m = jnp.mean(xf, axis=-1, keepdims=True)
    var = jnp.mean(jnp.square(xf - m), axis=-1, keepdims=True)
    return ((xf - m) * lax.rsqrt(var + eps) * g + b).astype(x.dtype)

def wkv_scan(state, r, w, k, v, kk, a):
    def step(s, inp):
        r_t, w_t, k_t, v_t, kk_t, a_t = inp
        sa = jnp.einsum('bhvk,bhk->bhv', s, -kk_t)
        s = (s * w_t[:, :, None, :] + sa[..., None] * (kk_t * a_t)[:, :, None, :]
             + v_t[..., None] * k_t[:, :, None, :])
        return s, jnp.einsum('bhvk,bhk->bhv', s, r_t)
    xs = tuple(jnp.moveaxis(t, 1, 0) for t in (r, w, k, v, kk, a))
    s_fin, o = lax.scan(step, state, xs)
    return jnp.moveaxis(o, 0, 1), s_fin

def short_conv_group(p_cv, conv_buf, conv_w):
    S = p_cv.shape[1]
    bg, cg, hv = jnp.split(p_cv, 3, axis=-1)
    z = cg * hv
    zp = jnp.concatenate([conv_buf.astype(z.dtype), z], axis=1)
    conv = sum(conv_w[j] * zp[:, j:j + S] for j in range(CONV_K))
    return bg * conv, zp[:, -(CONV_K - 1):]

def rwkv7_group(p_rw, prev_rw, state, mu, w0, w_up, a0, a_up, g_up, k_k, k_a, r_k, gn_g, gn_b):
    B, S, _ = p_rw.shape
    f32 = jnp.float32
    shifted = jnp.concatenate([prev_rw[:, None, :], p_rw[:, :-1]], axis=1)
    m = p_rw + (shifted - p_rw) * mu
    cuts = [RWKV_WIDTH, 2 * RWKV_WIDTH, 3 * RWKV_WIDTH, 3 * RWKV_WIDTH + W_LORA,
            3 * RWKV_WIDTH + W_LORA + A_LORA]
    r, k, v, wd, ad, gd = jnp.split(m, cuts, axis=-1)
    w_log = -jax.nn.softplus(-(w0 + jnp.tanh(wd) @ w_up).astype(f32)) - 0.5
    decay = jnp.exp(-jnp.exp(w_log))
    a = jax.nn.sigmoid((a0 + ad @ a_up).astype(f32))
    g = jax.nn.sigmoid(gd) @ g_up
    heads = lambda t: t.astype(f32).reshape(B, S, RWKV_HEADS, RWKV_HEAD)
    r, k, v, decay, a = heads(r), heads(k), heads(v), heads(decay), heads(a)
    kk = k * k_k.astype(f32).reshape(RWKV_HEADS, RWKV_HEAD)
    kk = kk / jnp.maximum(jnp.sqrt(jnp.sum(kk * kk, axis=-1, keepdims=True)), 1e-12)
    k = k * (1.0 + (a - 1.0) * k_a.astype(f32).reshape(RWKV_HEADS, RWKV_HEAD))
    o, s_new = wkv_scan(state.astype(f32), r, decay, k, v, kk, a)
    om = jnp.mean(o, axis=-1, keepdims=True)
    ov = jnp.mean(jnp.square(o - om), axis=-1, keepdims=True)
    o = ((o - om) * lax.rsqrt(ov + GN_EPS) * gn_g.reshape(RWKV_HEADS, RWKV_HEAD)
         + gn_b.reshape(RWKV_HEADS, RWKV_HEAD))
    o = o + jnp.sum(r * k * r_k.astype(f32), axis=-1, keepdims=True) * v
    y = o.reshape(B, S, RWKV_WIDTH).astype(p_rw.dtype) * g
    return y, s_new

def peer_ffn(x, w_q, sub_keys, peer_u, peer_v):
    B, S, D = x.shape
    T = B * S
    xt = x.reshape(T, D)
    q = (xt @ w_q).astype(jnp.float32).reshape(T, PEER_HEADS, 2, HALF)
    sc = jnp.einsum('thpd,hpnd->thpn', q, sub_keys.astype(jnp.float32))
    s_top, i_top = lax.top_k(sc, PEER_TOPK)
    cand = (s_top[:, :, 0, :, None] + s_top[:, :, 1, None, :]).reshape(T, PEER_HEADS, PEER_TOPK * PEER_TOPK)
    cidx = (i_top[:, :, 0, :, None] * N_KEYS + i_top[:, :, 1, None, :]).reshape(T, PEER_HEADS, PEER_TOPK * PEER_TOPK)
    best, pos = lax.top_k(cand, PEER_TOPK)
    idx = jnp.take_along_axis(cidx, pos, axis=-1).reshape(T, PEER_HEADS * PEER_TOPK)
    gate = jax.nn.softmax(best, axis=-1).reshape(T, PEER_HEADS * PEER_TOPK).astype(x.dtype)
    n_blk = -(-T // PEER_BLOCK)
    pad = n_blk * PEER_BLOCK - T
    xb = jnp.pad(xt, ((0, pad), (0, 0))).reshape(n_blk, PEER_BLOCK, D)
    ib = jnp.pad(idx, ((0, pad), (0, 0))).reshape(n_blk, PEER_BLOCK, -1)
    gb = jnp.pad(gate, ((0, pad), (0, 0))).reshape(n_blk, PEER_BLOCK, -1)

    def block(args):
        xc, ic, gc = args
        hu = jnp.einsum('tkd,td->tk', peer_u[ic], xc)
        act = jax.nn.gelu(hu, approximate=False) * gc
        return jnp.einsum('tk,tkd->td', act, peer_v[ic])

    out = lax.map(block, (xb, ib, gb)).reshape(n_blk * PEER_BLOCK, D)[:T]
    return out.reshape(B, S, D)

def decoder_layer(h, shift_prev, conv_buf, wkv, lp):
    (w_in, conv_w, mu, w0, w_up, a0, a_up, g_up, k_k, k_a, r_k, gn_g, gn_b, w_o,
     ln1_g, ln1_b, w_q, sub_keys, peer_u, peer_v, ln2_g, ln2_b) = lp
    proj = h @ w_in
    prev_rw = shift_prev.astype(h.dtype) @ w_in[:, 3 * CONV_WIDTH:]
    y_cv, conv_new = short_conv_group(proj[..., :3 * CONV_WIDTH], conv_buf, conv_w)
    y_rw, wkv_new = rwkv7_group(proj[..., 3 * CONV_WIDTH:], prev_rw, wkv, mu, w0, w_up, a0, a_up,
                                g_up, k_k, k_a, r_k, gn_g, gn_b)
    mix = jnp.concatenate([y_cv, y_rw], axis=-1) @ w_o
    h1 = layer_norm(ALPHA * h + mix, ln1_g, ln1_b)
    h2 = layer_norm(ALPHA * h1 + peer_ffn(h1, w_q, sub_keys, peer_u, peer_v), ln2_g, ln2_b)
    return h2, h[:, -1], conv_new, wkv_new

def trunk(h, shift0, conv0, wkv0, params):
    shifts, convs, wkvs = [], [], []
    for l in range(DEPTH):
        lp = tuple(p[l] for p in params)
        h, s_new, c_new, w_new = decoder_layer(h, shift0[l], conv0[l], wkv0[l], lp)
        shifts.append(s_new.astype(h.dtype))
        convs.append(c_new.astype(h.dtype))
        wkvs.append(w_new.astype(h.dtype))
    return h, jnp.stack(convs), jnp.stack(shifts), jnp.stack(wkvs)

def setup_inputs(seed: int = 0) -> dict:
    key = jax.random.key(seed)
    ks = jax.random.split(key, 32)
    f32 = jnp.float32
    nrm = lambda k, shape, s: jax.random.normal(k, shape, f32) * s
    L = DEPTH
    return {
        'x_prompt': nrm(ks[0], (BATCH, SEQ, D_MODEL), 1.0),
        'x_sample': nrm(ks[1], (DEC_BATCH, DEC_SEQ, D_MODEL), 1.0),
        'state_conv': nrm(ks[2], (L, DEC_BATCH, CONV_K - 1, CONV_WIDTH), 0.5),
        'state_shift': nrm(ks[3], (L, DEC_BATCH, D_MODEL), 1.0),
        'state_wkv': nrm(ks[4], (L, DEC_BATCH, RWKV_HEADS, RWKV_HEAD, RWKV_HEAD), 0.3),
        'meta_tokens': nrm(ks[5], (N_META, D_MODEL), 1.0),
        'ln_in_g': 1.0 + nrm(ks[6], (D_MODEL,), 0.02),
        'ln_in_b': nrm(ks[7], (D_MODEL,), 0.02),
        'w_in': nrm(ks[8], (L, D_MODEL, IN_COLS), D_MODEL ** -0.5),
        'conv_w': nrm(ks[9], (L, CONV_K, CONV_WIDTH), CONV_K ** -0.5),
        'mu': jax.random.uniform(ks[10], (L, RW_COLS), f32),
        'w0': jax.random.uniform(ks[11], (L, RWKV_WIDTH), f32, -3.0, 2.0),
        'w_up': nrm(ks[12], (L, W_LORA, RWKV_WIDTH), 0.5 * W_LORA ** -0.5),
        'a0': nrm(ks[13], (L, RWKV_WIDTH), 0.5),
        'a_up': nrm(ks[14], (L, A_LORA, RWKV_WIDTH), A_LORA ** -0.5),
        'g_up': nrm(ks[15], (L, G_LORA, RWKV_WIDTH), G_LORA ** -0.5),
        'k_k': 0.85 + nrm(ks[16], (L, RWKV_WIDTH), 0.05),
        'k_a': 1.0 + nrm(ks[17], (L, RWKV_WIDTH), 0.05),
        'r_k': nrm(ks[18], (L, RWKV_HEADS, RWKV_HEAD), 0.1),
        'gn_g': 1.0 + nrm(ks[19], (L, RWKV_WIDTH), 0.02),
        'gn_b': nrm(ks[20], (L, RWKV_WIDTH), 0.02),
        'w_o': nrm(ks[21], (L, MIX_WIDTH, D_MODEL), BETA * MIX_WIDTH ** -0.5),
        'ln1_g': 1.0 + nrm(ks[22], (L, D_MODEL), 0.02),
        'ln1_b': nrm(ks[23], (L, D_MODEL), 0.02),
        'w_q': nrm(ks[24], (L, D_MODEL, PEER_HEADS * QUERY_DIM), D_MODEL ** -0.5),
        'sub_keys': nrm(ks[25], (L, PEER_HEADS, 2, N_KEYS, HALF), HALF ** -0.5),
        'peer_u': nrm(ks[26], (L, N_EXPERTS, D_MODEL), D_MODEL ** -0.5),
        'peer_v': nrm(ks[27], (L, N_EXPERTS, D_MODEL), BETA),
        'ln2_g': 1.0 + nrm(ks[28], (L, D_MODEL), 0.02),
        'ln2_b': nrm(ks[29], (L, D_MODEL), 0.02),
    }

def reference(x_prompt, x_sample, state_conv, state_shift, state_wkv, meta_tokens, ln_in_g, ln_in_b,
              w_in, conv_w, mu, w0, w_up, a0, a_up, g_up, k_k, k_a, r_k, gn_g, gn_b, w_o,
              ln1_g, ln1_b, w_q, sub_keys, peer_u, peer_v, ln2_g, ln2_b):
    params = (w_in, conv_w, mu, w0, w_up, a0, a_up, g_up, k_k, k_a, r_k, gn_g, gn_b, w_o,
              ln1_g, ln1_b, w_q, sub_keys, peer_u, peer_v, ln2_g, ln2_b)
    dt = x_prompt.dtype
    meta = jnp.broadcast_to(meta_tokens.astype(dt)[None], (BATCH, N_META, D_MODEL))
    hp = layer_norm(jnp.concatenate([meta, x_prompt], axis=1), ln_in_g, ln_in_b)
    z_shift = jnp.zeros((DEPTH, BATCH, D_MODEL), dt)
    z_conv = jnp.zeros((DEPTH, BATCH, CONV_K - 1, CONV_WIDTH), dt)
    z_wkv = jnp.zeros((DEPTH, BATCH, RWKV_HEADS, RWKV_HEAD, RWKV_HEAD), jnp.float32)
    hp, p_conv, p_shift, p_wkv = trunk(hp, z_shift, z_conv, z_wkv, params)
    y_prompt = hp[:, N_META:]
    hs = layer_norm(x_sample, ln_in_g, ln_in_b)
    y_sample, s_conv, s_shift, s_wkv = trunk(hs, state_shift, state_conv, state_wkv, params)
    return (y_prompt, y_sample, p_conv, p_shift, p_wkv, s_conv, s_shift, s_wkv)


_drawn_inputs = setup_inputs


def setup_inputs(seed=0):
    import zlib

    import numpy as np

    out = dict(_drawn_inputs(seed))
    spreads = {}
    factors = {'k_k': 3.203, 'gn_g': 3.309, 'gn_b': 3.445, 'ln2_g': 2.708, 'ln2_b': 2.929}
    for name, (base, spread) in spreads.items():
        noise = np.random.default_rng([zlib.crc32(name.encode()), seed]).standard_normal(out[name].shape)
        drawn = base * np.exp(spread * noise) if base else spread * noise
        out[name] = __import__('jax').numpy.asarray(drawn.astype(out[name].dtype))
    for name, factor in factors.items():
        out[name] = (out[name] * factor).astype(out[name].dtype)
    return out
```

```python
from contextlib import ExitStack
import math

import concourse.bass as bass
from concourse import mybir

F32 = mybir.dt.float32
U32 = mybir.dt.uint32
ALU = mybir.AluOpType
ACT = mybir.ActivationFunctionType
AX_X = mybir.AxisListType.X

P = 128
D = 1024
KT = D // P
SEQ = 1024
NS = 8
N_META = 16
CONVW = 512
RW = 512
PAIRS = RW // P
HD = 64
HEADS = 8
W_LORA = A_LORA = 32
G_LORA = 96
IN_COLS = 3 * CONVW + 3 * RW + W_LORA + A_LORA + G_LORA
RW0 = 3 * CONVW
LORA0 = RW0 + 3 * RW
C_META = 2 * NS
C_PROMPT = C_META + N_META
PROJ_COLS = C_PROMPT + SEQ
COLS3 = PROJ_COLS // 3
CHUNK = 64
WKV_OFF = 32
WKV_COLS = PROJ_COLS + WKV_OFF
CHUNKS = WKV_COLS // CHUNK
W_META = C_META + WKV_OFF
LN_EPS = 1e-5
GN_EPS = HD * 1e-5
ALPHA = 2.0 ** 0.25
LOG_DECAY = math.exp(-0.5)
PEER_HEADS = 8
N_KEYS = 128
TOPK = 16
SLOTS = PEER_HEADS * TOPK
TBLOCKS = SEQ // P
NEG = -3.0e38
DEBUG = False


def signals(eng):
    count = {}

    def done(ins, sem):
        count[sem.name] = count.get(sem.name, 0) + 1
        ins.then_inc(sem, 1)
        eng.wait_ge(sem, count[sem.name])
    return done


def chained(eng, sem):
    count = [0]

    def step(ins):
        count[0] += 1
        ins.then_inc(sem, 1)
        eng.wait_ge(sem, count[0])
    return step


def input_phase(nc, t, d):
    ctx = ExitStack()
    with ctx:
        NX = 3
        xrow = ctx.enter_context(nc.sbuf_tensor("xrow", [P, NX, D], F32))
        ln_gb = ctx.enter_context(nc.sbuf_tensor("ln_gb", [P, 2, D], F32))
        stats = ctx.enter_context(nc.sbuf_tensor("stats", [P, NX, 12], F32))
        moments = ctx.enter_context(nc.sbuf_tensor("moments", [P, NX, 2], F32))
        rstd = ctx.enter_context(nc.sbuf_tensor("rstd", [P, NX, 1], F32))
        conv_rows = ctx.enter_context(nc.sbuf_tensor("conv_rows", [2 * NS, CONVW], F32))
        par_rows = ctx.enter_context(nc.sbuf_tensor("par_rows", [PAR_COLS, P], F32))
        turned = ctx.enter_context(nc.psum_tensor("turned", [P, 2, 512], F32))
        turned2 = ctx.enter_context(nc.psum_tensor("turned2", [P, 2, 512], F32))
        sem = lambda n: ctx.enter_context(nc.semaphore(n))
        const_loaded, conv_loaded = sem("const_loaded"), sem("conv_loaded")
        x_loaded = [sem(f"x_loaded{i}") for i in range(NX)]
        shift_loaded, ident_done, var_ready, std_ready = sem("shift_loaded"), sem("ident_done"), sem("var_ready"), sem("std_ready")
        vec_chain, norm_ready, turned_ready, turned_read = sem("vec_chain"), sem("norm_ready"), sem("turned_ready"), sem("turned_read")
        h_stored = t.h_stored
        rows_cleared = sem("rows_cleared")
        block = ctx.enter_context(nc.Block())
        TILES = 1 + TBLOCKS
        rows = [C_PROMPT] + [P] * TBLOCKS

        @block.sync
        def _(sp):
            sp.dma_start(ln_gb[:, 0, :], d["ln_in_g"][None, :].broadcast_to([P, D])).then_inc(const_loaded, 16)
            sp.dma_start(ln_gb[:, 1, :], d["ln_in_b"][None, :].broadcast_to([P, D])).then_inc(const_loaded, 16)
            def load_tile(i):
                s = i % NX
                if i >= NX:
                    sp.wait_ge(turned_ready, 2 * (i - NX + 1))
                    sp.wait_ge(h_stored[s], 16 * (i // NX))
                if i == 0:
                    sp.dma_start(xrow[0:NS, s, :], d["x_sample"][:, 0, :]).then_inc(x_loaded[s], 16)
                    sp.dma_start(xrow[NS:2 * NS, s, :], d["state_shift"][0]).then_inc(x_loaded[s], 16)
                    sp.dma_start(xrow[C_META:C_PROMPT, s, :], d["meta_tokens"]).then_inc(x_loaded[s], 16)
                else:
                    sp.dma_start(xrow[:, s, :], d["x_prompt"][0, (i - 1) * P:i * P, :]).then_inc(x_loaded[s], 16)
            for i in range(NX):
                load_tile(i)
            sp.dma_start(conv_rows[:, :], d["state_conv"][0].rearrange("b j c -> (b j) c")).then_inc(conv_loaded, 16)
            sp.wait_ge(rows_cleared, 1)
            for n in PARAMS:
                src = {"mu_r": d["mu"][0, 0:RW], "mu_k": d["mu"][0, RW:2 * RW], "mu_v": d["mu"][0, 2 * RW:3 * RW],
                       "r_k": d["r_k"][0].rearrange("h k -> (h k)"),
                       "cw0": d["conv_w"][0, 0], "cw1": d["conv_w"][0, 1], "cw2": d["conv_w"][0, 2]}.get(n)
                src = d[n][0] if src is None else src
                r0 = PARAMS.index(n) * PAIRS
                sp.dma_start(par_rows[r0:r0 + PAIRS, :], src.rearrange("(c p) -> c p", p=P)).then_inc(conv_loaded, 16)
            mu1 = d["mu"][0:1, 3 * RW:]
            sp.dma_start(par_rows[PAR_COLS - 2:PAR_COLS - 1, 0:2 * W_LORA], mu1[:, 0:2 * W_LORA]).then_inc(conv_loaded, 16)
            sp.dma_start(par_rows[PAR_COLS - 1:PAR_COLS, 0:G_LORA], mu1[:, 2 * W_LORA:]).then_inc(conv_loaded, 16)
            sp.wait_ge(norm_ready, 1)
            sp.dma_start(xrow[NS:2 * NS, 0, :], d["state_shift"][0]).then_inc(shift_loaded, 16)
            for i in range(NX, TILES):
                load_tile(i)

        @block.gpsimd
        def _(pool):
            done = signals(pool)
            done(pool.memset(t.ident[:, :], 0.0), ident_done)
            done(pool.affine_select(out=t.ident[:, :], in_=t.ident[:, :], compare_op=ALU.not_equal, fill=1.0,
                                    base=0, pattern=[[-1, P]], channel_multiplier=1), ident_done)
            done(pool.memset(t.head_ones[:, :], 0.0), ident_done)
            done(pool.memset(t.head_ones[0:HD, 0:HD], 1.0), ident_done)
            done(pool.memset(t.head_ones[HD:P, HD:P], 1.0), ident_done)
            for i in range(TILES):
                pool.wait_ge(norm_ready, i + 1)
                n = rows[i]
                c0 = 0 if i == 0 else C_PROMPT + (i - 1) * P
                if i == 0:
                    pool.dma_start(d["h_rows"][0:NS, :], xrow[0:NS, 0, :]).then_inc(h_stored[0], 16)
                else:
                    pool.dma_start(d["h_rows"][c0:c0 + n, :], xrow[:, i % NX, :]).then_inc(h_stored[i % NX], 16)
            for s in range(NX):
                pool.wait_ge(h_stored[s], 16 * len(range(s, TILES, NX)))

        @block.vector
        def _(dve):
            step = chained(dve, vec_chain)
            dve.memset(par_rows[32:PAR_COLS, :], 0.0).then_inc(rows_cleared, 1)
            dve.wait_ge(const_loaded, 32)
            for i in range(TILES):
                s, n = i % NX, rows[i]
                dve.wait_ge(x_loaded[s], 48 + 16 * (i // NX) if s == 0 else 16 * (i // NX + 1))
                x = xrow[0:n, s, :]
                dve.bn_stats(stats[0:n, s, 0:6], x[:, 0:512])
                step(dve.bn_stats(stats[0:n, s, 6:12], x[:, 512:1024]))
                step(dve.bn_aggr(moments[0:n, s, :], stats[0:n, s, :]))
                dve.tensor_scalar(rstd[0:n, s, :], moments[0:n, s, 1:2], LN_EPS, None, ALU.add).then_inc(var_ready, 1)
                dve.wait_ge(std_ready, i + 1)
                step(dve.reciprocal(rstd[0:n, s, :], rstd[0:n, s, :]))
                step(dve.tensor_scalar(x, x, moments[0:n, s, 0:1], rstd[0:n, s, :], ALU.subtract, ALU.mult))
                step(dve.tensor_tensor(x, x, ln_gb[0:n, 0, :], ALU.mult))
                dve.tensor_tensor(x, x, ln_gb[0:n, 1, :], ALU.add).then_inc(norm_ready, 1)

        @block.tensor
        def _(pe):
            pe.wait_ge(ident_done, 5)
            for i in range(TILES):
                s, n = i % NX, rows[i]
                pe.wait_ge(norm_ready, i + 1)
                if i == 0:
                    pe.wait_ge(shift_loaded, 16)
                for half in range(2):
                    if i >= 1:
                        pe.wait_ge(turned_read, 2 * i - 1 + half)
                    buf = (turned, turned2)[half]
                    for k in range(4):
                        kt = half * 4 + k
                        last = pe.transpose(buf[:, 0, k * P:k * P + n], xrow[0:n, s, kt * P:(kt + 1) * P], t.ident[0:n, 0:n])
                    last.then_inc(turned_ready, 1)
            pe.wait_ge(conv_loaded, 16 * (len(PARAMS) + 3))
            for c in range(4):
                last = pe.transpose(turned[:, 1, c * 16:c * 16 + 16], conv_rows[:, c * P:(c + 1) * P], t.ident[0:16, 0:16])
            pe.transpose(turned[:, 1, 64:64 + PAR_COLS], par_rows[:, :], t.ident[0:PAR_COLS, 0:PAR_COLS]).then_inc(turned_ready, 1)

        @block.scalar
        def _(act):
            act_chain = ctx.enter_context(nc.semaphore("in_act_chain"))
            for i in range(TILES):
                s, n = i % NX, rows[i]
                c0 = 0 if i == 0 else C_PROMPT + (i - 1) * P
                act.wait_ge(var_ready, i + 1)
                act.activation(rstd[0:n, s, :], rstd[0:n, s, :], ACT.Sqrt).then_inc(std_ready, 1)
                for half in range(2):
                    buf = (turned, turned2)[half]
                    act.wait_ge(turned_ready, 2 * i + 1 + half)
                    act.activation(t.hT[:, half * 4:half * 4 + 4, c0:c0 + n],
                                   buf[:, 0, :].rearrange("p (k n) -> p k n", k=4)[:, :, 0:n], ACT.Copy).then_inc(turned_read, 1)
            act.wait_ge(turned_ready, 2 * TILES + 1)
            act.activation(t.par[:, :], turned[:, 1, 64:64 + PAR_COLS], ACT.Copy).then_inc(act_chain, 1)
            act.activation(t.conv_state[:, :, :], turned[:, 1, 0:64].rearrange("p (c n) -> p c n", c=4), ACT.Copy).then_inc(act_chain, 1)
            act.wait_ge(act_chain, 2)


def project_phase(nc, t, d):
    ctx = ExitStack()
    with ctx:
        sb = lambda n, s: ctx.enter_context(nc.sbuf_tensor(n, s, F32))
        sem = lambda n: ctx.enter_context(nc.semaphore(n))
        NW = 2
        w_ring = sb("w_ring", [P, NW, KT, P])
        lora_up = sb("lora_up", [2 * W_LORA, RW])
        lora_wa = sb("lora_wa", [2 * W_LORA, PROJ_COLS])
        raw = sb("raw", [P, 2, PROJ_COLS])
        diff = sb("diff", [P, PROJ_COLS])
        sig = sb("sig", [P, PROJ_COLS])
        csig = sb("csig", [P, PROJ_COLS])
        p_inv = sb("p_inv", [P, PROJ_COLS])
        aa = sb("aa", [P, PROJ_COLS])
        keep = sb("keep", [P, PROJ_COLS])
        jobs_ps = [ctx.enter_context(nc.psum_tensor(f"job_ps{i}", [P, 3, 512], F32)) for i in range(2)]
        w_loaded = [sem(f"w_loaded{i}") for i in range(NW)]
        par_loaded = sem("par_loaded")
        job_done = sem("job_done")
        job_read = [sem("job_read0"), sem("job_read1")]
        raw_ready, raw_used, vec_chain, act_chain = sem("raw_ready"), sem("raw_used"), sem("vec_chain2"), sem("act_chain2")
        lora_mixed, lora_ready, kk_ready, square_ready = sem("lora_mixed"), sem("lora_ready"), sem("kk_ready"), sem("square_ready")
        sig_ready, sig_used, aa_ready, aa_used = sem("sig_ready"), sem("sig_used"), sem("aa_ready"), sem("aa_used")
        csig_ready, p_inv_ready, p_inv_used = sem("csig_ready"), sem("p_inv_ready"), sem("p_inv_used")
        p_prev_ready, p_cum_ready, p_cum_used, z_ready = sem("p_prev_ready"), sem("p_cum_ready"), sem("p_cum_used"), sem("z_ready")

        jobs = [("wa", 0, LORA0, 2 * W_LORA), ("gd", 0, LORA0 + 2 * W_LORA, G_LORA)]
        for c in range(PAIRS):
            jobs += [("k", c, RW0 + RW + c * P, P), ("w", c, None, P), ("a", c, None, P), ("r", c, RW0 + c * P, P),
                     ("norm", c, None, P), ("v", c, RW0 + 2 * RW + c * P, P)]
        for c in range(PAIRS):
            jobs += [("cg", c, CONVW + c * P, P), ("hv", c, 2 * CONVW + c * P, P), ("bg", c, c * P, P)]
        streamed = [i for i, job in enumerate(jobs) if job[2] is not None]
        in_raw = [i for i, job in enumerate(jobs) if job[0] not in ("w", "a", "hv", "bg")]

        def param(n, c):
            return t.par[:, PARAMS.index(n) * PAIRS + c:PARAMS.index(n) * PAIRS + c + 1]

        def ps(i, n=P):
            return jobs_ps[i % 2][0:n, :, 0:COLS3]

        def three(x):
            return x.rearrange("p (a b) -> p a b", a=3)

        block = ctx.enter_context(nc.Block())

        @block.sync
        def _(sp):
            for n, i in enumerate(streamed):
                _, _, c0, m = jobs[i]
                if n >= NW:
                    sp.wait_ge(job_done, streamed[n - NW] + 1)
                sp.dma_start(w_ring[:, n % NW, :, 0:m],
                             d["w_in"][0, :, c0:c0 + m].rearrange("(k p) c -> p k c", p=P)).then_inc(w_loaded[n % NW], 16)
                if n == 0:
                    sp.dma_start(lora_up[0:W_LORA, :], d["w_up"][0]).then_inc(par_loaded, 16)
                    sp.dma_start(lora_up[W_LORA:2 * W_LORA, :], d["a_up"][0]).then_inc(par_loaded, 16)

        @block.tensor
        def _(pe):
            for i, (kind, c, c0, m) in enumerate(jobs):
                if i >= 2:
                    pe.wait_ge(job_read[i % 2], i // 2)
                if c0 is not None:
                    n = streamed.index(i)
                    pe.wait_ge(w_loaded[n % NW], 16 * (n // NW + 1))
                    for k in range(KT):
                        for a in range(3):
                            last = pe.matmul(jobs_ps[i % 2][0:m, a, 0:COLS3], w_ring[:, n % NW, k, 0:m],
                                             t.hT[:, k, a * COLS3:(a + 1) * COLS3], start=(k == 0), stop=(k == KT - 1))
                else:
                    if kind == "norm":
                        pe.wait_ge(square_ready, c + 1)
                        lhsT, rhs = t.head_ones[:, :], p_inv[:, :]
                    else:
                        if i == 3:
                            pe.wait_ge(lora_ready, 1)
                            pe.wait_ge(lora_mixed, 1)
                            pe.wait_ge(par_loaded, 32)
                        rows = slice(0, W_LORA) if kind == "w" else slice(W_LORA, 2 * W_LORA)
                        lhsT, rhs = lora_up[rows, c * P:(c + 1) * P], lora_wa[rows, :]
                    for a in range(3):
                        last = pe.matmul(jobs_ps[i % 2][:, a, 0:COLS3], lhsT, rhs[:, a * COLS3:(a + 1) * COLS3],
                                         start=True, stop=True)
                last.then_inc(job_done, 1)

        @block.scalar
        def _(act):
            done = signals(act)
            done(act.activation(t.samp[:, 5, 0:1, 0], t.ident[:, 0:1], ACT.Copy), act_chain)
            for i, (kind, c, _, m) in enumerate(jobs):
                if i in in_raw:
                    n = in_raw.index(i)
                    if n >= 2:
                        act.wait_ge(raw_used, n - 1)
                    act.wait_ge(job_done, i + 1)
                    done(act.activation(three(raw[0:m, n % 2, :]), ps(i, m), ACT.Sqrt if kind == "norm" else ACT.Copy), raw_ready)
                    act.sem_inc(job_read[i % 2], 1)
                if kind == "wa":
                    act.wait_ge(lora_mixed, 1)
                    act.activation(lora_wa[0:W_LORA, :], lora_wa[0:W_LORA, :], ACT.Tanh).then_inc(lora_ready, 1)
                elif kind == "gd":
                    act.wait_ge(lora_mixed, 2)
                    act.activation(t.lora_g[0:G_LORA, :], t.lora_g[0:G_LORA, :], ACT.Sigmoid).then_inc(lora_ready, 1)
                elif kind == "k":
                    act.wait_ge(kk_ready, c + 1)
                    if c:
                        act.wait_ge(p_inv_used, c)
                    act.activation(p_inv[:, :], t.alpha[:, c, WKV_OFF:], ACT.Square).then_inc(square_ready, 1)
                elif kind == "w":
                    if c:
                        act.wait_ge(sig_used, c)
                    act.wait_ge(job_done, i + 1)
                    done(act.activation(three(sig[:, :]), ps(i), ACT.Sigmoid, bias=param("w0", c)), sig_ready)
                    act.sem_inc(job_read[i % 2], 1)
                    act.wait_ge(sig_ready, c + 1)
                    act.activation(t.samp[:, 5, :, c], sig[:, 0:NS], ACT.Exp, scale=-LOG_DECAY).then_inc(act_chain, 1)
                elif kind == "a":
                    if c:
                        act.wait_ge(aa_used, c)
                    act.wait_ge(job_done, i + 1)
                    done(act.activation(three(aa[:, :]), ps(i), ACT.Sigmoid, bias=param("a0", c)), aa_ready)
                    act.sem_inc(job_read[i % 2], 1)
                elif kind == "norm":
                    act.wait_ge(csig_ready, c + 1)
                    act.activation(p_inv[:, :], csig[:, :], ACT.Exp, scale=LOG_DECAY).then_inc(p_inv_ready, 1)
                    act.activation(sig[:, :], sig[:, :], ACT.Exp, scale=-LOG_DECAY).then_inc(p_prev_ready, 1)
                    act.wait_ge(p_inv_ready, c + 1)
                    act.activation(csig[:, :], csig[:, :], ACT.Exp, scale=-LOG_DECAY).then_inc(p_cum_ready, 1)

        @block.vector
        def _(dve):
            done = signals(dve)
            step = lambda ins: done(ins, vec_chain)
            step(dve.memset(keep[:, :], 1.0))
            step(dve.memset(keep[:, C_META:C_META + 1], 0.0))
            step(dve.memset(keep[:, C_PROMPT:].rearrange("p (a b) -> p a b", b=CHUNK)[:, :, 0:1], 0.0))
            step(dve.memset(diff[:, NS:2 * NS], 0.0))
            for x in (t.rho, t.alpha, t.beta, t.kappa, t.vT):
                step(dve.memset(x[:, :, 0:WKV_OFF], 0.0))

            def shift_mix(i, p, m, mu, out):
                dve.wait_ge(raw_ready, in_raw.index(i) + 1)
                step(dve.tensor_tensor(diff[0:m, 0:NS], p[0:m, NS:2 * NS], p[0:m, 0:NS], ALU.subtract))
                step(dve.memset(p[0:m, C_META - 1:C_META], 0.0))
                step(dve.tensor_tensor(diff[0:m, C_META:], p[0:m, C_META - 1:PROJ_COLS - 1], p[0:m, C_META:], ALU.subtract))
                done(dve.scalar_tensor_tensor(out=out, in0=diff[0:m, :], scalar=mu, in1=p[0:m, :], op0=ALU.mult, op1=ALU.add), raw_used)

            for i, (kind, c, _, m) in enumerate(jobs):
                al, be, ka, rh, vt = (x[:, c, WKV_OFF:] for x in (t.alpha, t.beta, t.kappa, t.rho, t.vT))
                p = raw[:, in_raw.index(i) % 2, :] if i in in_raw else None
                if kind == "wa":
                    shift_mix(i, p, m, t.mu_lora[0:m, 0:1], lora_wa[:, :])
                    dve.sem_inc(lora_mixed, 1)
                elif kind == "gd":
                    shift_mix(i, p, m, t.mu_lora[0:m, 1:2], t.lora_g[0:m, :])
                    dve.sem_inc(lora_mixed, 1)
                elif kind == "k":
                    shift_mix(i, p, P, param("mu_k", c), ka)
                    done(dve.tensor_scalar(al, ka, param("k_k", c), None, ALU.mult), kk_ready)
                elif kind == "w":
                    dve.wait_ge(sig_ready, c + 1)
                    dve.wait_ge(act_chain, c + 2)
                    if c:
                        dve.wait_ge(p_cum_used, c)
                    step(dve.tensor_tensor_scan(csig[:, :], keep[:, :], sig[:, :], 0.0, ALU.mult, ALU.add))
                    done(dve.tensor_tensor(sig[:, :], csig[:, :], sig[:, :], ALU.subtract), csig_ready)
                elif kind == "a":
                    dve.wait_ge(aa_ready, c + 1)
                    step(dve.tensor_scalar(diff[:, :], aa[:, :], 1.0, param("k_a", c), ALU.subtract, ALU.mult))
                    step(dve.scalar_tensor_tensor(out=ka, in0=diff[:, :], scalar=1.0, in1=ka, op0=ALU.add, op1=ALU.mult))
                    step(dve.memset(diff[:, NS:2 * NS], 0.0))
                elif kind == "r":
                    shift_mix(i, p, P, param("mu_r", c), rh)
                    step(dve.tensor_copy(t.samp[:, 0, :, c], rh[:, 0:NS]))
                elif kind == "norm":
                    dve.wait_ge(raw_ready, in_raw.index(i) + 1)
                    step(dve.tensor_scalar(p, p, 1e-12, None, ALU.max))
                    step(dve.reciprocal(p, p))
                    done(dve.tensor_tensor(al, al, p, ALU.mult), raw_used)
                    done(dve.tensor_tensor(be, al, aa[:, :], ALU.mult), aa_used)
                    step(dve.tensor_copy(t.samp[:, 1, :, c], ka[:, 0:NS]))
                    step(dve.tensor_copy(t.samp[:, 3, :, c], al[:, 0:NS]))
                    step(dve.tensor_copy(t.samp[:, 4, :, c], be[:, 0:NS]))
                    dve.wait_ge(p_inv_ready, c + 1)
                    step(dve.tensor_tensor(ka, ka, p_inv[:, :], ALU.mult))
                    done(dve.tensor_tensor(be, be, p_inv[:, :], ALU.mult), p_inv_used)
                    dve.wait_ge(p_prev_ready, c + 1)
                    done(dve.scalar_tensor_tensor(out=al, in0=al, scalar=-1.0, in1=sig[:, :], op0=ALU.mult, op1=ALU.mult), sig_used)
                    dve.wait_ge(p_cum_ready, c + 1)
                    step(dve.tensor_tensor(rh, rh, csig[:, :], ALU.mult))
                    done(dve.tensor_copy(t.p_end[:, c, :], csig[:, C_PROMPT - 1:PROJ_COLS:CHUNK]), p_cum_used)
                elif kind == "v":
                    shift_mix(i, p, P, param("mu_v", c), vt)
                    step(dve.tensor_copy(t.samp[:, 2, :, c], vt[:, 0:NS]))
                elif kind == "cg":
                    dve.wait_ge(raw_ready, in_raw.index(i) + 1)
                elif kind == "hv":
                    z, y = csig, t.yc[:, c, :]
                    cg = raw[:, in_raw.index(i - 1) % 2, :]
                    dve.wait_ge(job_done, i + 1)
                    done(dve.tensor_tensor(three(z[:, :]), ps(i), three(cg), ALU.mult), raw_used)
                    dve.sem_inc(job_read[i % 2], 1)
                    step(dve.memset(z[:, NS:2 * NS], 0.0))
                    step(dve.tensor_copy(t.z_out[:, c, 0:NS], z[:, 0:NS]))
                    done(dve.tensor_copy(t.z_out[:, c, NS:NS + 2], z[:, PROJ_COLS - 2:]), z_ready)
                    step(dve.tensor_scalar(y, z[:, :], param("cw2", c), None, ALU.mult))
                    for back, w in ((1, "cw1"), (2, "cw0")):
                        step(dve.scalar_tensor_tensor(out=y[:, C_META:], in0=z[:, C_META - back:PROJ_COLS - back], scalar=param(w, c),
                                                      in1=y[:, C_META:], op0=ALU.mult, op1=ALU.add))
                    old = t.conv_state[:, c, :].rearrange("p (b j) -> p j b", j=2)
                    for j, w in ((0, "cw0"), (1, "cw1")):
                        step(dve.scalar_tensor_tensor(out=y[:, 0:NS], in0=old[:, j, :], scalar=param(w, c),
                                                      in1=y[:, 0:NS], op0=ALU.mult, op1=ALU.add))
                elif kind == "bg":
                    y = t.yc[:, c, :]
                    dve.wait_ge(job_done, i + 1)
                    step(dve.tensor_tensor(three(y), ps(i), three(y), ALU.mult))
                    dve.sem_inc(job_read[i % 2], 1)
            for x in (t.rho, t.alpha, t.beta, t.kappa, t.vT):
                step(dve.memset(x[:, :, WKV_OFF:W_META], 0.0))

class Stages:

    def __init__(self, sem, names):
        self.sem, self.names = sem, names
        self.emitted = 0

    def start(self, eng):
        eng.sem_inc(self.sem, len(self.names))

    def done_by(self, ins, name):
        assert self.names[self.emitted % len(self.names)] == name, name
        self.emitted += 1
        ins.then_inc(self.sem, 1)

    def wait(self, eng, turn, *steps):
        steps = [(x, 0) if isinstance(x, str) else x for x in steps]
        eng.wait_ge(self.sem, turn * len(self.names) + max((1 - back) * len(self.names) + self.names.index(name) + 1
                                                         for name, back in steps))


def wkv_phase(nc, t, d):
    ctx = ExitStack()
    with ctx:
        sb = lambda n, s: ctx.enter_context(nc.sbuf_tensor(n, s, F32))
        sem = lambda n: ctx.enter_context(nc.semaphore(n))
        tile = lambda n: sb(n, [P, PAIRS, CHUNK])
        al, be, ka, rh, vt = (tile(n) for n in ("al", "be", "ka", "rh", "vt"))
        ud, ue, nd, r_, q_ = (tile(n) for n in ("ud", "ue", "nd", "r_", "q_"))
        g_ka, g_br, g_kr = (tile(n) for n in ("g_ka", "g_br", "g_kr"))
        u2, n2, u4, n4, u8, n8 = (tile(n) for n in ("u2", "n2", "u4", "n4", "u8", "n8"))
        mt, m_, m2 = tile("mt"), tile("m_"), tile("m2")
        be_t, ka_t, v_t, xx, sa = (tile(n) for n in ("be_t", "ka_t", "v_t", "xx", "sa"))
        st, st_new, s_out = tile("st"), tile("st_new"), tile("s_out")
        eye = sb("eye", [P, CHUNK])
        upper, upper_eq = sb("upper", [P, CHUNK]), sb("upper_eq", [P, CHUNK])
        upper_in, upper_out, lower_in = sb("upper_in", [P, CHUNK]), sb("upper_out", [P, CHUNK]), sb("lower_in", [P, CHUNK])
        banks = [ctx.enter_context(nc.psum_tensor(f"wkv_ps{i}", [P, 2, PAIRS, CHUNK], F32)) for i in range(8)]
        masks_done, stored = sem("masks_done"), sem("wkv_stored")
        waited, turned_state, state_ready = sem("wkv_waited"), sem("turned_state"), sem("state_ready")

        PRODUCTS = ["U", "N", "BT", "U2", "N2", "KA", "R1", "U4", "Q1", "N4", "KT", "R2", "U8", "Q2", "N8", "VT", "R3", "Q3",
                    "BR", "MT", "M", "KR", "M2", "Z1", "Z", "X", "SA", "S", "O"]
        COPIES = ["be_t", "u2", "n2", "u4", "n4", "ka_t", "u8", "n8", "v_t", "mt", "m", "m2", "xx", "al", "be", "ka", "vt",
                  "sa", "o", "rh"]
        VECTORS = ["ud", "nd", "r", "q", "ue", "g_ka", "r1", "q1", "r2", "q2", "r3", "q3", "g_br", "g_kr", "z1", "z", "s_sum", "s"]
        reader = {"U": ("V", "ue"), "N": ("V", "nd"), "BT": ("A", "be_t"), "U2": ("A", "u2"), "N2": ("A", "n2"), "KA": ("V", "g_ka"),
                  "R1": ("V", "r1"), "U4": ("A", "u4"), "Q1": ("V", "q1"), "N4": ("A", "n4"), "KT": ("A", "ka_t"), "R2": ("V", "r2"),
                  "U8": ("A", "u8"), "Q2": ("V", "q2"), "N8": ("A", "n8"), "VT": ("A", "v_t"), "R3": ("V", "r3"), "Q3": ("V", "q3"),
                  "BR": ("V", "g_br"), "MT": ("A", "mt"), "M": ("A", "m"), "KR": ("V", "g_kr"), "M2": ("A", "m2"), "Z1": ("V", "z1"),
                  "Z": ("V", "z"), "X": ("A", "xx"), "SA": ("A", "sa"), "S": ("V", "s_sum"), "O": ("A", "o")}
        products = Stages(sem("wkv_products"), PRODUCTS)
        copies = Stages(sem("wkv_copies"), COPIES)
        vectors = Stages(sem("wkv_vectors"), VECTORS)

        def ps(name):
            return banks[PRODUCTS.index(name) % 8][:, 0]

        def wide(mask):
            return mask[:, :].unsqueeze(1).broadcast_to([P, PAIRS, CHUNK])

        block = ctx.enter_context(nc.Block())

        @block.gpsimd
        def _(pool):
            done = signals(pool)

            def select(m, op, base, pattern, fill, row=1):
                for h in range(2):
                    done(pool.affine_select(out=m[h * HD:(h + 1) * HD], in_=m[h * HD:(h + 1) * HD], compare_op=op, fill=fill,
                                            base=base, pattern=pattern, channel_multiplier=row), masks_done)

            done(pool.memset(eye[:, :], 0.0), masks_done)
            select(eye[:, :], ALU.not_equal, 0, [[-1, CHUNK]], 1.0)
            for m in (upper, upper_eq, upper_in, lower_in):
                done(pool.memset(m[:, :], 1.0), masks_done)
            select(upper[:, :], ALU.is_gt, 0, [[1, CHUNK]], 0.0, -1)
            select(upper_eq[:, :], ALU.is_ge, 0, [[1, CHUNK]], 0.0, -1)
            for m in (upper_in, lower_in):
                select(m[:, :].rearrange("p (a b) -> p a b", b=16), ALU.is_ge, 0, [[-16, 4], [0, 16]], 0.0)
                select(m[:, :].rearrange("p (a b) -> p a b", b=16), ALU.is_gt, 16, [[16, 4], [0, 16]], 0.0, -1)
            select(lower_in[:, :], ALU.is_gt, 0, [[-1, CHUNK]], 0.0)
            select(upper_in[:, :], ALU.is_gt, 0, [[1, CHUNK]], 0.0, -1)
            done(pool.tensor_tensor(upper_out[:, :], upper[:, :], upper_in[:, :], ALU.subtract), masks_done)

        n_masks = 24

        @block.sync
        def _(sp):
            sp.wait_ge(state_ready, 1)
            for c in range(PAIRS):
                sp.dma_start(d["new_wkv_prompt"][0, 0, 2 * c:2 * c + 2].rearrange("h v k -> (h v) k"), s_out[:, c, :]).then_inc(stored, 16)
            sp.wait_ge(stored, 16 * PAIRS)

        @block.tensor
        def _(pe):
            def freed(name):
                i = PRODUCTS.index(name)
                if i >= 8:
                    return reader[PRODUCTS[i - 8]] + (0,)
                return reader[PRODUCTS[i + 8 * ((len(PRODUCTS) - 1 - i) // 8)]] + (1,)

            def product(turn, name, pairs, **needs):
                steps = {"V": list(needs.get("V", ())), "A": list(needs.get("A", ()))}
                which, step, back = freed(name)
                steps[which].append((step, back))
                for which, source in (("V", vectors), ("A", copies)):
                    if steps[which]:
                        source.wait(pe, turn, *steps[which])
                pe.sem_inc(waited, 1)
                for c in range(PAIRS):
                    for h in range(2):
                        rows = slice(h * HD, (h + 1) * HD)
                        for n, (a, b) in enumerate(pairs):
                            rhs = b[rows, :] if b is eye else b[rows, c, :]
                            last = pe.matmul(ps(name)[rows, c, :], a[rows, c, :], rhs, start=(n == 0), stop=(n == len(pairs) - 1))
                products.done_by(last, name)

            def chunk(turn):
                product(turn, "U", [(be, al)], A=[("al", 1), ("be", 1)])
                product(turn, "N", [(al, be)])
                product(turn, "BT", [(be, eye)])
                product(turn, "U2", [(nd, ud)], V=["nd"])
                product(turn, "N2", [(ud, nd)])
                product(turn, "KA", [(ka, al)], A=[("ka", 1)])
                product(turn, "R1", [(n2, r_)], A=["n2"], V=["q"])
                product(turn, "U4", [(n2, u2)])
                product(turn, "Q1", [(u2, q_)])
                product(turn, "N4", [(u2, n2)])
                product(turn, "KT", [(ka, eye)])
                product(turn, "R2", [(n4, r_)], A=["n4"], V=["r1"])
                product(turn, "U8", [(n4, u4)])
                product(turn, "Q2", [(u4, q_)], V=["q1"])
                product(turn, "N8", [(u4, n4)])
                product(turn, "VT", [(vt, eye)], A=[("vt", 1)])
                product(turn, "R3", [(n8, r_)], A=["n8"], V=["r2"])
                product(turn, "Q3", [(u8, q_)], V=["q2"])
                product(turn, "BR", [(be, rh)], A=[("rh", 1)])
                product(turn, "MT", [(q_, ue)], V=["q3"])
                product(turn, "M", [(ue, q_)])
                product(turn, "KR", [(ka, rh)])
                product(turn, "M2", [(mt, m_)], A=["m"])
                product(turn, "Z1", [(m_, r_)])
                product(turn, "Z", [(m2, r_)], A=["m2"], V=["z1"])
                product(turn, "X", [(al, st), (g_ka, v_t)], V=[("s", 1)])
                product(turn, "SA", [(r_, xx)], A=["xx"], V=["z"])
                product(turn, "S", [(be_t, sa), (ka_t, v_t)], A=["sa"])
                product(turn, "O", [(st, rh), (sa, g_br), (v_t, g_kr)])

            pe.wait_ge(masks_done, n_masks)
            products.start(pe)
            with pe.Fori(0, CHUNKS - 1) as turn:
                chunk(turn)
            chunk(CHUNKS - 1)
            vectors.wait(pe, CHUNKS - 1, "s")
            for c in range(PAIRS):
                for h in range(2):
                    rows = slice(h * HD, (h + 1) * HD)
                    last = pe.matmul(ps("U")[rows, c, :], st[rows, c, :], eye[rows, :], start=True, stop=True)
            last.then_inc(turned_state, 1)

        @block.scalar
        def _(act):
            def stage(turn, names):
                for name, dst, src in (("al", al, t.alpha), ("be", be, t.beta), ("ka", ka, t.kappa), ("vt", vt, t.vT), ("rh", rh, t.rho)):
                    if name in names:
                        copies.done_by(act.activation(dst[:, :, :], src[:, :, bass.ds(turn * CHUNK, CHUNK)], ACT.Copy), name)

            def copy(turn, product, name, dst):
                products.wait(act, turn, product)
                copies.done_by(act.activation(dst, ps(product), ACT.Copy), name)

            def chunk(turn, last=False):
                copy(turn, "BT", "be_t", be_t[:, :, :])
                copy(turn, "U2", "u2", u2[:, :, :])
                copy(turn, "N2", "n2", n2[:, :, :])
                copy(turn, "U4", "u4", u4[:, :, :])
                copy(turn, "N4", "n4", n4[:, :, :])
                copy(turn, "KT", "ka_t", ka_t[:, :, :])
                copy(turn, "U8", "u8", u8[:, :, :])
                copy(turn, "N8", "n8", n8[:, :, :])
                copy(turn, "VT", "v_t", v_t[:, :, :])
                copy(turn, "MT", "mt", mt[:, :, :])
                copy(turn, "M", "m", m_[:, :, :])
                copy(turn, "M2", "m2", m2[:, :, :])
                copy(turn, "X", "xx", xx[:, :, :])
                if not last:
                    stage(turn + 1, ("al", "be", "ka", "vt"))
                else:
                    copies.wait(act, turn, "xx")
                    act.sem_inc(copies.sem, 4)
                    copies.emitted += 4
                copy(turn, "SA", "sa", sa[:, :, :])
                copy(turn, "O", "o", t.alpha[:, :, bass.ds(turn * CHUNK, CHUNK)])
                if not last:
                    stage(turn + 1, ("rh",))

            act.sem_inc(copies.sem, len(COPIES) - 7)
            for name, dst, src in (("al", al, t.alpha), ("be", be, t.beta), ("ka", ka, t.kappa), ("vt", vt, t.vT)):
                act.activation(dst[:, :, :], src[:, :, 0:CHUNK], ACT.Copy).then_inc(copies.sem, 1)
            act.wait_ge(copies.sem, len(COPIES) - 3)
            act.sem_inc(copies.sem, 2)
            act.activation(rh[:, :, :], t.rho[:, :, 0:CHUNK], ACT.Copy).then_inc(copies.sem, 1)
            with act.Fori(0, CHUNKS - 1) as turn:
                chunk(turn)
            chunk(CHUNKS - 1, last=True)
            act.wait_ge(turned_state, 1)
            act.activation(s_out[:, :, :], ps("U"), ACT.Copy).then_inc(state_ready, 1)

        @block.vector
        def _(dve):
            dve.memset(st[:, :, :], 0.0).then_inc(vectors.sem, 1)
            dve.sem_inc(vectors.sem, len(VECTORS) - 1)
            dve.wait_ge(masks_done, n_masks)

            def masked(turn, product, name, dst, mask):
                products.wait(dve, turn, product)
                vectors.done_by(dve.tensor_tensor(dst[:, :, :], ps(product), wide(mask), ALU.mult), name)

            def plus(turn, product, name, dst, own=None):
                products.wait(dve, turn, product)
                vectors.wait(dve, turn, own)
                vectors.done_by(dve.tensor_tensor(dst[:, :, :], ps(product), dst[:, :, :], ALU.add), name)

            def chunk(turn):
                masked(turn, "U", "ud", ud, upper_in)
                masked(turn, "N", "nd", nd, lower_in)
                vectors.wait(dve, turn, "ud")
                vectors.done_by(dve.tensor_tensor(r_[:, :, :], ud[:, :, :], wide(eye), ALU.add), "r")
                vectors.wait(dve, turn, "nd")
                vectors.done_by(dve.tensor_tensor(q_[:, :, :], nd[:, :, :], wide(eye), ALU.add), "q")
                masked(turn, "U", "ue", ue, upper_out)
                masked(turn, "KA", "g_ka", g_ka, upper)
                plus(turn, "R1", "r1", r_, "r")
                plus(turn, "Q1", "q1", q_, "q")
                plus(turn, "R2", "r2", r_, "r1")
                plus(turn, "Q2", "q2", q_, "q1")
                plus(turn, "R3", "r3", r_, "r2")
                plus(turn, "Q3", "q3", q_, "q2")
                masked(turn, "BR", "g_br", g_br, upper_eq)
                masked(turn, "KR", "g_kr", g_kr, upper_eq)
                plus(turn, "Z1", "z1", r_, "r3")
                plus(turn, "Z", "z", r_, "z1")
                products.wait(dve, turn, "S")
                vectors.done_by(dve.tensor_tensor(st_new[:, :, :], ps("S"), st[:, :, :], ALU.add), "s_sum")
                products.wait(dve, turn, "O")
                vectors.wait(dve, turn, "s_sum")
                vectors.done_by(dve.tensor_tensor(st[:, :, :], st_new[:, :, :],
                                                 t.p_end[:, :, bass.ds(turn, 1)].broadcast_to([P, PAIRS, CHUNK]), ALU.mult), "s")

            with dve.Fori(0, CHUNKS - 1) as turn:
                chunk(turn)
            chunk(CHUNKS - 1)


def sample_phase(nc, t, d):
    ctx = ExitStack()
    with ctx:
        sb = lambda n, s: ctx.enter_context(nc.sbuf_tensor(n, s, F32))
        sem = lambda n: ctx.enter_context(nc.semaphore(n))
        BH = NS * HEADS
        rows_sb = sb("samp_rows_sb", [3 * NS * PAIRS, 2, P])
        vecs = sb("samp_vecs", [BH, 6, HD])
        state = sb("samp_state", [BH, HD, HD])
        term = sb("samp_term", [BH, HD, HD])
        sa, o_rows = sb("samp_sa", [BH, HD]), sb("samp_o", [BH, 2, HD])
        z_rows = sb("z_rows", [NS + 2, CONVW])
        turned = [ctx.enter_context(nc.psum_tensor(f"samp_ps{i}", [P, 512], F32)) for i in range(3)]
        state_loaded, vecs_loaded, rows_stored, all_stored = sem("state_loaded"), sem("vecs_loaded"), sem("rows_stored"), sem("samp_stored")
        pe_done, act_done, chain, state_new, o_ready = sem("samp_pe"), sem("samp_act"), sem("samp_chain"), sem("state_new"), sem("o_ready")
        block = ctx.enter_context(nc.Block())
        R = 3 * NS * PAIRS

        @block.sync
        def _(sp):
            sp.dma_start(state[:, :, :], d["state_wkv"][0].rearrange("b h v k -> (b h) v k")).then_inc(state_loaded, 16)
            sp.dma_start(d["new_shift_prompt"][0], d["h_rows"][PROJ_COLS - 1:PROJ_COLS, :]).then_inc(all_stored, 16)
            sp.dma_start(d["new_shift_sample"][0], d["h_rows"][0:NS, :]).then_inc(all_stored, 16)
            sp.dma_start(d["new_conv_sample"][0, :, 0, :], d["state_conv"][0, :, 1, :]).then_inc(all_stored, 16)
            sp.wait_ge(act_done, 2)
            for j in range(6):
                sp.dma_start(d["samp_rows"].rearrange("(b c) h j k -> (b c) h j k", b=NS)[:, :, j, :],
                             rows_sb[(j % 3) * 32:(j % 3) * 32 + 32, j // 3, :].rearrange("p (h k) -> p h k", h=2)).then_inc(rows_stored, 16)
            sp.wait_ge(rows_stored, 96)
            sp.dma_start(vecs[:, :, :], d["samp_rows"].rearrange("a h j k -> (a h) j k")).then_inc(vecs_loaded, 16)
            sp.wait_ge(act_done, 3)
            sp.dma_start(d["new_conv_sample"][0, :, 1, :], z_rows[0:NS, :]).then_inc(all_stored, 16)
            sp.dma_start(d["new_conv_prompt"][0, 0], z_rows[NS:NS + 2, :]).then_inc(all_stored, 16)
            sp.wait_ge(state_new, 1)
            sp.dma_start(d["new_wkv_sample"][0].rearrange("b h v k -> (b h) v k"), state[:, :, :]).then_inc(all_stored, 16)
            sp.wait_ge(all_stored, 96)

        @block.tensor
        def _(pe):
            flat = t.samp[:, :, :, :].rearrange("p j b c -> p (j b c)")
            for half in range(2):
                pe.transpose(turned[half][0:R, 0:P], flat[:, half * R:(half + 1) * R], t.ident[:, :]).then_inc(pe_done, 1)
            for c in range(PAIRS):
                last = pe.transpose(turned[2][0:NS + 2, c * P:(c + 1) * P], t.z_out[:, c, :], t.ident[:, :])
            last.then_inc(pe_done, 1)
            pe.wait_ge(o_ready, 1)
            pe.wait_ge(act_done, 1)
            pe.matmul(turned[0][:, 0:BH], o_rows[:, :, :].rearrange("p a b -> p (a b)"), t.ident[0:BH, 0:BH],
                      start=True, stop=True).then_inc(pe_done, 1)

        @block.scalar
        def _(act):
            for half in range(2):
                act.wait_ge(pe_done, half + 1)
                act.activation(rows_sb[:, half, :], turned[half][0:R, 0:P], ACT.Copy).then_inc(act_done, 1)
            act.wait_ge(pe_done, 3)
            act.activation(z_rows[:, :], turned[2][0:NS + 2, :], ACT.Copy).then_inc(act_done, 1)
            act.wait_ge(pe_done, 4)
            for h in range(2):
                rows = slice(h * HD, (h + 1) * HD)
                src = turned[0][rows, 0:BH].rearrange("p (b c h) -> p h c b", b=NS, c=PAIRS)[:, h]
                act.activation(t.alpha[rows, :, WKV_OFF:WKV_OFF + NS], src, ACT.Copy).then_inc(act_done, 1)

        @block.vector
        def _(dve):
            done = signals(dve)
            step = lambda ins: done(ins, chain)
            full = [BH, HD, HD]
            along_k = lambda x: x.unsqueeze(1).broadcast_to(full)
            along_v = lambda x: x.unsqueeze(2).broadcast_to(full)
            for j, x in ((0, t.rho), (1, t.kappa), (2, t.vT)):
                step(dve.tensor_copy(x[:, :, WKV_OFF:WKV_OFF + NS], t.samp[:, j].rearrange("p b c -> p c b")))
            dve.wait_ge(state_loaded, 16)
            dve.wait_ge(vecs_loaded, 16)
            r, k, v, kk, kka, w = (vecs[:, j, :] for j in range(6))
            step(dve.tensor_tensor(term[:, :, :], state[:, :, :], along_k(kk), ALU.mult))
            step(dve.tensor_reduce(sa[:, :], term[:, :, :], AX_X, ALU.add))
            step(dve.tensor_tensor(state[:, :, :], state[:, :, :], along_k(w), ALU.mult))
            step(dve.tensor_tensor(term[:, :, :], along_v(sa[:, :]), along_k(kka), ALU.mult))
            step(dve.tensor_tensor(state[:, :, :], state[:, :, :], term[:, :, :], ALU.subtract))
            step(dve.tensor_tensor(term[:, :, :], along_v(v), along_k(k), ALU.mult))
            done(dve.tensor_tensor(state[:, :, :], state[:, :, :], term[:, :, :], ALU.add), state_new)
            step(dve.tensor_tensor(term[:, :, :], state[:, :, :], along_k(r), ALU.mult))
            step(dve.tensor_reduce(o_rows[:, 0, :], term[:, :, :], AX_X, ALU.add))
            dve.tensor_copy(o_rows[:, 1, :], o_rows[:, 0, :]).then_inc(o_ready, 1)


def norm_phase(nc, t, d):
    ctx = ExitStack()
    with ctx:
        sb = lambda n, s: ctx.enter_context(nc.sbuf_tensor(n, s, F32))
        sem = lambda n: ctx.enter_context(nc.semaphore(n))
        g_up = sb("g_up", [G_LORA, RW])
        square = sb("gn_square", [P, 2, PROJ_COLS])
        rk = sb("gn_rk", [P, 2, PROJ_COLS])
        std = sb("gn_std", [P, 2, PROJ_COLS])
        sets = [ctx.enter_context(nc.psum_tensor(f"gn_ps{i}", [P, 3, 512], F32)) for i in range(2)]
        rk_chain = sem("rk_chain")
        g_loaded, product, read, chain = sem("g_loaded"), sem("gn_product"), sem("gn_read"), sem("gn_chain")
        rk_ready, d_ready, square_ready, var_ready, std_ready = sem("rk_ready"), sem("d_ready"), sem("gn_square_ready"), sem("gn_var"), sem("gn_std_s")
        block = ctx.enter_context(nc.Block())
        KINDS = ["mean", "bonus", "var", "gate"]

        @block.sync
        def _(sp):
            sp.dma_start(g_up[:, :], d["g_up"][0]).then_inc(g_loaded, 16)

        @block.gpsimd
        def _(pool):
            done = signals(pool)
            for c in range(PAIRS):
                if c >= 2:
                    pool.wait_ge(product, 4 * (c - 2) + 2)
                rkc = rk[:, c % 2, :]
                done(pool.tensor_tensor(rkc, t.rho[:, c, WKV_OFF:], t.kappa[:, c, WKV_OFF:], ALU.mult), rk_chain)
                pool.tensor_scalar(rkc, rkc, t.par[:, PARAMS.index("r_k") * PAIRS + c:PARAMS.index("r_k") * PAIRS + c + 1], None,
                                   ALU.mult).then_inc(rk_ready, 1)

        @block.tensor
        def _(pe):
            pe.wait_ge(g_loaded, 16)
            for c in range(PAIRS):
                for j, kind in enumerate(KINDS):
                    n = 4 * c + j
                    if n >= 2:
                        pe.wait_ge(read, n - 1)
                    lhsT, rhs = {"mean": (t.head_ones[:, :], t.alpha[:, c, WKV_OFF:]), "bonus": (t.head_ones[:, :], rk[:, c % 2, :]),
                                 "var": (t.head_ones[:, :], square[:, c % 2, :]),
                                 "gate": (g_up[:, c * P:(c + 1) * P], t.lora_g[:, :])}[kind]
                    if kind == "bonus":
                        pe.wait_ge(rk_ready, c + 1)
                    if kind == "var":
                        pe.wait_ge(square_ready, c + 1)
                    for a in range(3):
                        last = pe.matmul(sets[n % 2][:, a, 0:COLS3], lhsT, rhs[:, a * COLS3:(a + 1) * COLS3], start=True, stop=True)
                    last.then_inc(product, 1)

        @block.scalar
        def _(act):
            for c in range(PAIRS):
                act.wait_ge(d_ready, c + 1)
                if c >= 2:
                    act.wait_ge(product, 4 * (c - 2) + 3)
                act.activation(square[:, c % 2, :], t.alpha[:, c, WKV_OFF:], ACT.Square).then_inc(square_ready, 1)
                act.wait_ge(var_ready, c + 1)
                act.activation(std[:, c % 2, :], std[:, c % 2, :], ACT.Sqrt).then_inc(std_ready, 1)

        @block.vector
        def _(dve):
            done = signals(dve)
            step = lambda ins: done(ins, chain)
            three = lambda x: x.rearrange("p (a b) -> p a b", a=3)

            def ps(n):
                return sets[n % 2][:, :, 0:COLS3]
            for c in range(PAIRS):
                o, v = t.alpha[:, c, WKV_OFF:], t.vT[:, c, WKV_OFF:]
                sd = std[:, c % 2, :]
                par = lambda n: t.par[:, PARAMS.index(n) * PAIRS + c:PARAMS.index(n) * PAIRS + c + 1]
                dve.wait_ge(product, 4 * c + 1)
                done(dve.scalar_tensor_tensor(out=three(o), in0=ps(4 * c), scalar=-1.0 / HD, in1=three(o), op0=ALU.mult, op1=ALU.add), read)
                dve.sem_inc(d_ready, 1)
                dve.wait_ge(product, 4 * c + 2)
                done(dve.tensor_tensor(three(v), ps(4 * c + 1), three(v), ALU.mult), read)
                dve.wait_ge(product, 4 * c + 3)
                done(dve.tensor_scalar(three(sd), ps(4 * c + 2), 1.0 / HD, GN_EPS, ALU.mult, ALU.add), read)
                dve.sem_inc(var_ready, 1)
                dve.wait_ge(std_ready, c + 1)
                step(dve.reciprocal(sd, sd))
                step(dve.tensor_tensor(o, o, sd, ALU.mult))
                step(dve.tensor_scalar(o, o, par("gn_g"), par("gn_b"), ALU.mult, ALU.add))
                step(dve.tensor_tensor(o, o, v, ALU.add))
                dve.wait_ge(product, 4 * c + 4)
                done(dve.tensor_tensor(three(o), ps(4 * c + 3), three(o), ALU.mult), read)


def mix_phase(nc, t, d):
    ctx = ExitStack()
    with ctx:
        sb = lambda n, s: ctx.enter_context(nc.sbuf_tensor(n, s, F32))
        sem = lambda n: ctx.enter_context(nc.semaphore(n))
        w_o = sb("w_o", [P, KT, D])
        gb = sb("ln1_gb", [P, 2, D])
        y = sb("mix_y", [P, 2, KT, P])
        h = sb("mix_h", [P, 2, D])
        stats, moments, rstd = sb("mix_stats", [P, 2, 12]), sb("mix_moments", [P, 2, 2]), sb("mix_rstd", [P, 2, 1])
        mixed = [ctx.enter_context(nc.psum_tensor(f"mix_ps{i}", [P, 2, 512], F32)) for i in range(2)]
        turned = [ctx.enter_context(nc.psum_tensor(f"mix_turned{i}", [P, 2, 4, P], F32)) for i in range(2)]
        w_loaded, h_loaded, stored = sem("wo_loaded"), [sem("h_loaded0"), sem("h_loaded1")], t.h1_stored
        half_y = sem("half_y")
        y_ready, mix_ready, chain, var_ready, std_ready = sem("y_ready"), sem("mix_ready"), sem("mix_chain"), sem("mix_var"), sem("mix_std")
        mix_read, h1_ready, turned_ready, turned_read = sem("mix_read"), sem("h1_ready"), sem("mix_turned"), sem("mix_turned_read")
        block = ctx.enter_context(nc.Block())
        TILES = TBLOCKS + 1
        rows = [P] * TBLOCKS + [NS]
        col0 = [C_PROMPT + i * P for i in range(TBLOCKS)] + [0]

        @block.sync
        def _(sp):
            for k in range(KT):
                sp.dma_start(w_o[:, k, :], d["w_o"][0, k * P:(k + 1) * P, :]).then_inc(w_loaded, 16)
            for j, n in enumerate(("ln1_g", "ln1_b")):
                sp.dma_start(gb[:, j, :], d[n][0:1, :].broadcast_to([P, D])).then_inc(w_loaded, 16)
            for i in range(TILES):
                s = i % 2
                if i >= 2:
                    sp.wait_ge(turned_ready, i - 1)
                    sp.wait_ge(stored[s], 16 * (i // 2))
                sp.dma_start(h[0:rows[i], s, :], d["h_rows"][col0[i]:col0[i] + rows[i], :]).then_inc(h_loaded[s], 16)

        @block.gpsimd
        def _(pool):
            for i in range(TILES):
                pool.wait_ge(h1_ready, i + 1)
                pool.dma_start(d["h1_rows"][i * P:i * P + rows[i], :], h[0:rows[i], i % 2, :]).then_inc(stored[i % 2], 16)
            pool.wait_ge(stored[0], 16 * 5)
            pool.wait_ge(stored[1], 16 * 4)

        @block.tensor
        def _(pe):
            pe.wait_ge(w_loaded, 16 * (KT + 2))

            def turn(i):
                n = rows[i]
                pe.wait_ge(h1_ready, i + 1)
                if i >= 2:
                    pe.wait_ge(turned_read, i - 1)
                for k in range(KT):
                    last = pe.transpose(turned[i % 2][:, k // 4, k % 4, 0:n], h[0:n, i % 2, k * P:(k + 1) * P], t.ident[0:n, 0:n])
                last.then_inc(turned_ready, 1)

            for i in range(TILES):
                n = rows[i]
                pe.wait_ge(y_ready, i + 1)
                if i >= 2:
                    pe.wait_ge(mix_read, i - 1)
                for k in range(KT):
                    for half in range(2):
                        last = pe.matmul(mixed[i % 2][0:n, half, :], y[:, i % 2, k, 0:n], w_o[:, k, half * 512:(half + 1) * 512],
                                         start=(k == 0), stop=(k == KT - 1))
                last.then_inc(mix_ready, 1)
                if i >= 1:
                    turn(i - 1)
            turn(TILES - 1)

        @block.scalar
        def _(act):
            def stage(i):
                n, c0 = rows[i], col0[i]
                if i >= 2:
                    act.wait_ge(mix_ready, i - 1)
                act.activation(y[:, i % 2, 0:PAIRS, 0:n], t.yc[:, :, c0:c0 + n], ACT.Copy).then_inc(half_y, 1)
                act.wait_ge(half_y, i + 1)
                act.activation(y[:, i % 2, PAIRS:, 0:n], t.alpha[:, :, WKV_OFF + c0:WKV_OFF + c0 + n], ACT.Copy).then_inc(y_ready, 1)
            stage(0)
            for i in range(TILES):
                if i + 1 < TILES:
                    stage(i + 1)
                act.wait_ge(var_ready, i + 1)
                act.activation(rstd[0:rows[i], i % 2, :], rstd[0:rows[i], i % 2, :], ACT.Sqrt).then_inc(std_ready, 1)
                act.wait_ge(turned_ready, i + 1)
                act.activation(t.h1T[:, :, i * P:i * P + rows[i]],
                               turned[i % 2][:, :, :, 0:rows[i]].rearrange("p a b n -> p (a b) n"), ACT.Copy).then_inc(turned_read, 1)

        @block.vector
        def _(dve):
            done = signals(dve)
            step = lambda ins: done(ins, chain)
            for i in range(TILES):
                s, n = i % 2, rows[i]
                x = h[0:n, s, :]
                dve.wait_ge(h_loaded[s], 16 * (i // 2 + 1))
                dve.wait_ge(mix_ready, i + 1)
                done(dve.scalar_tensor_tensor(out=x, in0=x, scalar=ALPHA, in1=mixed[s][0:n, :, :].rearrange("p a b -> p (a b)"),
                                              op0=ALU.mult, op1=ALU.add), mix_read)
                step(dve.bn_stats(stats[0:n, s, 0:6], x[:, 0:512]))
                step(dve.bn_stats(stats[0:n, s, 6:12], x[:, 512:1024]))
                step(dve.bn_aggr(moments[0:n, s, :], stats[0:n, s, :]))
                done(dve.tensor_scalar(rstd[0:n, s, :], moments[0:n, s, 1:2], LN_EPS, None, ALU.add), var_ready)
                dve.wait_ge(std_ready, i + 1)
                step(dve.reciprocal(rstd[0:n, s, :], rstd[0:n, s, :]))
                step(dve.tensor_scalar(x, x, moments[0:n, s, 0:1], rstd[0:n, s, :], ALU.subtract, ALU.mult))
                step(dve.tensor_tensor(x, x, gb[0:n, 0, :], ALU.mult))
                done(dve.tensor_tensor(x, x, gb[0:n, 1, :], ALU.add), h1_ready)


def keys_phase(nc, t, d):
    ctx = ExitStack()
    with ctx:
        sb = lambda n, s, dt=F32: ctx.enter_context(nc.sbuf_tensor(n, s, dt))
        sem = lambda n: ctx.enter_context(nc.semaphore(n))
        T = SEQ + NS
        T3 = T // 3
        NT = TBLOCKS + 1
        rows = [P] * TBLOCKS + [NS]
        NW = 3
        HP = 2 * PEER_HEADS
        w_ring, k_rows = sb("wq_ring", [P, NW, KT, P]), sb("key_rows", [P, NW, N_KEYS])
        q, keysT = sb("q_T", [P, 2, T]), sb("keys_T", [P, 2, N_KEYS])
        best_first = sb("best_first", [P, N_KEYS])
        vals, places = sb("top_vals", [P, TOPK]), sb("top_places", [P, TOPK], U32)
        q_ps = ctx.enter_context(nc.psum_tensor("q_ps", [P, 3, 512], F32))
        key_ps = ctx.enter_context(nc.psum_tensor("key_ps", [P, 512], F32))
        sc_ps = ctx.enter_context(nc.psum_tensor("score_ps", [P, 4, 4, N_KEYS], F32))
        loaded = [sem(f"wq_loaded{i}") for i in range(NW)]
        q_ready, q_read, key_turned, key_ready, scores_ready, scores_read, chain = (
            sem("q_ready"), sem("q_read"), sem("key_turned"), sem("key_ready"), sem("scores_ready"), sem("scores_read"), sem("top_chain"))
        block = ctx.enter_context(nc.Block())

        @block.sync
        def _(sp):
            for j in range(HP):
                s = j % NW
                if j >= NW:
                    sp.wait_ge(q_ready, j - NW + 1)
                    sp.wait_ge(key_turned, j - NW + 1)
                sp.dma_start(w_ring[:, s, :, :], d["w_q"][0, :, j * P:(j + 1) * P].rearrange("(k p) c -> p k c", p=P)).then_inc(loaded[s], 16)
                sp.dma_start(k_rows[:, s, :], d["sub_keys"][0, j // 2, j % 2]).then_inc(loaded[s], 16)

        @block.tensor
        def _(pe):
            def score(j):
                pe.wait_ge(q_read, j + 1)
                pe.wait_ge(key_ready, j + 1)
                for b in range(NT):
                    n = j * NT + b
                    if n >= 4:
                        pe.wait_ge(scores_read, n - 3)
                    pe.matmul(sc_ps[0:rows[b], n % 4, 0, :], q[:, j % 2, b * P:b * P + rows[b]], keysT[:, j % 2, :],
                              start=True, stop=True).then_inc(scores_ready, 1)

            for j in range(HP):
                pe.wait_ge(loaded[j % NW], 32 * (j // NW + 1))
                if j >= 1:
                    pe.wait_ge(key_ready, j)
                pe.transpose(key_ps[:, 0:P], k_rows[:, j % NW, :], t.ident[:, :]).then_inc(key_turned, 1)
                if j >= 1:
                    pe.wait_ge(q_read, j)
                for k in range(KT):
                    for a in range(3):
                        last = pe.matmul(q_ps[:, a, 0:T3], w_ring[:, j % NW, k, :], t.h1T[:, k, a * T3:(a + 1) * T3],
                                         start=(k == 0), stop=(k == KT - 1))
                last.then_inc(q_ready, 1)
                if j >= 1:
                    score(j - 1)
            score(HP - 1)

        @block.scalar
        def _(act):
            for j in range(HP):
                if j >= 2:
                    act.wait_ge(scores_ready, (j - 1) * NT)
                act.wait_ge(key_turned, j + 1)
                act.activation(keysT[:, j % 2, :], key_ps[:, 0:P], ACT.Copy).then_inc(key_ready, 1)
                act.wait_ge(q_ready, j + 1)
                act.activation(q[:, j % 2, :].rearrange("p (a b) -> p a b", a=3), q_ps[:, :, 0:T3], ACT.Copy).then_inc(q_read, 1)

        @block.vector
        def _(dve):
            done = signals(dve)
            step = lambda ins: done(ins, chain)
            for j in range(HP):
                for b in range(NT):
                    n, r = j * NT + b, rows[b]
                    sc = sc_ps[0:r, n % 4, 0, :]
                    dst = (b * PEER_HEADS + j // 2, j % 2)
                    v = t.top_val[0:r, dst[0], dst[1], :]
                    dve.wait_ge(scores_ready, n + 1)
                    step(dve.max(v[:, 0:8], sc))
                    step(dve.max_index(places[0:r, 0:8], v[:, 0:8], sc))
                    done(dve.match_replace(best_first[0:r, :], v[:, 0:8], sc, NEG), scores_read)
                    step(dve.max(v[:, 8:16], best_first[0:r, :]))
                    step(dve.max_index(places[0:r, 8:16], v[:, 8:16], best_first[0:r, :]))
                    step(dve.tensor_copy(t.top_idx[0:r, dst[0], dst[1], :], places[0:r, :]))


def pick_experts(dve, step, rows, val, idx, k, best, expert):
    n = slice(0, rows)
    sq = [rows, TOPK, TOPK]
    step(dve.tensor_tensor(k.sums[n], val[n, 0, :].unsqueeze(2).broadcast_to(sq), val[n, 1, :].unsqueeze(1).broadcast_to(sq), ALU.add))
    flat, flat2 = k.sums[n].rearrange("p a b -> p (a b)"), k.sums2[n].rearrange("p a b -> p (a b)")
    step(dve.max(best[n, 0:8], flat))
    step(dve.max_index(k.place[n, 0:8], best[n, 0:8], flat))
    step(dve.match_replace(flat2, best[n, 0:8], flat, NEG))
    step(dve.max(best[n, 8:16], flat2))
    step(dve.max_index(k.place[n, 8:16], best[n, 8:16], flat2))
    step(dve.tensor_single_scalar(k.half[n, 0, :], k.place[n, :], 4, ALU.logical_shift_right))
    step(dve.tensor_single_scalar(k.half[n, 1, :], k.place[n, :], TOPK - 1, ALU.bitwise_and))
    for j in range(2):
        step(dve.tensor_tensor(k.sums[n], k.half[n, j, :].unsqueeze(2).broadcast_to(sq), k.iota[n, :].unsqueeze(1).broadcast_to(sq), ALU.is_equal))
        step(dve.tensor_tensor(k.sums[n], k.sums[n], idx[n, j, :].unsqueeze(1).broadcast_to(sq), ALU.mult))
        step(dve.tensor_reduce(k.number[n, j, :], k.sums[n], AX_X, ALU.add))
    return dve.scalar_tensor_tensor(out=expert[n, :], in0=k.number[n, 0, :], scalar=float(N_KEYS), in1=k.number[n, 1, :],
                                    op0=ALU.mult, op1=ALU.add)


def pick_tiles(nc, ctx, name):
    k = Tiles()
    k.sums = ctx.enter_context(nc.sbuf_tensor(name + "_sums", [P, TOPK, TOPK], F32))
    k.sums2 = ctx.enter_context(nc.sbuf_tensor(name + "_sums2", [P, TOPK, TOPK], F32))
    k.place = ctx.enter_context(nc.sbuf_tensor(name + "_place", [P, TOPK], U32))
    k.half = ctx.enter_context(nc.sbuf_tensor(name + "_half", [P, 2, TOPK], U32))
    k.number = ctx.enter_context(nc.sbuf_tensor(name + "_number", [P, 2, TOPK], F32))
    k.iota = ctx.enter_context(nc.sbuf_tensor(name + "_iota", [P, TOPK], F32))
    return k


def gather(pool, ring, table, index):
    return pool.indirect_dma_start(out=ring, out_offset=None, in_=table, in_offset=bass.IndirectOffsetOnAxis(ap=index, axis=0))


def sample_experts_phase(nc, t, d):
    ctx = ExitStack()
    with ctx:
        sb = lambda n, s, dt=F32: ctx.enter_context(nc.sbuf_tensor(n, s, dt))
        sem = lambda n: ctx.enter_context(nc.semaphore(n))
        k = pick_tiles(nc, ctx, "sp")
        PER = P // NS
        EACH = SLOTS // PER
        best, ex = sb("sp_best", [NS, PEER_HEADS, TOPK]), sb("sp_ex", [NS, PEER_HEADS, TOPK])
        expert = sb("sp_expert", [NS, PEER_HEADS, TOPK], U32)
        total = sb("sp_total", [NS, PEER_HEADS, 1])
        idx, gate = sb("sp_idx", [P, EACH], U32), sb("sp_gate", [P, EACH])
        x, u, v = sb("sp_x", [P, D]), sb("sp_u", [P, EACH, D]), sb("sp_v", [P, EACH, D])
        hu = sb("sp_hu", [P, EACH])
        acc, own, gb = sb("sp_acc", [P, D]), sb("sp_own", [NS, D]), sb("sp_gb", [NS, 2, D])
        select = sb("sp_select", [P, NS])
        stats, moments, rstd = sb("sp_stats", [NS, 12]), sb("sp_moments", [NS, 2]), sb("sp_rstd", [NS, 1])
        out_ps = ctx.enter_context(nc.psum_tensor("sp_ps", [NS, 2, 512], F32))
        consts, chain, diff_ready, exp_ready, picked, stored, reloaded, x_loaded = (
            sem("sp_consts"), sem("sp_chain"), sem("sp_diff"), sem("sp_exp"), sem("sp_picked"), sem("sp_stored"), sem("sp_reloaded"), sem("sp_x_loaded"))
        u_landed, v_landed, hu_ready, gelu_ready, acc_ready, summed, var_ready, std_ready, y_ready, y_stored = (
            t.sp_landed[0], t.sp_landed[1], sem("sp_hu_ready"), sem("sp_gelu"), sem("sp_acc_ready"), sem("sp_summed"),
            sem("sp_var"), sem("sp_std"), sem("sp_y"), sem("sp_y_stored"))
        block = ctx.enter_context(nc.Block())

        @block.sync
        def _(sp):
            for b in range(NS):
                sp.dma_start(x[b * PER:(b + 1) * PER, :], d["h1_rows"][SEQ + b:SEQ + b + 1, :].broadcast_to([PER, D])).then_inc(x_loaded, 16)
            sp.dma_start(own[:, :], d["h1_rows"][SEQ:SEQ + NS, :]).then_inc(x_loaded, 16)
            for j, n in enumerate(("ln2_g", "ln2_b")):
                sp.dma_start(gb[:, j, :], d[n][0:1, :].broadcast_to([NS, D])).then_inc(x_loaded, 16)
            sp.wait_ge(picked, 2)
            sp.dma_start(d["sp_idx"], expert[:, :, :].rearrange("p a b -> p (a b)")).then_inc(stored, 16)
            sp.dma_start(d["sp_gate"], ex[:, :, :].rearrange("p a b -> p (a b)")).then_inc(stored, 16)
            sp.wait_ge(stored, 32)
            sp.dma_start(idx[:, :], d["sp_idx"].rearrange("b (s e) -> (b s) e", e=EACH)).then_inc(reloaded, 16)
            sp.dma_start(gate[:, :], d["sp_gate"].rearrange("b (s e) -> (b s) e", e=EACH)).then_inc(reloaded, 16)
            sp.wait_ge(y_ready, 1)
            sp.dma_start(d["y_sample"][:, 0, :], own[:, :]).then_inc(y_stored, 16)
            sp.wait_ge(y_stored, 16)

        @block.gpsimd
        def _(pool):
            done = signals(pool)
            done(pool.iota(k.iota[:, :], [[1, TOPK]], base=0, channel_multiplier=0, allow_small_or_imprecise_dtypes=True), consts)
            done(pool.memset(select[:, :], 1.0), consts)
            done(pool.affine_select(out=select[:, :], in_=select[:, :], compare_op=ALU.is_ge, fill=0.0, base=0,
                                    pattern=[[-PER, NS]], channel_multiplier=1), consts)
            done(pool.affine_select(out=select[:, :], in_=select[:, :], compare_op=ALU.is_gt, fill=0.0, base=PER,
                                    pattern=[[PER, NS]], channel_multiplier=-1), consts)
            pool.wait_ge(reloaded, 32)
            for e in range(EACH):
                gather(pool, u[:, e, :], d["peer_u"][0], idx[:, e:e + 1]).then_inc(u_landed, 16)
            for e in range(EACH):
                gather(pool, v[:, e, :], d["peer_v"][0], idx[:, e:e + 1]).then_inc(v_landed, 16)

        @block.tensor
        def _(pe):
            pe.wait_ge(consts, 4)
            pe.wait_ge(acc_ready, 1)
            for half in range(2):
                last = pe.matmul(out_ps[:, half, :], select[:, :], acc[:, half * 512:(half + 1) * 512], start=True, stop=True)
            last.then_inc(summed, 1)

        @block.scalar
        def _(act):
            act.wait_ge(diff_ready, 1)
            act.activation(ex[:, :, :], ex[:, :, :], ACT.Exp).then_inc(exp_ready, 1)
            act.wait_ge(hu_ready, 1)
            act.activation(hu[:, :], hu[:, :], ACT.Gelu).then_inc(gelu_ready, 1)
            act.wait_ge(var_ready, 1)
            act.activation(rstd[:, :], rstd[:, :], ACT.Sqrt).then_inc(std_ready, 1)

        @block.vector
        def _(dve):
            done = signals(dve)
            step = lambda ins: done(ins, chain)
            dve.wait_ge(consts, 1)
            for h in range(PEER_HEADS):
                turn = TBLOCKS * PEER_HEADS + h
                step(pick_experts(dve, step, NS, t.top_val[:, turn], t.top_idx[:, turn], k, best[:, h, :], expert[:, h, :]))
            shape = [NS, PEER_HEADS, TOPK]
            done(dve.tensor_tensor(ex[:, :, :], best[:, :, :], best[:, :, 0:1].broadcast_to(shape), ALU.subtract), diff_ready)
            dve.sem_inc(picked, 1)
            dve.wait_ge(exp_ready, 1)
            step(dve.tensor_reduce(total[:, :, :], ex[:, :, :], AX_X, ALU.add))
            step(dve.reciprocal(total[:, :, :], total[:, :, :]))
            done(dve.tensor_tensor(ex[:, :, :], ex[:, :, :], total[:, :, :].broadcast_to(shape), ALU.mult), picked)
            dve.wait_ge(x_loaded, 16 * (NS + 3))
            dve.wait_ge(u_landed, 16 * EACH)
            for e in range(EACH):
                step(dve.tensor_tensor_reduce(u[:, e, :], u[:, e, :], x[:, :], 1.0, 0.0, ALU.mult, ALU.add, hu[:, e:e + 1]))
            dve.sem_inc(hu_ready, 1)
            dve.wait_ge(gelu_ready, 1)
            step(dve.tensor_tensor(hu[:, :], hu[:, :], gate[:, :], ALU.mult))
            dve.wait_ge(v_landed, 16 * EACH)
            step(dve.tensor_scalar(acc[:, :], v[:, 0, :], hu[:, 0:1], None, ALU.mult))
            for e in range(1, EACH):
                step(dve.scalar_tensor_tensor(out=acc[:, :], in0=v[:, e, :], scalar=hu[:, e:e + 1], in1=acc[:, :], op0=ALU.mult, op1=ALU.add))
            dve.sem_inc(acc_ready, 1)
            dve.wait_ge(summed, 1)
            y = own[:, :]
            step(dve.scalar_tensor_tensor(out=y, in0=y, scalar=ALPHA, in1=out_ps[:, :, :].rearrange("p a b -> p (a b)"),
                                          op0=ALU.mult, op1=ALU.add))
            step(dve.bn_stats(stats[:, 0:6], y[:, 0:512]))
            step(dve.bn_stats(stats[:, 6:12], y[:, 512:1024]))
            step(dve.bn_aggr(moments[:, :], stats[:, :]))
            done(dve.tensor_scalar(rstd[:, :], moments[:, 1:2], LN_EPS, None, ALU.add), var_ready)
            dve.wait_ge(std_ready, 1)
            step(dve.reciprocal(rstd[:, :], rstd[:, :]))
            step(dve.tensor_scalar(y, y, moments[:, 0:1], rstd[:, :], ALU.subtract, ALU.mult))
            step(dve.tensor_tensor(y, y, gb[:, 0, :], ALU.mult))
            done(dve.tensor_tensor(y, y, gb[:, 1, :], ALU.add), y_ready)


def experts_phase(nc, t, d):
    ctx = ExitStack()
    with ctx:
        sb = lambda n, s, dt=F32: ctx.enter_context(nc.sbuf_tensor(n, s, dt))
        sem = lambda n: ctx.enter_context(nc.semaphore(n))
        k = pick_tiles(nc, ctx, "ep")
        TURNS = TBLOCKS * PEER_HEADS
        u, v = sb("u_ring", [P, TOPK, D]), sb("v_ring", [P, TOPK, D])
        diag = sb("diag", [P, TOPK, P])
        idx_u, idx_v = sb("idx_u", [P, 2, TOPK], U32), sb("idx_v", [P, 2, TOPK], U32)
        val, num = sb("head_val", [P, 2, TOPK]), sb("head_num", [P, 2, TOPK])
        best, neg_max = sb("head_best", [P, 2, TOPK]), sb("neg_max", [P, 2, 1])
        ex, total = sb("head_ex", [P, 2, TOPK]), sb("head_total", [P, 2, 1])
        hu, act_v = sb("hu", [P, 2, TOPK]), sb("act_v", [P, 2, TOPK])
        x, x_next, res, y, gb = sb("x_rows", [P, D]), sb("x_next", [P, D]), sb("res", [P, D]), sb("y_rows", [P, D]), sb("ln2_gb", [P, 2, D])
        stats, moments, rstd = sb("ep_stats", [P, 12]), sb("ep_moments", [P, 2]), sb("ep_rstd", [P, 1])
        out_ps = ctx.enter_context(nc.psum_tensor("ep_ps", [P, 2, 512], F32))
        u_landed = [sem(f"u_landed{s}") for s in range(TOPK)]
        v_landed = [sem(f"v_landed{s}") for s in range(TOPK)]
        consts, gb_loaded, x_loaded, x_taken = sem("ep_consts"), sem("gb_loaded"), sem("x_loaded"), sem("x_taken")
        turn_chain, block_chain, start_chain = sem("turn_chain"), sem("block_chain"), sem("start_chain")
        picked, idx_v_ready, dots, gelu_ready, act_ready, diag_ready, v_used = (
            sem("picked"), sem("idx_v_ready"), sem("dots"), sem("gelu_ready"), sem("act_ready"), sem("diag_ready"), sem("v_used"))
        exp_ready, sum_read, var_ready, std_ready, y_ready, y_stored, y_free = (
            sem("exp_ready"), sem("sum_read"), sem("ep_var"), sem("ep_std"), sem("ep_y"), sem("ep_y_stored"), sem("y_free"))
        waited_pool, waited_dve = sem("waited_pool"), sem("waited_dve")
        h1, y_out = d["h1_rows"], d["y_prompt"][0]
        block = ctx.enter_context(nc.Block())

        block_of = [None]

        def over_turns(eng, turn_body, finish):
            H = PEER_HEADS

            def rest_of_block(b, tail):
                turn_body(b * H + 1, 1, "", False)
                with eng.Fori(0, H // 2 - 2) as pair:
                    turn_body(b * H + pair * 2 + 2, 0, "", False)
                    turn_body(b * H + pair * 2 + 3, 1, "", False)
                turn_body(b * H + H - 2, 0, "", tail)
                turn_body(b * H + H - 1, 1, "last", tail)

            turn_body(0, 0, "first", False)
            with eng.Fori(0, TBLOCKS - 1) as b:
                block_of[0] = b
                rest_of_block(b, False)
                turn_body(b * H + H, 0, "first", False)
                finish(b)
            rest_of_block(TBLOCKS - 1, True)
            finish(TBLOCKS - 1)

        @block.sync
        def _(sp):
            for j, n in enumerate(("ln2_g", "ln2_b")):
                sp.dma_start(gb[:, j, :], d[n][0:1, :].broadcast_to([P, D])).then_inc(gb_loaded, 16)
            sp.dma_start(x_next[:, :], h1[0:P, :]).then_inc(x_loaded, 16)
            with sp.Fori(1, TBLOCKS) as b:
                sp.wait_ge(x_taken, b)
                sp.dma_start(x_next[:, :], h1[bass.ds(b * P, P), :]).then_inc(x_loaded, 16)
                sp.wait_ge(y_ready, b)
                sp.dma_start(y_out[bass.ds((b - 1) * P, P), :], y[:, :]).then_inc(y_stored, 16)
                sp.wait_ge(y_stored, b * 16)
                sp.sem_inc(y_free, 1)
            sp.wait_ge(y_ready, TBLOCKS)
            sp.dma_start(y_out[SEQ - P:SEQ, :], y[:, :]).then_inc(y_stored, 16)
            sp.wait_ge(y_stored, 16 * TBLOCKS)

        @block.gpsimd
        def _(pool):
            pool.iota(k.iota[:, :], [[1, TOPK]], base=0, channel_multiplier=0, allow_small_or_imprecise_dtypes=True).then_inc(consts, 1)
            pool.wait_ge(picked, 1)
            for s in range(TOPK):
                gather(pool, u[:, s, :], d["peer_u"][0], idx_u[:, 0, s:s + 1]).then_inc(u_landed[s], 16)

            def turn_body(turn, par, place, tail):
                for s in range(TOPK):
                    if not (tail and place == "last"):
                        if s == 0:
                            pool.wait_ge(picked, turn + 2)
                        pool.wait_ge(dots, turn * TOPK + s + 1)
                        pool.sem_inc(waited_pool, 1)
                        gather(pool, u[:, s, :], d["peer_u"][0], idx_u[:, 1 - par, s:s + 1]).then_inc(u_landed[s], 16)
                    if s == 0:
                        pool.wait_ge(idx_v_ready, turn + 1)
                    pool.wait_ge(v_used, turn * TOPK + s + 1)
                    pool.sem_inc(waited_pool, 1)
                    gather(pool, v[:, s, :], d["peer_v"][0], idx_v[:, par, s:s + 1]).then_inc(v_landed[s], 16)
            over_turns(pool, turn_body, lambda b: None)

        @block.tensor
        def _(pe):
            pe.sem_inc(v_used, TOPK)

            def turn_body(turn, par, place, tail):
                for s in range(TOPK):
                    if place == "first" and s == 0 and not isinstance(turn, int):
                        pe.wait_ge(sum_read, block_of[0] + 1)
                    pe.wait_ge(v_landed[s], (turn + 1) * 16)
                    pe.wait_ge(diag_ready, turn * TOPK + s + 1)
                    for half in range(2):
                        mm = pe.matmul(out_ps[:, half, :], diag[:, s, :], v[:, s, half * 512:(half + 1) * 512],
                                       start=place == "first" and s == 0, stop=place == "last" and s == TOPK - 1)
                    mm.then_inc(v_used, 1)
            over_turns(pe, turn_body, lambda b: None)

        @block.scalar
        def _(act):
            def exp_of(turn, par):
                act.wait_ge(picked, turn + 1)
                act.activation(ex[:, par, :], best[:, par, :], ACT.Exp, bias=neg_max[:, par, :], accum_out=total[:, par, :]).then_inc(exp_ready, 1)

            def turn_body(turn, par, place, tail):
                act.wait_ge(dots, (turn + 1) * TOPK)
                act.activation(act_v[:, par, :], hu[:, par, :], ACT.Gelu).then_inc(gelu_ready, 1)
                act.wait_ge(act_ready, turn + 1)
                for s in range(TOPK):
                    act.wait_ge(v_used, turn * TOPK + s + 1)
                    act.activation(diag[:, s, :], t.ident[:, :], ACT.Copy, scale=act_v[:, par, s:s + 1]).then_inc(diag_ready, 1)
                if not tail:
                    exp_of(turn + 2, par)

            def finish(b):
                act.wait_ge(var_ready, b + 1)
                act.activation(rstd[:, :], rstd[:, :], ACT.Sqrt).then_inc(std_ready, 1)

            exp_of(0, 0)
            exp_of(1, 1)
            over_turns(act, turn_body, finish)

        @block.vector
        def _(dve):
            done = signals(dve)
            PICK_STEPS = 18
            TURN_STEPS = PICK_STEPS + 1
            BLOCK_STEPS = 9

            def pick(turn, par, step):
                step(dve.tensor_copy(val[:, :, :], t.top_val[:, bass.ds(turn, 1), :, :].rearrange("p a b c -> p (a b) c")))
                step(dve.tensor_copy(num[:, :, :], t.top_idx[:, bass.ds(turn, 1), :, :].rearrange("p a b c -> p (a b) c")))
                step(pick_experts(dve, step, P, val, num, k, best[:, par, :], idx_u[:, par, :]))
                step(dve.tensor_scalar(neg_max[:, par, :], best[:, par, 0:1], -1.0, None, ALU.mult))
                dve.sem_inc(picked, 1)

            def counted(sem, base):
                n = [0]

                def step(ins):
                    n[0] += 1
                    ins.then_inc(sem, 1)
                    dve.wait_ge(sem, base + n[0])
                    dve.sem_inc(waited_dve, 1)
                return step, n

            def turn_body(turn, par, place, tail):
                if place == "first" and not isinstance(turn, int):
                    take_rows(block_of[0] + 1)
                for s in range(TOPK):
                    dve.wait_ge(u_landed[s], (turn + 1) * 16)
                    dve.tensor_tensor_reduce(u[:, s, :], u[:, s, :], x[:, :], 1.0, 0.0, ALU.mult, ALU.add,
                                             hu[:, par, s:s + 1]).then_inc(dots, 1)
                step, n = counted(turn_chain, turn * TURN_STEPS)
                if not (tail and place == "last"):
                    dve.wait_ge(v_used, (turn + 1) * TOPK)
                    dve.tensor_copy(idx_v[:, 1 - par, :], idx_u[:, 1 - par, :]).then_inc(idx_v_ready, 1)
                dve.wait_ge(exp_ready, turn + 1)
                step(dve.reciprocal(total[:, par, :], total[:, par, :]))
                dve.wait_ge(gelu_ready, turn + 1)
                dve.scalar_tensor_tensor(out=act_v[:, par, :], in0=act_v[:, par, :], scalar=total[:, par, :], in1=ex[:, par, :],
                                         op0=ALU.mult, op1=ALU.mult).then_inc(act_ready, 1)
                if not tail:
                    pick(turn + 2, par, step)
                    assert n[0] == TURN_STEPS, n
                else:
                    dve.sem_inc(turn_chain, TURN_STEPS - n[0])

            def take_rows(b):
                step, _ = counted(block_chain, (b - 1) * BLOCK_STEPS)
                step(dve.tensor_scalar(res[:, :], x[:, :], ALPHA, None, ALU.mult))
                dve.wait_ge(x_loaded, (b + 1) * 16)
                done_take(dve.tensor_copy(x[:, :], x_next[:, :]), b)

            def done_take(ins, b):
                ins.then_inc(x_taken, 1)
                dve.wait_ge(x_taken, b + 1)

            def finish(b):
                last = isinstance(b, int)
                step, n = counted(block_chain, b * BLOCK_STEPS + 1)
                if last:
                    dve.tensor_scalar(res[:, :], x[:, :], ALPHA, None, ALU.mult).then_inc(block_chain, 1)
                    dve.wait_ge(block_chain, b * BLOCK_STEPS + 1)
                dve.wait_ge(v_used, (b + 1) * (PEER_HEADS * TOPK) + TOPK)
                dve.wait_ge(y_free, b + 1)
                dve.tensor_tensor(y[:, :], out_ps[:, :, :].rearrange("p a b -> p (a b)"), res[:, :], ALU.add).then_inc(sum_read, 1)
                dve.wait_ge(sum_read, b + 1)
                step(dve.bn_stats(stats[:, 0:6], y[:, 0:512]))
                step(dve.bn_stats(stats[:, 6:12], y[:, 512:1024]))
                step(dve.bn_aggr(moments[:, :], stats[:, :]))
                dve.tensor_scalar(rstd[:, :], moments[:, 1:2], LN_EPS, None, ALU.add).then_inc(var_ready, 1)
                dve.wait_ge(std_ready, b + 1)
                step(dve.reciprocal(rstd[:, :], rstd[:, :]))
                step(dve.tensor_scalar(y[:, :], y[:, :], moments[:, 0:1], rstd[:, :], ALU.subtract, ALU.mult))
                step(dve.tensor_tensor(y[:, :], y[:, :], gb[:, 0, :], ALU.mult))
                dve.tensor_tensor(y[:, :], y[:, :], gb[:, 1, :], ALU.add).then_inc(y_ready, 1)
                assert n[0] + 1 <= BLOCK_STEPS
                if not last:
                    dve.sem_inc(block_chain, BLOCK_STEPS - 1 - n[0])

            dve.wait_ge(consts, 1)
            dve.sem_inc(y_free, 1)
            for turn in range(2):
                pick(turn, turn, lambda ins: done(ins, start_chain))
            dve.tensor_copy(idx_v[:, 0, :], idx_u[:, 0, :]).then_inc(idx_v_ready, 1)
            dve.wait_ge(gb_loaded, 32)
            dve.wait_ge(x_loaded, 16)
            done_take(dve.tensor_copy(x[:, :], x_next[:, :]), 0)
            over_turns(dve, turn_body, finish)


PARAMS = ["w0", "a0", "k_k", "k_a", "r_k", "gn_g", "gn_b", "mu_r", "mu_k", "mu_v", "cw0", "cw1", "cw2"]

PAR_COLS = len(PARAMS) * PAIRS + 2


class Tiles:
    pass


def clear_semaphores(nc):
    used = sorted(nc.released_uncleared_semaphores)
    while used:
        n = 1
        while n < len(used) and used[n] == used[0] + n:
            n += 1
        nc.gpsimd.sem_clear(range(used[0], used[0] + n))
        used = used[n:]
    nc.all_engine_barrier()


def build(nc, d):
    t = Tiles()
    outer, upto2, upto4, upto5, upto6 = (ExitStack() for _ in range(5))
    with outer:
        sb = lambda n, s, c=outer: c.enter_context(nc.sbuf_tensor(n, s, F32))
        t.h_stored, t.h1_stored, t.sp_landed = ([outer.enter_context(nc.semaphore(f"{n}{i}")) for i in range(c)]
                                                for n, c in (("h_stored", 3), ("h1_stored", 2), ("sp_landed", 2)))
        t.ident, t.head_ones = sb("ident", [P, P]), sb("head_ones", [P, P])
        t.par = sb("par", [P, PAR_COLS])
        t.mu_lora = t.par[:, PAR_COLS - 2:]
        t.samp = sb("samp", [P, 6, NS, PAIRS])
        t.p_end = sb("p_end", [P, PAIRS, CHUNKS])
        t.z_out = sb("z_out", [P, PAIRS, NS + 2])
        t.conv_state = sb("conv_state", [P, PAIRS, 2 * NS])
        t.top_val = sb("top_val", [P, (TBLOCKS + 1) * PEER_HEADS, 2, TOPK])
        t.top_idx = sb("top_idx", [P, (TBLOCKS + 1) * PEER_HEADS, 2, TOPK])
        with upto5:
            t.yc = sb("yc", [P, PAIRS, PROJ_COLS], upto5)
            t.alpha = sb("alpha", [P, PAIRS, WKV_COLS], upto5)
            with upto4:
                t.lora_g = sb("lora_g", [G_LORA, PROJ_COLS], upto4)
                t.rho, t.beta = sb("rho", [P, PAIRS, WKV_COLS], upto4), sb("beta", [P, PAIRS, WKV_COLS], upto4)
                t.kappa, t.vT = sb("kappa", [P, PAIRS, WKV_COLS], upto4), sb("vT", [P, PAIRS, WKV_COLS], upto4)
                with upto2:
                    t.hT = sb("hT", [P, KT, PROJ_COLS], upto2)
                    input_phase(nc, t, d)
                    project_phase(nc, t, d)
                wkv_phase(nc, t, d)
                sample_phase(nc, t, d)
                norm_phase(nc, t, d)
            with upto6:
                t.h1T = sb("h1T", [P, KT, SEQ + NS], upto6)
                mix_phase(nc, t, d)
                keys_phase(nc, t, d)
        sample_experts_phase(nc, t, d)
        clear_semaphores(nc)
        experts_phase(nc, t, d)


_INS = ['x_prompt', 'x_sample', 'state_conv', 'state_shift', 'state_wkv', 'meta_tokens', 'ln_in_g', 'ln_in_b',
        'w_in', 'conv_w', 'mu', 'w0', 'w_up', 'a0', 'a_up', 'g_up', 'k_k', 'k_a', 'r_k', 'gn_g', 'gn_b', 'w_o',
        'ln1_g', 'ln1_b', 'w_q', 'sub_keys', 'peer_u', 'peer_v', 'ln2_g', 'ln2_b']
_OUTS = [("y_prompt", (1, SEQ, D)), ("y_sample", (NS, 1, D)), ("new_conv_prompt", (1, 1, 2, CONVW)),
         ("new_shift_prompt", (1, 1, D)), ("new_wkv_prompt", (1, 1, HEADS, HD, HD)),
         ("new_conv_sample", (1, NS, 2, CONVW)), ("new_shift_sample", (1, NS, D)),
         ("new_wkv_sample", (1, NS, HEADS, HD, HD))]
_SCRATCH = [("h_rows", (PROJ_COLS, D), F32), ("samp_rows", (NS * PAIRS, 2, 6, HD), F32), ("h1_rows", (SEQ + NS, D), F32),
            ("sp_idx", (NS, SLOTS), U32), ("sp_gate", (NS, SLOTS), F32)]


def kernel(**inputs):
    import numpy as _np
    import concourse.bacc as _bacc
    from concourse import mybir as _mybir
    from concourse.bass_utils import run_bass_kernel_spmd as _run

    nc = _bacc.Bacc("TRN2", target_bir_lowering=False, num_devices=1)
    arrays, tensors = {}, {}
    for name in _INS:
        a = _np.ascontiguousarray(inputs[name])
        arrays[f"in_{name}_dram"] = a
        tensors[name] = nc.dram_tensor(f"in_{name}_dram", a.shape, _mybir.dt.from_np(a.dtype), kind="ExternalInput").ap()
    for i, (name, shape) in enumerate(_OUTS):
        tensors[name] = nc.dram_tensor(f"out_{i}_dram", shape, _mybir.dt.float32, kind="ExternalOutput").ap()
    for name, shape, dt in _SCRATCH:
        tensors[name] = nc.dram_tensor(f"scratch_{name}", shape, dt, kind="Internal").ap()
    build(nc, tensors)
    r = _run(nc, [arrays], core_ids=[0])
    return tuple(r.results[0][f"out_{i}_dram"] for i in range(len(_OUTS)))
```

```python
from contextlib import ExitStack
import math

import concourse.bass as bass
from concourse import mybir

F32 = mybir.dt.float32
U32 = mybir.dt.uint32
ALU = mybir.AluOpType
ACT = mybir.ActivationFunctionType
AX_X = mybir.AxisListType.X

P = 128
D = 1024
KT = D // P
SEQ = 1024
NS = 8
N_META = 16
CONVW = 512
RW = 512
PAIRS = RW // P
HD = 64
HEADS = 8
W_LORA = A_LORA = 32
G_LORA = 96
IN_COLS = 3 * CONVW + 3 * RW + W_LORA + A_LORA + G_LORA
RW0 = 3 * CONVW
LORA0 = RW0 + 3 * RW
C_META = 2 * NS
C_PROMPT = C_META + N_META
PROJ_COLS = C_PROMPT + SEQ
COLS3 = PROJ_COLS // 3
CHUNK = 64
WKV_OFF = 32
WKV_COLS = PROJ_COLS + WKV_OFF
CHUNKS = WKV_COLS // CHUNK
W_META = C_META + WKV_OFF
LN_EPS = 1e-5
GN_EPS = HD * 1e-5
ALPHA = 2.0 ** 0.25
LOG_DECAY = math.exp(-0.5)
PEER_HEADS = 8
N_KEYS = 128
TOPK = 16
SLOTS = PEER_HEADS * TOPK
TBLOCKS = SEQ // P
HP = 2 * PEER_HEADS
NEG = -3.0e38


def signals(eng):
    count = {}

    def done(ins, sem):
        count[sem.name] = count.get(sem.name, 0) + 1
        ins.then_inc(sem, 1)
        eng.wait_ge(sem, count[sem.name])
    return done


def chained(eng, sem):
    count = [0]

    def step(ins):
        count[0] += 1
        ins.then_inc(sem, 1)
        eng.wait_ge(sem, count[0])
    return step


def input_phase(nc, t, d):
    ctx = ExitStack()
    with ctx:
        NX = 3
        xrow = ctx.enter_context(nc.sbuf_tensor("xrow", [P, NX, D], F32))
        ln_gb = ctx.enter_context(nc.sbuf_tensor("ln_gb", [P, 2, D], F32))
        stats = ctx.enter_context(nc.sbuf_tensor("stats", [P, NX, 12], F32))
        moments = ctx.enter_context(nc.sbuf_tensor("moments", [P, NX, 2], F32))
        rstd = ctx.enter_context(nc.sbuf_tensor("rstd", [P, NX, 1], F32))
        conv_rows = ctx.enter_context(nc.sbuf_tensor("conv_rows", [2 * NS, CONVW], F32))
        key_rows = ctx.enter_context(nc.sbuf_tensor("key_rows", [N_KEYS, HP, P], F32))
        par_rows = ctx.enter_context(nc.sbuf_tensor("par_rows", [PAR_COLS, P], F32))
        turned = ctx.enter_context(nc.psum_tensor("turned", [P, 2, 512], F32))
        keys_ps = ctx.enter_context(nc.psum_tensor("keys_ps", [P, 2, 4, N_KEYS], F32))
        turned2 = ctx.enter_context(nc.psum_tensor("turned2", [P, 2, 512], F32))
        sem = lambda n: ctx.enter_context(nc.semaphore(n))
        const_loaded, conv_loaded = sem("const_loaded"), sem("conv_loaded")
        x_loaded = [sem(f"x_loaded{i}") for i in range(NX)]
        shift_loaded, ident_done, var_ready, std_ready = sem("shift_loaded"), sem("ident_done"), sem("var_ready"), sem("std_ready")
        vec_chain, norm_ready, turned_ready, turned_read = sem("vec_chain"), sem("norm_ready"), sem("turned_ready"), sem("turned_read")
        h_stored = t.h_stored
        rows_cleared, keys_loaded, keys_turned, keys_read = sem("rows_cleared"), sem("keys_loaded"), sem("keys_turned"), sem("keys_read")
        block = ctx.enter_context(nc.Block())
        TILES = 1 + TBLOCKS
        rows = [C_PROMPT] + [P] * TBLOCKS

        @block.sync
        def _(sp):
            sp.dma_start(ln_gb[:, 0, :], d["ln_in_g"][None, :].broadcast_to([P, D])).then_inc(const_loaded, 16)
            sp.dma_start(ln_gb[:, 1, :], d["ln_in_b"][None, :].broadcast_to([P, D])).then_inc(const_loaded, 16)
            def load_tile(i):
                s = i % NX
                if i >= NX:
                    sp.wait_ge(turned_ready, 2 * (i - NX + 1))
                    sp.wait_ge(h_stored[s], 16 * (i // NX))
                if i == 0:
                    sp.dma_start(xrow[0:NS, s, :], d["x_sample"][:, 0, :]).then_inc(x_loaded[s], 16)
                    sp.dma_start(xrow[NS:2 * NS, s, :], d["state_shift"][0]).then_inc(x_loaded[s], 16)
                    sp.dma_start(xrow[C_META:C_PROMPT, s, :], d["meta_tokens"]).then_inc(x_loaded[s], 16)
                else:
                    sp.dma_start(xrow[:, s, :], d["x_prompt"][0, (i - 1) * P:i * P, :]).then_inc(x_loaded[s], 16)
            for i in range(NX):
                load_tile(i)
            sp.dma_start(conv_rows[:, :], d["state_conv"][0].rearrange("b j c -> (b j) c")).then_inc(conv_loaded, 16)
            sp.wait_ge(rows_cleared, 1)
            for n in PARAMS:
                src = {"mu_r": d["mu"][0, 0:RW], "mu_k": d["mu"][0, RW:2 * RW], "mu_v": d["mu"][0, 2 * RW:3 * RW],
                       "r_k": d["r_k"][0].rearrange("h k -> (h k)"),
                       "cw0": d["conv_w"][0, 0], "cw1": d["conv_w"][0, 1], "cw2": d["conv_w"][0, 2]}.get(n)
                src = d[n][0] if src is None else src
                r0 = PARAMS.index(n) * PAIRS
                sp.dma_start(par_rows[r0:r0 + PAIRS, :], src.rearrange("(c p) -> c p", p=P)).then_inc(conv_loaded, 16)
            mu1 = d["mu"][0:1, 3 * RW:]
            sp.dma_start(par_rows[PAR_COLS - 2:PAR_COLS - 1, 0:2 * W_LORA], mu1[:, 0:2 * W_LORA]).then_inc(conv_loaded, 16)
            sp.dma_start(par_rows[PAR_COLS - 1:PAR_COLS, 0:G_LORA], mu1[:, 2 * W_LORA:]).then_inc(conv_loaded, 16)
            sp.dma_start(key_rows[:, :, :], d["sub_keys"][0].rearrange("h s n k -> n (h s) k")).then_inc(keys_loaded, 16)
            sp.wait_ge(norm_ready, 1)
            sp.dma_start(xrow[NS:2 * NS, 0, :], d["state_shift"][0]).then_inc(shift_loaded, 16)
            for i in range(NX, TILES):
                load_tile(i)

        @block.gpsimd
        def _(pool):
            done = signals(pool)
            done(pool.memset(t.ident[:, :], 0.0), ident_done)
            done(pool.affine_select(out=t.ident[:, :], in_=t.ident[:, :], compare_op=ALU.not_equal, fill=1.0,
                                    base=0, pattern=[[-1, P]], channel_multiplier=1), ident_done)
            done(pool.memset(t.head_ones[:, :], 0.0), ident_done)
            done(pool.memset(t.head_ones[0:HD, 0:HD], 1.0), ident_done)
            done(pool.memset(t.head_ones[HD:P, HD:P], 1.0), ident_done)
            for i in range(TILES):
                pool.wait_ge(norm_ready, i + 1)
                n = rows[i]
                c0 = 0 if i == 0 else C_PROMPT + (i - 1) * P
                if i == 0:
                    pool.dma_start(d["h_rows"][0:NS, :], xrow[0:NS, 0, :]).then_inc(h_stored[0], 16)
                else:
                    pool.dma_start(d["h_rows"][c0:c0 + n, :], xrow[:, i % NX, :]).then_inc(h_stored[i % NX], 16)
            for s in range(NX):
                pool.wait_ge(h_stored[s], 16 * len(range(s, TILES, NX)))

        @block.vector
        def _(dve):
            step = chained(dve, vec_chain)
            dve.memset(par_rows[32:PAR_COLS, :], 0.0).then_inc(rows_cleared, 1)
            dve.wait_ge(const_loaded, 32)
            for i in range(TILES):
                s, n = i % NX, rows[i]
                dve.wait_ge(x_loaded[s], 48 + 16 * (i // NX) if s == 0 else 16 * (i // NX + 1))
                x = xrow[0:n, s, :]
                dve.bn_stats(stats[0:n, s, 0:6], x[:, 0:512])
                step(dve.bn_stats(stats[0:n, s, 6:12], x[:, 512:1024]))
                step(dve.bn_aggr(moments[0:n, s, :], stats[0:n, s, :]))
                dve.tensor_scalar(rstd[0:n, s, :], moments[0:n, s, 1:2], LN_EPS, None, ALU.add).then_inc(var_ready, 1)
                dve.wait_ge(std_ready, i + 1)
                step(dve.reciprocal(rstd[0:n, s, :], rstd[0:n, s, :]))
                step(dve.tensor_scalar(x, x, moments[0:n, s, 0:1], rstd[0:n, s, :], ALU.subtract, ALU.mult))
                step(dve.tensor_tensor(x, x, ln_gb[0:n, 0, :], ALU.mult))
                dve.tensor_tensor(x, x, ln_gb[0:n, 1, :], ALU.add).then_inc(norm_ready, 1)

        @block.tensor
        def _(pe):
            pe.wait_ge(ident_done, 5)
            for i in range(TILES):
                s, n = i % NX, rows[i]
                pe.wait_ge(norm_ready, i + 1)
                if i == 0:
                    pe.wait_ge(shift_loaded, 16)
                for half in range(2):
                    if i >= 1:
                        pe.wait_ge(turned_read, 2 * i - 1 + half)
                    buf = (turned, turned2)[half]
                    for k in range(4):
                        kt = half * 4 + k
                        last = pe.transpose(buf[:, 0, k * P:k * P + n], xrow[0:n, s, kt * P:(kt + 1) * P], t.ident[0:n, 0:n])
                    last.then_inc(turned_ready, 1)
            pe.wait_ge(conv_loaded, 16 * (len(PARAMS) + 3))
            for c in range(4):
                last = pe.transpose(turned[:, 1, c * 16:c * 16 + 16], conv_rows[:, c * P:(c + 1) * P], t.ident[0:16, 0:16])
            pe.transpose(turned[:, 1, 64:64 + PAR_COLS], par_rows[:, :], t.ident[0:PAR_COLS, 0:PAR_COLS]).then_inc(turned_ready, 1)
            pe.wait_ge(keys_loaded, 16)
            for g in range(HP // 4):
                if g >= 2:
                    pe.wait_ge(keys_read, g - 1)
                for n in range(4):
                    last = pe.transpose(keys_ps[:, g % 2, n, :], key_rows[:, 4 * g + n, :], t.ident[:, :])
                last.then_inc(keys_turned, 1)

        @block.scalar
        def _(act):
            act_chain = ctx.enter_context(nc.semaphore("in_act_chain"))
            for i in range(TILES):
                s, n = i % NX, rows[i]
                c0 = 0 if i == 0 else C_PROMPT + (i - 1) * P
                act.wait_ge(var_ready, i + 1)
                act.activation(rstd[0:n, s, :], rstd[0:n, s, :], ACT.Sqrt).then_inc(std_ready, 1)
                for half in range(2):
                    buf = (turned, turned2)[half]
                    act.wait_ge(turned_ready, 2 * i + 1 + half)
                    act.activation(t.hT[:, half * 4:half * 4 + 4, c0:c0 + n],
                                   buf[:, 0, :].rearrange("p (k n) -> p k n", k=4)[:, :, 0:n], ACT.Copy).then_inc(turned_read, 1)
            act.wait_ge(turned_ready, 2 * TILES + 1)
            act.activation(t.par[:, :], turned[:, 1, 64:64 + PAR_COLS], ACT.Copy).then_inc(act_chain, 1)
            act.activation(t.conv_state[:, :, :], turned[:, 1, 0:64].rearrange("p (c n) -> p c n", c=4), ACT.Copy).then_inc(act_chain, 1)
            act.wait_ge(act_chain, 2)
            for g in range(HP // 4):
                act.wait_ge(keys_turned, g + 1)
                act.activation(t.keysT[:, 4 * g:4 * g + 4, :], keys_ps[:, g % 2, :, :], ACT.Copy).then_inc(keys_read, 1)


def project_phase(nc, t, d):
    ctx = ExitStack()
    with ctx:
        sb = lambda n, s: ctx.enter_context(nc.sbuf_tensor(n, s, F32))
        sem = lambda n: ctx.enter_context(nc.semaphore(n))
        NW = 3
        OPERANDS = ("alpha", "beta", "kappa", "rho", "vT")
        alpha, beta, kappa, rho, vT = (sb(n, [P, 2, WKV_COLS]) for n in OPERANDS)
        yc = sb("yc", [P, 2, PROJ_COLS])
        lora_g = sb("lora_g", [G_LORA, PROJ_COLS])
        pair_ready, y_done = sem("pair_ready"), sem("y_done")
        w_ring = sb("w_ring", [P, NW, KT, P])
        lora_up = sb("lora_up", [2 * W_LORA, RW])
        lora_wa = sb("lora_wa", [2 * W_LORA, PROJ_COLS])
        raw = sb("raw", [P, 2, PROJ_COLS])
        diff = sb("diff", [P, PROJ_COLS])
        sig = sb("sig", [P, PROJ_COLS])
        csig = sb("csig", [P, PROJ_COLS])
        p_inv = sb("p_inv", [P, PROJ_COLS])
        aa = sb("aa", [P, PROJ_COLS])
        keep = sb("keep", [P, PROJ_COLS])
        jobs_ps = [ctx.enter_context(nc.psum_tensor(f"job_ps{i}", [P, 3, 512], F32)) for i in range(2)]
        w_loaded = [sem(f"w_loaded{i}") for i in range(NW)]
        par_loaded = sem("par_loaded")
        job_done = sem("job_done")
        job_read = [sem("job_read0"), sem("job_read1")]
        raw_ready, raw_used, vec_chain, act_chain = sem("raw_ready"), sem("raw_used"), sem("vec_chain2"), sem("act_chain2")
        lora_mixed, lora_ready, kk_ready, square_ready = sem("lora_mixed"), sem("lora_ready"), sem("kk_ready"), sem("square_ready")
        sig_ready, sig_used, aa_ready, aa_used = sem("sig_ready"), sem("sig_used"), sem("aa_ready"), sem("aa_used")
        csig_ready, p_inv_ready, p_inv_used = sem("csig_ready"), sem("p_inv_ready"), sem("p_inv_used")
        p_prev_ready, p_cum_ready, p_cum_used, z_ready = sem("p_prev_ready"), sem("p_cum_ready"), sem("p_cum_used"), sem("z_ready")

        jobs = [("wa", 0, LORA0, 2 * W_LORA), ("gd", 0, LORA0 + 2 * W_LORA, G_LORA)]
        for c in range(PAIRS):
            jobs += [("k", c, RW0 + RW + c * P, P), ("w", c, None, P), ("a", c, None, P), ("r", c, RW0 + c * P, P),
                     ("norm", c, None, P), ("v", c, RW0 + 2 * RW + c * P, P)]
        for c in range(PAIRS):
            jobs += [("cg", c, CONVW + c * P, P), ("hv", c, 2 * CONVW + c * P, P), ("bg", c, c * P, P)]
        streamed = [i for i, job in enumerate(jobs) if job[2] is not None]
        in_raw = [i for i, job in enumerate(jobs) if job[0] not in ("w", "a", "hv", "bg")]

        def param(n, c):
            return t.par[:, PARAMS.index(n) * PAIRS + c:PARAMS.index(n) * PAIRS + c + 1]

        def ps(i, n=P):
            return jobs_ps[i % 2][0:n, :, 0:COLS3]

        def three(x):
            return x.rearrange("p (a b) -> p a b", a=3)

        block = ctx.enter_context(nc.Block())

        @block.sync
        def _(sp):
            for n, i in enumerate(streamed):
                _, _, c0, m = jobs[i]
                if n >= NW:
                    sp.wait_ge(job_done, streamed[n - NW] + 1)
                sp.dma_start(w_ring[:, n % NW, :, 0:m],
                             d["w_in"][0, :, c0:c0 + m].rearrange("(k p) c -> p k c", p=P)).then_inc(w_loaded[n % NW], 16)
                if n == 0:
                    sp.dma_start(lora_up[0:W_LORA, :], d["w_up"][0]).then_inc(par_loaded, 16)
                    sp.dma_start(lora_up[W_LORA:2 * W_LORA, :], d["a_up"][0]).then_inc(par_loaded, 16)

        @block.gpsimd
        def _(pool):
            pool.wait_ge(lora_ready, 2)
            pool.dma_start(d["lora_g"], lora_g[:, :]).then_inc(t.y_spilled[0], 16)
            for c in range(PAIRS):
                pool.wait_ge(pair_ready, c + 1)
                for j, x in enumerate((alpha, beta, kappa, rho, vT)):
                    pool.dma_start(d["operands"][j, :, c, :], x[:, c % 2, :]).then_inc(t.spilled[c % 2], 16)
            for c in range(PAIRS):
                pool.wait_ge(y_done, c + 1)
                pool.dma_start(d["y_conv"][:, c, :], yc[:, c % 2, :]).then_inc(t.y_spilled[c % 2], 16)
            for s in range(2):
                pool.wait_ge(t.spilled[s], 160)
            pool.wait_ge(t.y_spilled[0], 48)
            pool.wait_ge(t.y_spilled[1], 32)

        @block.tensor
        def _(pe):
            for i, (kind, c, c0, m) in enumerate(jobs):
                if i >= 2:
                    pe.wait_ge(job_read[i % 2], i // 2)
                if c0 is not None:
                    n = streamed.index(i)
                    pe.wait_ge(w_loaded[n % NW], 16 * (n // NW + 1))
                    for k in range(KT):
                        for a in range(3):
                            last = pe.matmul(jobs_ps[i % 2][0:m, a, 0:COLS3], w_ring[:, n % NW, k, 0:m],
                                             t.hT[:, k, a * COLS3:(a + 1) * COLS3], start=(k == 0), stop=(k == KT - 1))
                else:
                    if kind == "norm":
                        pe.wait_ge(square_ready, c + 1)
                        lhsT, rhs = t.head_ones[:, :], p_inv[:, :]
                    else:
                        if i == 3:
                            pe.wait_ge(lora_ready, 1)
                            pe.wait_ge(lora_mixed, 1)
                            pe.wait_ge(par_loaded, 32)
                        rows = slice(0, W_LORA) if kind == "w" else slice(W_LORA, 2 * W_LORA)
                        lhsT, rhs = lora_up[rows, c * P:(c + 1) * P], lora_wa[rows, :]
                    for a in range(3):
                        last = pe.matmul(jobs_ps[i % 2][:, a, 0:COLS3], lhsT, rhs[:, a * COLS3:(a + 1) * COLS3],
                                         start=True, stop=True)
                last.then_inc(job_done, 1)

        @block.scalar
        def _(act):
            done = signals(act)
            done(act.activation(t.samp[:, 5, 0:1, 0], t.ident[:, 0:1], ACT.Copy), act_chain)
            for i, (kind, c, _, m) in enumerate(jobs):
                if i in in_raw:
                    n = in_raw.index(i)
                    if n >= 2:
                        act.wait_ge(raw_used, n - 1)
                    act.wait_ge(job_done, i + 1)
                    done(act.activation(three(raw[0:m, n % 2, :]), ps(i, m), ACT.Sqrt if kind == "norm" else ACT.Copy), raw_ready)
                    act.sem_inc(job_read[i % 2], 1)
                if kind == "wa":
                    act.wait_ge(lora_mixed, 1)
                    act.activation(lora_wa[0:W_LORA, :], lora_wa[0:W_LORA, :], ACT.Tanh).then_inc(lora_ready, 1)
                elif kind == "gd":
                    act.wait_ge(lora_mixed, 2)
                    act.activation(lora_g[0:G_LORA, :], lora_g[0:G_LORA, :], ACT.Sigmoid).then_inc(lora_ready, 1)
                elif kind == "k":
                    act.wait_ge(kk_ready, c + 1)
                    if c:
                        act.wait_ge(p_inv_used, c)
                    act.activation(p_inv[:, :], alpha[:, c % 2, WKV_OFF:], ACT.Square).then_inc(square_ready, 1)
                elif kind == "w":
                    if c:
                        act.wait_ge(sig_used, c)
                    act.wait_ge(job_done, i + 1)
                    done(act.activation(three(sig[:, :]), ps(i), ACT.Sigmoid, bias=param("w0", c)), sig_ready)
                    act.sem_inc(job_read[i % 2], 1)
                    act.wait_ge(sig_ready, c + 1)
                    act.activation(t.samp[:, 5, :, c], sig[:, 0:NS], ACT.Exp, scale=-LOG_DECAY).then_inc(act_chain, 1)
                elif kind == "a":
                    if c:
                        act.wait_ge(aa_used, c)
                    act.wait_ge(job_done, i + 1)
                    done(act.activation(three(aa[:, :]), ps(i), ACT.Sigmoid, bias=param("a0", c)), aa_ready)
                    act.sem_inc(job_read[i % 2], 1)
                elif kind == "norm":
                    act.wait_ge(csig_ready, c + 1)
                    act.activation(p_inv[:, :], csig[:, :], ACT.Exp, scale=LOG_DECAY).then_inc(p_inv_ready, 1)
                    act.activation(sig[:, :], sig[:, :], ACT.Exp, scale=-LOG_DECAY).then_inc(p_prev_ready, 1)
                    act.wait_ge(p_inv_ready, c + 1)
                    act.activation(csig[:, :], csig[:, :], ACT.Exp, scale=-LOG_DECAY).then_inc(p_cum_ready, 1)

        @block.vector
        def _(dve):
            done = signals(dve)
            step = lambda ins: done(ins, vec_chain)
            step(dve.memset(keep[:, :], 1.0))
            step(dve.memset(keep[:, C_META:C_META + 1], 0.0))
            step(dve.memset(keep[:, C_PROMPT:].rearrange("p (a b) -> p a b", b=CHUNK)[:, :, 0:1], 0.0))
            step(dve.memset(diff[:, NS:2 * NS], 0.0))
            for x in (alpha, beta, kappa, rho, vT):
                step(dve.memset(x[:, :, 0:WKV_OFF], 0.0))

            def shift_mix(i, p, m, mu, out):
                dve.wait_ge(raw_ready, in_raw.index(i) + 1)
                step(dve.tensor_tensor(diff[0:m, 0:NS], p[0:m, NS:2 * NS], p[0:m, 0:NS], ALU.subtract))
                step(dve.memset(p[0:m, C_META - 1:C_META], 0.0))
                step(dve.tensor_tensor(diff[0:m, C_META:], p[0:m, C_META - 1:PROJ_COLS - 1], p[0:m, C_META:], ALU.subtract))
                done(dve.scalar_tensor_tensor(out=out, in0=diff[0:m, :], scalar=mu, in1=p[0:m, :], op0=ALU.mult, op1=ALU.add), raw_used)

            for i, (kind, c, _, m) in enumerate(jobs):
                al, be, ka, rh, vt = (x[:, c % 2, WKV_OFF:] for x in (alpha, beta, kappa, rho, vT))
                p = raw[:, in_raw.index(i) % 2, :] if i in in_raw else None
                if kind == "wa":
                    shift_mix(i, p, m, t.mu_lora[0:m, 0:1], lora_wa[:, :])
                    dve.sem_inc(lora_mixed, 1)
                elif kind == "gd":
                    shift_mix(i, p, m, t.mu_lora[0:m, 1:2], lora_g[0:m, :])
                    dve.sem_inc(lora_mixed, 1)
                elif kind == "k":
                    if c >= 2:
                        dve.wait_ge(t.spilled[c % 2], 16 * 5)
                    shift_mix(i, p, P, param("mu_k", c), ka)
                    done(dve.tensor_scalar(al, ka, param("k_k", c), None, ALU.mult), kk_ready)
                elif kind == "w":
                    dve.wait_ge(sig_ready, c + 1)
                    dve.wait_ge(act_chain, c + 2)
                    if c:
                        dve.wait_ge(p_cum_used, c)
                    step(dve.tensor_tensor_scan(csig[:, :], keep[:, :], sig[:, :], 0.0, ALU.mult, ALU.add))
                    done(dve.tensor_tensor(sig[:, :], csig[:, :], sig[:, :], ALU.subtract), csig_ready)
                elif kind == "a":
                    dve.wait_ge(aa_ready, c + 1)
                    step(dve.tensor_scalar(diff[:, :], aa[:, :], 1.0, param("k_a", c), ALU.subtract, ALU.mult))
                    step(dve.scalar_tensor_tensor(out=ka, in0=diff[:, :], scalar=1.0, in1=ka, op0=ALU.add, op1=ALU.mult))
                    step(dve.memset(diff[:, NS:2 * NS], 0.0))
                elif kind == "r":
                    shift_mix(i, p, P, param("mu_r", c), rh)
                    step(dve.tensor_copy(t.samp[:, 0, :, c], rh[:, 0:NS]))
                elif kind == "norm":
                    dve.wait_ge(raw_ready, in_raw.index(i) + 1)
                    step(dve.tensor_scalar(p, p, 1e-12, None, ALU.max))
                    step(dve.reciprocal(p, p))
                    done(dve.tensor_tensor(al, al, p, ALU.mult), raw_used)
                    done(dve.tensor_tensor(be, al, aa[:, :], ALU.mult), aa_used)
                    step(dve.tensor_copy(t.samp[:, 1, :, c], ka[:, 0:NS]))
                    step(dve.tensor_copy(t.samp[:, 3, :, c], al[:, 0:NS]))
                    step(dve.tensor_copy(t.samp[:, 4, :, c], be[:, 0:NS]))
                    dve.wait_ge(p_inv_ready, c + 1)
                    step(dve.tensor_tensor(ka, ka, p_inv[:, :], ALU.mult))
                    done(dve.tensor_tensor(be, be, p_inv[:, :], ALU.mult), p_inv_used)
                    dve.wait_ge(p_prev_ready, c + 1)
                    done(dve.scalar_tensor_tensor(out=al, in0=al, scalar=-1.0, in1=sig[:, :], op0=ALU.mult, op1=ALU.mult), sig_used)
                    dve.wait_ge(p_cum_ready, c + 1)
                    step(dve.tensor_tensor(rh, rh, csig[:, :], ALU.mult))
                    done(dve.tensor_copy(t.p_end[:, c, :], csig[:, C_PROMPT - 1:PROJ_COLS:CHUNK]), p_cum_used)
                elif kind == "v":
                    shift_mix(i, p, P, param("mu_v", c), vt)
                    step(dve.tensor_copy(t.samp[:, 2, :, c], vt[:, 0:NS]))
                    for x in (al, be, ka, rh, vt):
                        step(dve.memset(x[:, 0:C_META], 0.0))
                    dve.sem_inc(pair_ready, 1)
                elif kind == "cg":
                    dve.wait_ge(raw_ready, in_raw.index(i) + 1)
                elif kind == "hv":
                    z, y = csig, yc[:, c % 2, :]
                    cg = raw[:, in_raw.index(i - 1) % 2, :]
                    dve.wait_ge(job_done, i + 1)
                    done(dve.tensor_tensor(three(z[:, :]), ps(i), three(cg), ALU.mult), raw_used)
                    dve.sem_inc(job_read[i % 2], 1)
                    step(dve.memset(z[:, NS:2 * NS], 0.0))
                    step(dve.tensor_copy(t.z_out[:, c, 0:NS], z[:, 0:NS]))
                    done(dve.tensor_copy(t.z_out[:, c, NS:NS + 2], z[:, PROJ_COLS - 2:]), z_ready)
                    if c >= 2:
                        dve.wait_ge(t.y_spilled[c % 2], 32 - 16 * (c % 2))
                    step(dve.tensor_scalar(y, z[:, :], param("cw2", c), None, ALU.mult))
                    for back, w in ((1, "cw1"), (2, "cw0")):
                        step(dve.scalar_tensor_tensor(out=y[:, C_META:], in0=z[:, C_META - back:PROJ_COLS - back], scalar=param(w, c),
                                                      in1=y[:, C_META:], op0=ALU.mult, op1=ALU.add))
                    old = t.conv_state[:, c, :].rearrange("p (b j) -> p j b", j=2)
                    for j, w in ((0, "cw0"), (1, "cw1")):
                        step(dve.scalar_tensor_tensor(out=y[:, 0:NS], in0=old[:, j, :], scalar=param(w, c),
                                                      in1=y[:, 0:NS], op0=ALU.mult, op1=ALU.add))
                elif kind == "bg":
                    y = yc[:, c % 2, :]
                    dve.wait_ge(job_done, i + 1)
                    step(dve.tensor_tensor(three(y), ps(i), three(y), ALU.mult))
                    dve.sem_inc(job_read[i % 2], 1)
                    dve.sem_inc(y_done, 1)

class Stages:

    def __init__(self, sem, names):
        self.sem, self.names = sem, names
        self.emitted = 0

    def start(self, eng):
        eng.sem_inc(self.sem, len(self.names))

    def done_by(self, ins, name):
        assert self.names[self.emitted % len(self.names)] == name, name
        self.emitted += 1
        ins.then_inc(self.sem, 1)

    def wait(self, eng, turn, *steps):
        steps = [(x, 0) if isinstance(x, str) else x for x in steps]
        eng.wait_ge(self.sem, turn * len(self.names) + max((1 - back) * len(self.names) + self.names.index(name) + 1
                                                         for name, back in steps))


def sample_phase(nc, t, d):
    ctx = ExitStack()
    with ctx:
        sb = lambda n, s: ctx.enter_context(nc.sbuf_tensor(n, s, F32))
        sem = lambda n: ctx.enter_context(nc.semaphore(n))
        BH = NS * HEADS
        rows_sb = sb("samp_rows_sb", [3 * NS * PAIRS, 2, P])
        vecs = sb("samp_vecs", [BH, 6, HD])
        state = sb("samp_state", [BH, HD, HD])
        term = sb("samp_term", [BH, HD, HD])
        sa, o_rows = sb("samp_sa", [BH, HD]), sb("samp_o_rows", [BH, 2, HD])
        z_rows = sb("z_rows", [NS + 2, CONVW])
        turned = [ctx.enter_context(nc.psum_tensor(f"samp_ps{i}", [P, 512], F32)) for i in range(3)]
        state_loaded, vecs_loaded, rows_stored, all_stored = sem("state_loaded"), sem("vecs_loaded"), sem("rows_stored"), sem("samp_stored")
        pe_done, act_done, chain, state_new, o_ready = sem("samp_pe"), sem("samp_act"), sem("samp_chain"), sem("state_new"), sem("o_ready")
        block = ctx.enter_context(nc.Block())
        R = 3 * NS * PAIRS

        @block.sync
        def _(sp):
            sp.dma_start(state[:, :, :], d["state_wkv"][0].rearrange("b h v k -> (b h) v k")).then_inc(state_loaded, 16)
            sp.dma_start(d["new_shift_prompt"][0], d["h_rows"][PROJ_COLS - 1:PROJ_COLS, :]).then_inc(all_stored, 16)
            sp.dma_start(d["new_shift_sample"][0], d["h_rows"][0:NS, :]).then_inc(all_stored, 16)
            sp.dma_start(d["new_conv_sample"][0, :, 0, :], d["state_conv"][0, :, 1, :]).then_inc(all_stored, 16)
            sp.wait_ge(act_done, 2)
            for j in range(6):
                sp.dma_start(d["samp_rows"].rearrange("(b c) h j k -> (b c) h j k", b=NS)[:, :, j, :],
                             rows_sb[(j % 3) * 32:(j % 3) * 32 + 32, j // 3, :].rearrange("p (h k) -> p h k", h=2)).then_inc(rows_stored, 16)
            sp.wait_ge(rows_stored, 96)
            sp.dma_start(vecs[:, :, :], d["samp_rows"].rearrange("a h j k -> (a h) j k")).then_inc(vecs_loaded, 16)
            sp.wait_ge(act_done, 3)
            sp.dma_start(d["new_conv_sample"][0, :, 1, :], z_rows[0:NS, :]).then_inc(all_stored, 16)
            sp.dma_start(d["new_conv_prompt"][0, 0], z_rows[NS:NS + 2, :]).then_inc(all_stored, 16)
            sp.wait_ge(state_new, 1)
            sp.dma_start(d["new_wkv_sample"][0].rearrange("b h v k -> (b h) v k"), state[:, :, :]).then_inc(all_stored, 16)
            sp.wait_ge(all_stored, 96)

        @block.tensor
        def _(pe):
            flat = t.samp[:, :, :, :].rearrange("p j b c -> p (j b c)")
            for half in range(2):
                pe.transpose(turned[half][0:R, 0:P], flat[:, half * R:(half + 1) * R], t.ident[:, :]).then_inc(pe_done, 1)
            for c in range(PAIRS):
                last = pe.transpose(turned[2][0:NS + 2, c * P:(c + 1) * P], t.z_out[:, c, :], t.ident[:, :])
            last.then_inc(pe_done, 1)
            pe.wait_ge(o_ready, 1)
            pe.wait_ge(act_done, 1)
            pe.matmul(turned[0][:, 0:BH], o_rows[:, :, :].rearrange("p a b -> p (a b)"), t.ident[0:BH, 0:BH],
                      start=True, stop=True).then_inc(pe_done, 1)

        @block.scalar
        def _(act):
            for half in range(2):
                act.wait_ge(pe_done, half + 1)
                act.activation(rows_sb[:, half, :], turned[half][0:R, 0:P], ACT.Copy).then_inc(act_done, 1)
            act.wait_ge(pe_done, 3)
            act.activation(z_rows[:, :], turned[2][0:NS + 2, :], ACT.Copy).then_inc(act_done, 1)
            act.wait_ge(pe_done, 4)
            for h in range(2):
                rows = slice(h * HD, (h + 1) * HD)
                src = turned[0][rows, 0:BH].rearrange("p (b c h) -> p h c b", b=NS, c=PAIRS)[:, h]
                act.activation(t.samp_o[rows, :, :], src, ACT.Copy).then_inc(act_done, 1)

        @block.vector
        def _(dve):
            done = signals(dve)
            step = lambda ins: done(ins, chain)
            full = [BH, HD, HD]
            along_k = lambda x: x.unsqueeze(1).broadcast_to(full)
            along_v = lambda x: x.unsqueeze(2).broadcast_to(full)
            dve.wait_ge(state_loaded, 16)
            dve.wait_ge(vecs_loaded, 16)
            r, k, v, kk, kka, w = (vecs[:, j, :] for j in range(6))
            step(dve.tensor_tensor(term[:, :, :], state[:, :, :], along_k(kk), ALU.mult))
            step(dve.tensor_reduce(sa[:, :], term[:, :, :], AX_X, ALU.add))
            step(dve.tensor_tensor(state[:, :, :], state[:, :, :], along_k(w), ALU.mult))
            step(dve.tensor_tensor(term[:, :, :], along_v(sa[:, :]), along_k(kka), ALU.mult))
            step(dve.tensor_tensor(state[:, :, :], state[:, :, :], term[:, :, :], ALU.subtract))
            step(dve.tensor_tensor(term[:, :, :], along_v(v), along_k(k), ALU.mult))
            done(dve.tensor_tensor(state[:, :, :], state[:, :, :], term[:, :, :], ALU.add), state_new)
            step(dve.tensor_tensor(term[:, :, :], state[:, :, :], along_k(r), ALU.mult))
            step(dve.tensor_reduce(o_rows[:, 0, :], term[:, :, :], AX_X, ALU.add))
            dve.tensor_copy(o_rows[:, 1, :], o_rows[:, 0, :]).then_inc(o_ready, 1)


def pick_experts(dve, step, rows, val, idx, k, best, expert):
    n = slice(0, rows)
    sq = [rows, TOPK, TOPK]
    step(dve.tensor_tensor(k.sums[n], val[n, 0, :].unsqueeze(2).broadcast_to(sq), val[n, 1, :].unsqueeze(1).broadcast_to(sq), ALU.add))
    flat, flat2 = k.sums[n].rearrange("p a b -> p (a b)"), k.sums2[n].rearrange("p a b -> p (a b)")
    step(dve.max(best[n, 0:8], flat))
    step(dve.max_index(k.place[n, 0:8], best[n, 0:8], flat))
    step(dve.match_replace(flat2, best[n, 0:8], flat, NEG))
    step(dve.max(best[n, 8:16], flat2))
    step(dve.max_index(k.place[n, 8:16], best[n, 8:16], flat2))
    step(dve.tensor_single_scalar(k.half[n, 0, :], k.place[n, :], 4, ALU.logical_shift_right))
    step(dve.tensor_single_scalar(k.half[n, 1, :], k.place[n, :], TOPK - 1, ALU.bitwise_and))
    for j in range(2):
        step(dve.tensor_tensor(k.sums[n], k.half[n, j, :].unsqueeze(2).broadcast_to(sq), k.iota[n, :].unsqueeze(1).broadcast_to(sq), ALU.is_equal))
        step(dve.tensor_tensor(k.sums[n], k.sums[n], idx[n, j, :].unsqueeze(1).broadcast_to(sq), ALU.mult))
        step(dve.tensor_reduce(k.number[n, j, :], k.sums[n], AX_X, ALU.add))
    return dve.scalar_tensor_tensor(out=expert[n, :], in0=k.number[n, 0, :], scalar=float(N_KEYS), in1=k.number[n, 1, :],
                                    op0=ALU.mult, op1=ALU.add)


def pick_tiles(nc, ctx, name):
    k = Tiles()
    k.sums = ctx.enter_context(nc.sbuf_tensor(name + "_sums", [P, TOPK, TOPK], F32))
    k.sums2 = ctx.enter_context(nc.sbuf_tensor(name + "_sums2", [P, TOPK, TOPK], F32))
    k.place = ctx.enter_context(nc.sbuf_tensor(name + "_place", [P, TOPK], U32))
    k.half = ctx.enter_context(nc.sbuf_tensor(name + "_half", [P, 2, TOPK], U32))
    k.number = ctx.enter_context(nc.sbuf_tensor(name + "_number", [P, 2, TOPK], F32))
    k.iota = ctx.enter_context(nc.sbuf_tensor(name + "_iota", [P, TOPK], F32))
    return k


def gather(pool, ring, table, index):
    return pool.indirect_dma_start(out=ring, out_offset=None, in_=table, in_offset=bass.IndirectOffsetOnAxis(ap=index, axis=0))


def sample_experts_phase(nc, t, d):
    ctx = ExitStack()
    with ctx:
        sb = lambda n, s, dt=F32: ctx.enter_context(nc.sbuf_tensor(n, s, dt))
        sem = lambda n: ctx.enter_context(nc.semaphore(n))
        k = pick_tiles(nc, ctx, "sp")
        PER = P // NS
        EACH = SLOTS // PER
        best, ex = sb("sp_best", [NS, PEER_HEADS, TOPK]), sb("sp_ex", [NS, PEER_HEADS, TOPK])
        expert = sb("sp_expert", [NS, PEER_HEADS, TOPK], U32)
        total = sb("sp_total", [NS, PEER_HEADS, 1])
        idx, gate = sb("sp_idx", [P, EACH], U32), sb("sp_gate", [P, EACH])
        x, u, v = sb("sp_x", [P, D]), sb("sp_u", [P, EACH, D]), sb("sp_v", [P, EACH, D])
        hu = sb("sp_hu", [P, EACH])
        acc, own, gb = sb("sp_acc", [P, D]), sb("sp_own", [NS, D]), sb("sp_gb", [NS, 2, D])
        select = sb("sp_select", [P, NS])
        stats, moments, rstd = sb("sp_stats", [NS, 12]), sb("sp_moments", [NS, 2]), sb("sp_rstd", [NS, 1])
        out_ps = ctx.enter_context(nc.psum_tensor("sp_ps", [NS, 2, 512], F32))
        consts, chain, diff_ready, exp_ready, picked, stored, reloaded, x_loaded = (
            sem("sp_consts"), sem("sp_chain"), sem("sp_diff"), sem("sp_exp"), sem("sp_picked"), sem("sp_stored"), sem("sp_reloaded"), sem("sp_x_loaded"))
        u_landed, v_landed, hu_ready, gelu_ready, acc_ready, summed, var_ready, std_ready, y_ready, y_stored = (
            t.sp_landed[0], t.sp_landed[1], sem("sp_hu_ready"), sem("sp_gelu"), sem("sp_acc_ready"), sem("sp_summed"),
            sem("sp_var"), sem("sp_std"), sem("sp_y"), sem("sp_y_stored"))
        block = ctx.enter_context(nc.Block())

        @block.sync
        def _(sp):
            for b in range(NS):
                sp.dma_start(x[b * PER:(b + 1) * PER, :], d["h1_rows"][b:b + 1, :].broadcast_to([PER, D])).then_inc(x_loaded, 16)
            sp.dma_start(own[:, :], d["h1_rows"][:, :]).then_inc(x_loaded, 16)
            for j, n in enumerate(("ln2_g", "ln2_b")):
                sp.dma_start(gb[:, j, :], d[n][0:1, :].broadcast_to([NS, D])).then_inc(x_loaded, 16)
            sp.wait_ge(picked, 2)
            sp.dma_start(d["sp_idx"], expert[:, :, :].rearrange("p a b -> p (a b)")).then_inc(stored, 16)
            sp.dma_start(d["sp_gate"], ex[:, :, :].rearrange("p a b -> p (a b)")).then_inc(stored, 16)
            sp.wait_ge(stored, 32)
            sp.dma_start(idx[:, :], d["sp_idx"].rearrange("b (s e) -> (b s) e", e=EACH)).then_inc(reloaded, 16)
            sp.dma_start(gate[:, :], d["sp_gate"].rearrange("b (s e) -> (b s) e", e=EACH)).then_inc(reloaded, 16)
            sp.wait_ge(y_ready, 1)
            sp.dma_start(d["y_sample"][:, 0, :], own[:, :]).then_inc(y_stored, 16)
            sp.wait_ge(y_stored, 16)

        @block.gpsimd
        def _(pool):
            done = signals(pool)
            done(pool.iota(k.iota[:, :], [[1, TOPK]], base=0, channel_multiplier=0, allow_small_or_imprecise_dtypes=True), consts)
            done(pool.memset(select[:, :], 1.0), consts)
            done(pool.affine_select(out=select[:, :], in_=select[:, :], compare_op=ALU.is_ge, fill=0.0, base=0,
                                    pattern=[[-PER, NS]], channel_multiplier=1), consts)
            done(pool.affine_select(out=select[:, :], in_=select[:, :], compare_op=ALU.is_gt, fill=0.0, base=PER,
                                    pattern=[[PER, NS]], channel_multiplier=-1), consts)
            pool.wait_ge(reloaded, 32)
            for e in range(EACH):
                gather(pool, u[:, e, :], d["peer_u"][0], idx[:, e:e + 1]).then_inc(u_landed, 16)
            for e in range(EACH):
                gather(pool, v[:, e, :], d["peer_v"][0], idx[:, e:e + 1]).then_inc(v_landed, 16)

        @block.tensor
        def _(pe):
            pe.wait_ge(consts, 4)
            pe.wait_ge(acc_ready, 1)
            for half in range(2):
                last = pe.matmul(out_ps[:, half, :], select[:, :], acc[:, half * 512:(half + 1) * 512], start=True, stop=True)
            last.then_inc(summed, 1)

        @block.scalar
        def _(act):
            act.wait_ge(diff_ready, 1)
            act.activation(ex[:, :, :], ex[:, :, :], ACT.Exp).then_inc(exp_ready, 1)
            act.wait_ge(hu_ready, 1)
            act.activation(hu[:, :], hu[:, :], ACT.Gelu).then_inc(gelu_ready, 1)
            act.wait_ge(var_ready, 1)
            act.activation(rstd[:, :], rstd[:, :], ACT.Sqrt).then_inc(std_ready, 1)

        @block.vector
        def _(dve):
            done = signals(dve)
            step = lambda ins: done(ins, chain)
            dve.wait_ge(consts, 1)
            for h in range(PEER_HEADS):
                step(pick_experts(dve, step, NS, t.top_val[:, h], t.top_idx[:, h], k, best[:, h, :], expert[:, h, :]))
            shape = [NS, PEER_HEADS, TOPK]
            done(dve.tensor_tensor(ex[:, :, :], best[:, :, :], best[:, :, 0:1].broadcast_to(shape), ALU.subtract), diff_ready)
            dve.sem_inc(picked, 1)
            dve.wait_ge(exp_ready, 1)
            step(dve.tensor_reduce(total[:, :, :], ex[:, :, :], AX_X, ALU.add))
            step(dve.reciprocal(total[:, :, :], total[:, :, :]))
            done(dve.tensor_tensor(ex[:, :, :], ex[:, :, :], total[:, :, :].broadcast_to(shape), ALU.mult), picked)
            dve.wait_ge(x_loaded, 16 * (NS + 3))
            dve.wait_ge(u_landed, 16 * EACH)
            for e in range(EACH):
                step(dve.tensor_tensor_reduce(u[:, e, :], u[:, e, :], x[:, :], 1.0, 0.0, ALU.mult, ALU.add, hu[:, e:e + 1]))
            dve.sem_inc(hu_ready, 1)
            dve.wait_ge(gelu_ready, 1)
            step(dve.tensor_tensor(hu[:, :], hu[:, :], gate[:, :], ALU.mult))
            dve.wait_ge(v_landed, 16 * EACH)
            step(dve.tensor_scalar(acc[:, :], v[:, 0, :], hu[:, 0:1], None, ALU.mult))
            for e in range(1, EACH):
                step(dve.scalar_tensor_tensor(out=acc[:, :], in0=v[:, e, :], scalar=hu[:, e:e + 1], in1=acc[:, :], op0=ALU.mult, op1=ALU.add))
            dve.sem_inc(acc_ready, 1)
            dve.wait_ge(summed, 1)
            y = own[:, :]
            step(dve.scalar_tensor_tensor(out=y, in0=y, scalar=ALPHA, in1=out_ps[:, :, :].rearrange("p a b -> p (a b)"),
                                          op0=ALU.mult, op1=ALU.add))
            step(dve.bn_stats(stats[:, 0:6], y[:, 0:512]))
            step(dve.bn_stats(stats[:, 6:12], y[:, 512:1024]))
            step(dve.bn_aggr(moments[:, :], stats[:, :]))
            done(dve.tensor_scalar(rstd[:, :], moments[:, 1:2], LN_EPS, None, ALU.add), var_ready)
            dve.wait_ge(std_ready, 1)
            step(dve.reciprocal(rstd[:, :], rstd[:, :]))
            step(dve.tensor_scalar(y, y, moments[:, 0:1], rstd[:, :], ALU.subtract, ALU.mult))
            step(dve.tensor_tensor(y, y, gb[:, 0, :], ALU.mult))
            done(dve.tensor_tensor(y, y, gb[:, 1, :], ALU.add), y_ready)


class Stages:

    def __init__(self, sem, names):
        self.sem, self.names = sem, names
        self.emitted = 0

    def start(self, eng):
        eng.sem_inc(self.sem, len(self.names))

    def at(self, name):
        assert self.names[self.emitted % len(self.names)] == name, name
        self.emitted += 1
        return self.sem

    def value(self, turn, *steps):
        steps = [(x, 0) if isinstance(x, str) else x for x in steps]
        return turn * len(self.names) + max((1 - back) * len(self.names) + self.names.index(name) + 1 for name, back in steps)


def steady_phase(nc, t, d):
    ctx = ExitStack()
    with ctx:
        sb = lambda n, s, dt=F32: ctx.enter_context(nc.sbuf_tensor(n, s, dt))
        sem = lambda n: ctx.enter_context(nc.semaphore(n))
        H = PEER_HEADS
        RING = 8
        N_CONSTS = 25
        NW = 4
        ALL = RW
        k = pick_tiles(nc, ctx, "ep")
        u, v = sb("u_ring", [P, RING, D]), sb("v_ring", [P, RING, D])
        diag = sb("diag", [P, RING, P])
        idx = sb("idx", [P, 4, TOPK], U32)
        best, neg_max = sb("head_best", [P, 2, TOPK]), sb("neg_max", [P, 2, 1])
        ex, total = sb("head_ex", [P, 2, TOPK]), sb("head_total", [P, 2, 1])
        hu, act_v = sb("hu", [P, 2, TOPK]), sb("act_v", [P, 2, TOPK])
        x, res, y = sb("x_rows", [P, D]), sb("res", [P, D]), sb("y_rows", [P, D])
        ln2_gb, ln1_gb = sb("ln2_gb", [P, 2, D]), sb("ln1_gb", [P, 2, D])
        stats, moments, rstd = sb("ep_stats", [P, 12]), sb("ep_moments", [P, 2]), sb("ep_rstd", [P, 1])
        ops = sb("ops", [P, 5, PAIRS, P])
        al2, be2, ka2, rh2, vt2 = (ops[:, j] for j in range(5))
        o = sb("wkv_o", [P, PAIRS, P])
        yc, lora = sb("yc_block", [P, PAIRS, P]), sb("lora_block", [G_LORA, P])
        tile = lambda n: sb(n, [P, PAIRS, CHUNK])
        ud, ue, nd, r_, q_ = (tile(n) for n in ("ud", "ue", "nd", "r_", "q_"))
        shared = sb("front_shared", [P, 6, PAIRS, CHUNK])
        g_ka, g_br, g_kr, be_t, ka_t, v_t = (shared[:, i] for i in range(6))
        rk, square, gn_std = (shared[:, 2 * i:2 * i + 2].rearrange("p a c n -> p (a c n)").rearrange("p (c n) -> p c n", c=PAIRS) for i in range(3))
        u2, n2, u4, n4, u8, n8 = (tile(n) for n in ("u2", "n2", "u4", "n4", "u8", "n8"))
        mt, m_, m2, xx, sa = u2, n2, u4, n4, u8
        st, st_new, s_out = tile("st"), ud, ue
        eye, upper, upper_eq = sb("eye", [P, CHUNK]), sb("upper", [P, CHUNK]), sb("upper_eq", [P, CHUNK])
        upper_in, upper_out, lower_in = sb("upper_in", [P, CHUNK]), sb("upper_out", [P, CHUNK]), sb("lower_in", [P, CHUNK])
        g_up, w_o = sb("g_up", [G_LORA, RW]), sb("w_o", [P, KT, D])
        h, h1T = sb("h_block", [P, D]), sb("h1T", [P, KT, P])
        st1, mo1, rs1 = sb("ln1_stats", [P, 12]), sb("ln1_moments", [P, 2]), sb("ln1_rstd", [P, 1])
        w_q, q = sb("wq_ring", [P, NW, KT, P]), sb("q_T", [P, 2, P])
        others = sb("others", [P, N_KEYS])
        places = sb("top_places", [P, TOPK], U32)
        out_ps = ctx.enter_context(nc.psum_tensor("ep_ps", [P, 2, 512], F32))
        bank = [ctx.enter_context(nc.psum_tensor(f"front_ps{i}", [P, 512], F32)) for i in range(4)]
        wide_ps = ctx.enter_context(nc.psum_tensor("front_wide", [P, 2, 512], F32))

        u_landed = [sem(f"u_landed{s}") for s in range(RING)]
        v_landed = [sem(f"v_landed{s}") for s in range(RING)]
        wq_loaded = [sem(f"wq_loaded{s}") for s in range(NW)]
        consts, const_loaded, ops_loaded, h_loaded = sem("st_consts"), sem("st_const_loaded"), sem("ops_loaded"), sem("h_loaded")
        x_taken, turn_chain, block_chain, start_chain = sem("x_taken"), sem("turn_chain"), sem("block_chain"), sem("start_chain")
        picked, dots, gelu_ready, act_ready, diag_ready, v_used = (
            sem("picked"), sem("dots"), sem("gelu_ready"), sem("act_ready"), sem("diag_ready"), sem("v_used"))
        exp_ready, sum_read, var_ready, std_ready, y_ready, y_stored, y_free = (
            sem("exp_ready"), sem("sum_read"), sem("ep_var"), sem("ep_std"), sem("ep_y"), sem("ep_y_stored"), sem("y_free"))
        waited_pool, waited_dve, waited_pe, waited_sp = (sem(f"waited_{e}") for e in ("pool", "dve", "pe", "sp"))
        state_turned, state_out, state_stored, h1_stored = sem("state_turned"), sem("state_out"), sem("state_stored"), sem("h1_stored")
        sample_ready = sem("sample_ready")

        HALVES = [["U", "N", "BT", "U2", "N2", "KA", "R1", "U4", "Q1", "N4", "KT", "R2", "U8", "Q2", "N8"],
                  ["VT", "R3", "Q3", "BR", "MT", "M", "KR", "M2", "Z1", "X", "Z", "SA", "S", "O"]]
        PRODUCTS = HALVES[0] + HALVES[1]
        products = Stages(sem("wkv_products"), PRODUCTS)
        copies = Stages(sem("wkv_copies"), ["be_t", "u2", "n2", "u4", "n4", "ka_t", "u8", "n8", "v_t", "mt", "m", "m2", "xx", "sa", "o"])
        vectors = Stages(sem("wkv_vectors"), ["ud", "r", "nd", "q", "ue", "g_ka", "r1", "q1", "r2", "q2", "r3", "q3", "g_br", "g_kr",
                                              "z1", "z", "s_sum", "s"])
        reader = {"U": (vectors, "ue"), "N": (vectors, "nd"), "BT": (copies, "be_t"), "U2": (copies, "u2"), "N2": (copies, "n2"),
                  "KA": (vectors, "g_ka"), "R1": (vectors, "r1"), "U4": (copies, "u4"), "Q1": (vectors, "q1"), "N4": (copies, "n4"),
                  "KT": (copies, "ka_t"), "R2": (vectors, "r2"), "U8": (copies, "u8"), "Q2": (vectors, "q2"), "N8": (copies, "n8"),
                  "VT": (copies, "v_t"), "R3": (vectors, "r3"), "Q3": (vectors, "q3"), "BR": (vectors, "g_br"), "MT": (copies, "mt"),
                  "M": (copies, "m"), "KR": (vectors, "g_kr"), "M2": (copies, "m2"), "Z1": (vectors, "z1"), "Z": (vectors, "z"),
                  "X": (copies, "xx"), "SA": (copies, "sa"), "S": (vectors, "s_sum"), "O": (copies, "o")}
        front_pe = Stages(sem("front_pe"), ["mean", "bonus", "gate", "var", "mix", "turned"]
                          + [n for j in range(HP) for n in (f"q{j}", f"s{j}")])
        front_act = Stages(sem("front_act"), ["square", "gn_std", "ln_std", "h1T"] + [f"q{j}" for j in range(HP)])
        front_dve = Stages(sem("front_dve"), ["rk0", "rk", "centred", "bonus", "var", "inv", "scaled", "gain", "offset", "plus", "y",
                                              "sum", "bn0", "bn1", "aggr", "ln_var", "ln_inv", "ln_x", "ln_g", "h1"]
                           + [f"{n}{j}" for j in range(HP) for n in ("max", "place", "others", "max2_", "place2_", "top")])

        def ps(name):
            i = PRODUCTS.index(name) % 6
            return (bank[i] if i < 4 else wide_ps[:, i - 4])[:, 0:PAIRS * CHUNK].rearrange("p (c n) -> p c n", c=PAIRS)

        def flat(x):
            return x.rearrange("p a b -> p (a b)")

        def score_ps(j):
            return (wide_ps[:, 0], wide_ps[:, 1], bank[0], bank[1])[j % 4]

        SCORE_SLOTS = [1 + (2 * TOPK - 4) * j // (HP - 1) for j in range(HP)]
        assert SCORE_SLOTS[-1] + 1 < 2 * TOPK

        def queries(n, s, back=0):
            return [j for j in range(HP) if SCORE_SLOTS[j] == (n - 6) * TOPK + s - back]

        def over_turns(eng, a_turn, finish):
            a_turn(0, 0, None, sums=False)
            with eng.Fori(0, TBLOCKS - 1) as b:
                for n in range(1, H):
                    a_turn(b * H + n, n, b + 1)
                a_turn(b * H + H, 0, None, new_block=b + 1)
                finish(b)
            for n in range(1, H):
                a_turn((TBLOCKS - 1) * H + n, n, TBLOCKS)
            a_turn(TBLOCKS * H, 0, None, dots_left=False)
            finish(TBLOCKS - 1)

        def front(slot, nb):
            for n in range(1, H):
                for s in range(TOPK):
                    slot(nb, n, s)

        def chunk_slot(nb, n, s):
            names = HALVES[(n - 1) % 2]
            return nb * 2 + 1 + (n - 1) // 2, names[s] if s < len(names) else None, (n - 1) // 2 * CHUNK

        block = ctx.enter_context(nc.Block())

        @block.sync
        def _(sp):
            def load_ops(c0, dst, n, p0):
                for j in range(5):
                    sp.dma_start(ops[:, j, :, dst:dst + n], d["operands"][j][:, :, bass.ds(c0, n)]).then_inc(ops_loaded, 16)
                sp.dma_start(yc[:, :, 0:n], d["y_conv"][:, :, bass.ds(p0, n)]).then_inc(ops_loaded, 16)
                sp.dma_start(lora[:, 0:n], d["lora_g"][:, bass.ds(p0, n)]).then_inc(ops_loaded, 16)

            def load_block(nb):
                load_ops(nb * P + 2 * WKV_OFF, 0, P, nb * P + C_PROMPT)

            def load_wq(nb):
                for j in range(HP):
                    sp.wait_ge(front_pe.sem, front_pe.value(nb, f"q{j - NW}" if j >= NW else (f"q{j + HP - NW}", 1)))
                    sp.sem_inc(waited_sp, 1)
                    sp.dma_start(w_q[:, j % NW, :, :], d["w_q"][0, :, j * P:(j + 1) * P].rearrange("(k p) c -> p k c", p=P)).then_inc(wq_loaded[j % NW], 16)

            def load_h(nb):
                sp.dma_start(h[:, :], d["h_rows"][bass.ds(nb * P + C_PROMPT, P), :]).then_inc(h_loaded, 16)

            load_ops(0, CHUNK, CHUNK, 0)
            load_h(0)
            for kt in range(KT):
                sp.dma_start(w_o[:, kt, :], d["w_o"][0, kt * P:(kt + 1) * P, :]).then_inc(const_loaded, 16)
            sp.dma_start(g_up[:, :], d["g_up"][0]).then_inc(const_loaded, 16)
            for j, n in enumerate(("ln1_g", "ln1_b")):
                sp.dma_start(ln1_gb[:, j, :], d[n][0:1, :].broadcast_to([P, D])).then_inc(const_loaded, 16)
            for j, n in enumerate(("ln2_g", "ln2_b")):
                sp.dma_start(ln2_gb[:, j, :], d[n][0:1, :].broadcast_to([P, D])).then_inc(const_loaded, 16)
            sp.wait_ge(products.sem, products.value(0, "O"))
            sp.wait_ge(ops_loaded, 112)
            load_block(0)
            load_wq(0)

            def after_norm(nb):
                sp.wait_ge(front_dve.sem, front_dve.value(nb, "y"))
                sp.sem_inc(waited_sp, 1)
                sp.wait_ge(front_pe.sem, front_pe.value(nb, "mix"))
                sp.sem_inc(waited_sp, 1)

            def store_y(b):
                sp.wait_ge(y_ready, b + 1)
                sp.sem_inc(waited_sp, 1)
                sp.dma_start(d["y_prompt"][0, bass.ds(b * P, P), :], y[:, :]).then_inc(y_stored, 16)
                sp.wait_ge(y_stored, b * 16 + 16)
                sp.sem_inc(waited_sp, 1)
                sp.sem_inc(y_free, 1)

            after_norm(0)
            load_block(1)
            sp.wait_ge(x_taken, 1)
            load_h(1)
            with sp.Fori(0, TBLOCKS - 2) as b:
                load_wq(b + 1)
                after_norm(b + 1)
                load_block(b + 2)
                sp.wait_ge(x_taken, b + 2)
                sp.sem_inc(waited_sp, 1)
                load_h(b + 2)
                store_y(b)
            load_wq(TBLOCKS - 1)
            after_norm(TBLOCKS - 1)
            sp.dma_start(yc[:, :, 0:NS], d["y_conv"][:, :, 0:NS]).then_inc(ops_loaded, 16)
            sp.dma_start(lora[:, 0:NS], d["lora_g"][:, 0:NS]).then_inc(ops_loaded, 16)
            sp.wait_ge(x_taken, TBLOCKS)
            sp.dma_start(h[0:NS, :], d["h_rows"][0:NS, :]).then_inc(h_loaded, 16)
            store_y(TBLOCKS - 2)
            load_wq(TBLOCKS)
            sp.wait_ge(state_out, 1)
            for c in range(PAIRS):
                sp.dma_start(d["new_wkv_prompt"][0, 0, 2 * c:2 * c + 2].rearrange("h v k -> (h v) k"), s_out[:, c, :]).then_inc(state_stored, 16)
            sp.wait_ge(front_dve.sem, front_dve.value(TBLOCKS, "h1"))
            sp.dma_start(d["h1_rows"], h[0:NS, :]).then_inc(h1_stored, 16)
            store_y(TBLOCKS - 1)
            sp.wait_ge(state_stored, 16 * PAIRS)
            sp.wait_ge(h1_stored, 16)

        @block.gpsimd
        def _(pool):
            done = signals(pool)
            n_consts = [0]

            def const(ins):
                n_consts[0] += 1
                done(ins, consts)

            def select(m, op, base, pattern, fill, row=1):
                for head in range(2):
                    const(pool.affine_select(out=m[head * HD:(head + 1) * HD], in_=m[head * HD:(head + 1) * HD], compare_op=op,
                                             fill=fill, base=base, pattern=pattern, channel_multiplier=row))

            const(pool.memset(eye[:, :], 0.0))
            select(eye[:, :], ALU.not_equal, 0, [[-1, CHUNK]], 1.0)
            for m in (upper, upper_eq, upper_in, lower_in):
                const(pool.memset(m[:, :], 1.0))
            select(upper[:, :], ALU.is_gt, 0, [[1, CHUNK]], 0.0, -1)
            select(upper_eq[:, :], ALU.is_ge, 0, [[1, CHUNK]], 0.0, -1)
            for m in (upper_in, lower_in):
                select(m[:, :].rearrange("p (a b) -> p a b", b=16), ALU.is_ge, 0, [[-16, 4], [0, 16]], 0.0)
                select(m[:, :].rearrange("p (a b) -> p a b", b=16), ALU.is_gt, 16, [[16, 4], [0, 16]], 0.0, -1)
            select(lower_in[:, :], ALU.is_gt, 0, [[-1, CHUNK]], 0.0)
            select(upper_in[:, :], ALU.is_gt, 0, [[1, CHUNK]], 0.0, -1)
            const(pool.tensor_tensor(upper_out[:, :], upper[:, :], upper_in[:, :], ALU.subtract))
            const(pool.iota(k.iota[:, :], [[1, TOPK]], base=0, channel_multiplier=0, allow_small_or_imprecise_dtypes=True))
            assert n_consts[0] == N_CONSTS, n_consts

            pool.wait_ge(picked, 1)
            for s in range(RING):
                gather(pool, u[:, s, :], d["peer_u"][0], idx[:, 0, s:s + 1]).then_inc(u_landed[s], 16)

            def a_turn(turn, n, nb, sums=True, dots_left=True, new_block=None):
                last = n == H - 1 and isinstance(turn, int)
                for s in range(TOPK):
                    own = s + RING < TOPK
                    row = (s + RING) % TOPK
                    if dots_left and (own or not last):
                        if row == 0:
                            pool.wait_ge(picked, turn + 2)
                        pool.wait_ge(dots, turn * TOPK + s + 1)
                        pool.sem_inc(waited_pool, 1)
                        gather(pool, u[:, s % RING, :], d["peer_u"][0],
                               idx[:, (n if own else n + 1) % 4, row:row + 1]).then_inc(u_landed[s % RING], 16)
                    if (sums if own else dots_left):
                        pool.wait_ge(v_used, turn * TOPK + s - RING + 1)
                        pool.sem_inc(waited_pool, 1)
                        gather(pool, v[:, s % RING, :], d["peer_v"][0],
                               idx[:, (n - 1 if own else n) % 4, row:row + 1]).then_inc(v_landed[s % RING], 16)
            over_turns(pool, a_turn, lambda b: None)

        @block.tensor
        def _(pe):
            def chunk_step(ci, name, dst):
                al, be, ka, rh, vt = (x[:, :, dst:dst + CHUNK] for x in (al2, be2, ka2, rh2, vt2))

                def product(name, pairs, V=(), A=()):
                    i = PRODUCTS.index(name)
                    stages, step = reader[PRODUCTS[i - 6] if i >= 6 else PRODUCTS[i + 6 * ((len(PRODUCTS) - 1 - i) // 6)]]
                    bank_read = (step, 0 if i >= 6 else 1)
                    V = list(V) + ([bank_read] if stages is vectors else [])
                    A = list(A) + ([bank_read] if stages is copies else [])
                    if V:
                        pe.wait_ge(vectors.sem, vectors.value(ci, *V))
                    if A:
                        pe.wait_ge(copies.sem, copies.value(ci, *A))
                    pe.sem_inc(waited_pe, 1)
                    for c in range(PAIRS):
                        for head in range(2):
                            rows = slice(head * HD, (head + 1) * HD)
                            for n, (a, b) in enumerate(pairs):
                                last = pe.matmul(ps(name)[rows, c, :], a[rows, c, :], b[rows, :] if b is eye else b[rows, c, :],
                                                 start=(n == 0), stop=(n == len(pairs) - 1))
                    last.then_inc(products.at(name), 1)

                operands, V, A = {
                    "U": ([(be, al)], [], []), "N": ([(al, be)], [], []), "BT": ([(be, eye)], [], []),
                    "U2": ([(nd, ud)], ["nd"], []), "N2": ([(ud, nd)], [], []), "KA": ([(ka, al)], [], []),
                    "R1": ([(n2, r_)], ["q"], ["n2"]), "U4": ([(n2, u2)], [], []), "Q1": ([(u2, q_)], [], []),
                    "N4": ([(u2, n2)], [], []), "KT": ([(ka, eye)], [], []), "R2": ([(n4, r_)], ["r1"], ["n4"]),
                    "U8": ([(n4, u4)], [], []), "Q2": ([(u4, q_)], ["q1"], []), "N8": ([(u4, n4)], [], []),
                    "VT": ([(vt, eye)], [], []), "R3": ([(n8, r_)], ["r2"], ["n8"]), "Q3": ([(u8, q_)], ["q2"], []),
                    "BR": ([(be, rh)], [], []), "MT": ([(q_, ue)], ["q3"], []), "M": ([(ue, q_)], [], []),
                    "KR": ([(ka, rh)], [], []), "M2": ([(mt, m_)], [], ["m"]), "Z1": ([(m_, r_)], [], []),
                    "X": ([(al, st), (g_ka, v_t)], [("s", 1)], []), "Z": ([(m2, r_)], ["z1"], ["m2"]),
                    "SA": ([(r_, xx)], ["z"], ["xx"]), "S": ([(be_t, sa), (ka_t, v_t)], [], ["sa"]),
                    "O": ([(st, rh), (sa, g_br), (v_t, g_kr)], [], [])}[name]
                product(name, operands, V, A)

            def norm_slot(nb, s, rows):
                if s == 0:
                    if rows == P:
                        pe.wait_ge(copies.sem, copies.value(nb * 2 + 2, "o"))
                        pe.wait_ge(vectors.sem, vectors.value(nb * 2 + 2, "s"))
                    pe.wait_ge(front_dve.sem, front_dve.value(nb, "rk"))
                    pe.sem_inc(waited_pe, 1)
                    pe.matmul(bank[0][:, :], t.head_ones[:, :], flat(o), start=True, stop=True).then_inc(front_pe.at("mean"), 1)
                elif s == 1:
                    pe.matmul(bank[1][:, :], t.head_ones[:, :], flat(rk), start=True, stop=True).then_inc(front_pe.at("bonus"), 1)
                elif s == 2:
                    for c in range(PAIRS):
                        last = pe.matmul(bank[2][:, c * P:(c + 1) * P], g_up[:, c * P:(c + 1) * P], lora[:, :], start=True, stop=True)
                    last.then_inc(front_pe.at("gate"), 1)
                elif s == 3:
                    pe.wait_ge(front_act.sem, front_act.value(nb, "square"))
                    pe.sem_inc(waited_pe, 1)
                    pe.matmul(bank[3][:, :], t.head_ones[:, :], flat(square), start=True, stop=True).then_inc(front_pe.at("var"), 1)
                elif s - 4 < KT:
                    kt = s - 4
                    if kt == PAIRS:
                        pe.wait_ge(front_dve.sem, front_dve.value(nb, "y"))
                        pe.sem_inc(waited_pe, 1)
                    y_in = yc[:, kt, :] if kt < PAIRS else o[:, kt - PAIRS, :]
                    for half in range(2):
                        last = pe.matmul(wide_ps[0:rows, half, :], y_in[:, 0:rows], w_o[:, kt, half * 512:(half + 1) * 512],
                                         start=(kt == 0), stop=(kt == KT - 1))
                    if kt == KT - 1:
                        last.then_inc(front_pe.at("mix"), 1)

            def turn_h1(nb, rows):
                pe.wait_ge(front_dve.sem, front_dve.value(nb, "h1"))
                pe.sem_inc(waited_pe, 1)
                for kt in range(KT):
                    last = pe.transpose(bank[kt // 4][:, (kt % 4) * P:(kt % 4) * P + rows], h[0:rows, kt * P:(kt + 1) * P],
                                        t.ident[0:rows, 0:rows])
                last.then_inc(front_pe.at("turned"), 1)

            def query(nb, j, rows):
                pe.wait_ge(wq_loaded[j % NW], (nb * (HP // NW) + j // NW + 1) * 16)
                pe.wait_ge(front_act.sem, front_act.value(nb, f"q{j - 2}" if j >= 2 else "h1T"))
                pe.sem_inc(waited_pe, 1)
                for kt in range(KT):
                    last = pe.matmul(bank[2 + j % 2][:, 0:rows], w_q[:, j % NW, kt, :], h1T[:, kt, 0:rows],
                                     start=(kt == 0), stop=(kt == KT - 1))
                last.then_inc(front_pe.at(f"q{j}"), 1)

            def key_scores(nb, j, rows):
                pe.wait_ge(front_act.sem, front_act.value(nb, f"q{j}"))
                if j >= 4:
                    pe.wait_ge(front_dve.sem, front_dve.value(nb, f"others{j - 4}"))
                pe.sem_inc(waited_pe, 1)
                pe.matmul(score_ps(j)[0:rows, 0:N_KEYS], q[:, j % 2, 0:rows], t.keysT[:, j, :],
                          start=True, stop=True).then_inc(front_pe.at(f"s{j}"), 1)

            def front_slot(nb, n, s):
                rows = NS if isinstance(nb, int) and nb == TBLOCKS else P
                if n <= 4 and rows == P:
                    if n == 1 and s == 0:
                        pe.wait_ge(ops_loaded, (nb + 2) * 112)
                        pe.wait_ge(front_dve.sem, front_dve.value(nb, (f"top{HP - 1}", 1)))
                        pe.sem_inc(waited_pe, 1)
                    ci, name, dst = chunk_slot(nb, n, s)
                    if name:
                        chunk_step(ci, name, dst)
                elif (n, s) == (1, 0):
                    pe.wait_ge(front_dve.sem, front_dve.value(nb, (f"top{HP - 1}", 1)))
                    for c in range(PAIRS):
                        for head in range(2):
                            r = slice(head * HD, (head + 1) * HD)
                            last = pe.matmul(bank[0][r, c * HD:(c + 1) * HD], st[r, c, :], eye[r, :], start=True, stop=True)
                    last.then_inc(state_turned, 1)
                elif n == 5:
                    if rows == NS and s == 0:
                        pe.wait_ge(ops_loaded, (TBLOCKS + 1) * 112 + 32)
                        pe.wait_ge(state_out, 1)
                    norm_slot(nb, s, rows)
                elif n >= 6:
                    if (n, s) == (6, 0):
                        turn_h1(nb, rows)
                    for j in queries(n, s, 1):
                        key_scores(nb, j, rows)
                    for j in queries(n, s):
                        query(nb, j, rows)

            def a_turn(turn, n, nb, sums=True, dots_left=True, new_block=None):
                head = (n - 1) % H
                for s in range(TOPK):
                    if sums:
                        if n == 1 and s == 0:
                            pe.wait_ge(sum_read, nb)
                        pe.wait_ge(v_landed[s % RING], (turn * 2 + s // RING - 1) * 16)
                        pe.wait_ge(diag_ready, (turn - 1) * TOPK + s + 1)
                        for half in range(2):
                            mm = pe.matmul(out_ps[:, half, :], diag[:, s % RING, :], v[:, s % RING, half * 512:(half + 1) * 512],
                                           start=head == 0 and s == 0, stop=head == H - 1 and s == TOPK - 1)
                        mm.then_inc(v_used, 1)
                    if nb is not None:
                        front_slot(nb, n, s)

            front_pe.start(pe)
            products.start(pe)
            pe.sem_inc(v_used, RING)
            pe.sem_inc(sum_read, 1)
            pe.wait_ge(consts, N_CONSTS)
            pe.wait_ge(const_loaded, 16 * (KT + 5))
            pe.wait_ge(ops_loaded, 112)
            for name in PRODUCTS:
                chunk_step(0, name, CHUNK)
            front(front_slot, 0)
            over_turns(pe, a_turn, lambda b: None)

        @block.scalar
        def _(act):
            def chunk_step(ci, name, dst):
                copied = {"BT": be_t, "U2": u2, "N2": n2, "U4": u4, "N4": n4, "KT": ka_t, "U8": u8, "N8": n8, "VT": v_t, "MT": mt,
                          "M": m_, "M2": m2, "X": xx, "SA": sa, "O": o[:, :, dst:dst + CHUNK]}
                if name in copied:
                    act.wait_ge(products.sem, products.value(ci, name))
                    act.activation(copied[name][:, :, :], ps(name), ACT.Copy).then_inc(copies.at(reader[name][1]), 1)

            def front_slot(nb, n, s):
                rows = NS if isinstance(nb, int) and nb == TBLOCKS else P
                if n <= 4 and rows == P:
                    chunk_step(*chunk_slot(nb, n, s))
                elif (n, s) == (1, 0):
                    act.wait_ge(state_turned, 1)
                    act.activation(flat(s_out), bank[0][:, 0:PAIRS * HD], ACT.Copy).then_inc(state_out, 1)
                elif (n, s) == (5, 2):
                    act.wait_ge(front_dve.sem, front_dve.value(nb, "centred"))
                    act.activation(flat(square), flat(o), ACT.Square).then_inc(front_act.at("square"), 1)
                elif (n, s) == (5, 4):
                    act.wait_ge(front_dve.sem, front_dve.value(nb, "var"))
                    act.activation(flat(gn_std), flat(gn_std), ACT.Sqrt).then_inc(front_act.at("gn_std"), 1)
                elif (n, s) == (5, 14):
                    act.wait_ge(front_dve.sem, front_dve.value(nb, "ln_var"))
                    act.activation(rs1[0:rows, :], rs1[0:rows, :], ACT.Sqrt).then_inc(front_act.at("ln_std"), 1)
                elif (n, s) == (6, 0):
                    act.wait_ge(front_pe.sem, front_pe.value(nb, "turned"))
                    for half in range(2):
                        ins = act.activation(h1T[:, 4 * half:4 * half + 4, 0:rows],
                                             bank[half][:, :].rearrange("p (k n) -> p k n", k=4)[:, :, 0:rows], ACT.Copy)
                    ins.then_inc(front_act.at("h1T"), 1)
                elif n >= 6:
                    for j in queries(n, s):
                        act.wait_ge(front_pe.sem, front_pe.value(nb, f"q{j}"))
                        act.activation(q[:, j % 2, 0:rows], bank[2 + j % 2][:, 0:rows], ACT.Copy).then_inc(front_act.at(f"q{j}"), 1)

            def exp_of(turn, par):
                act.wait_ge(picked, turn + 1)
                act.activation(ex[:, par, :], best[:, par, :], ACT.Exp, bias=neg_max[:, par, :], accum_out=total[:, par, :]).then_inc(exp_ready, 1)

            def a_turn(turn, n, nb, sums=True, dots_left=True, new_block=None):
                par = n % 2
                last = n == H - 1 and isinstance(turn, int)
                for s in range(TOPK):
                    if sums:
                        if s == 0:
                            act.wait_ge(act_ready, turn)
                        act.wait_ge(v_used, (turn - 1) * TOPK + s + 1)
                        act.activation(diag[:, s % RING, :], t.ident[:, :], ACT.Copy, scale=act_v[:, 1 - par, s:s + 1]).then_inc(diag_ready, 1)
                    if s == 4 and dots_left and not last:
                        exp_of(turn + 1, 1 - par)
                    if nb is not None:
                        front_slot(nb, n, s)
                if dots_left:
                    act.wait_ge(dots, (turn + 1) * TOPK)
                    act.activation(act_v[:, par, :], hu[:, par, :], ACT.Gelu).then_inc(gelu_ready, 1)

            def finish(b):
                act.wait_ge(var_ready, b + 1)
                act.activation(rstd[:, :], rstd[:, :], ACT.Sqrt).then_inc(std_ready, 1)

            copies.start(act)
            front_act.start(act)
            for name in PRODUCTS:
                chunk_step(0, name, CHUNK)
            front(front_slot, 0)
            exp_of(0, 0)
            over_turns(act, a_turn, finish)

        @block.vector
        def _(dve):
            done = signals(dve)
            TURN_STEPS = 17
            BLOCK_STEPS = 8

            def wide(mask):
                return mask[:, :].unsqueeze(1).broadcast_to([P, PAIRS, CHUNK])

            def chunk_step(ci, name, dst):
                def masked(step, out, mask):
                    dve.wait_ge(products.sem, products.value(ci, name))
                    dve.tensor_tensor(out[:, :, :], ps(name), wide(mask), ALU.mult).then_inc(vectors.at(step), 1)

                def plus_eye(step, out, x, x_step):
                    dve.wait_ge(vectors.sem, vectors.value(ci, x_step))
                    dve.tensor_tensor(out[:, :, :], x[:, :, :], wide(eye), ALU.add).then_inc(vectors.at(step), 1)

                def plus(step, out, own):
                    dve.wait_ge(products.sem, products.value(ci, name))
                    dve.wait_ge(vectors.sem, vectors.value(ci, own))
                    dve.tensor_tensor(out[:, :, :], ps(name), out[:, :, :], ALU.add).then_inc(vectors.at(step), 1)

                sums = {"R1": (r_, "r"), "Q1": (q_, "q"), "R2": (r_, "r1"), "Q2": (q_, "q1"), "R3": (r_, "r2"), "Q3": (q_, "q2"),
                        "Z1": (r_, "r3"), "Z": (r_, "z1")}
                if name == "U":
                    dve.wait_ge(vectors.sem, vectors.value(ci, ("s", 1)))
                    masked("ud", ud, upper_in)
                    plus_eye("r", r_, ud, "ud")
                elif name == "N":
                    masked("nd", nd, lower_in)
                    plus_eye("q", q_, nd, "nd")
                elif name == "BT":
                    dve.tensor_tensor(ue[:, :, :], ps("U"), wide(upper_out), ALU.mult).then_inc(vectors.at("ue"), 1)
                elif name in ("KA", "BR", "KR"):
                    out, mask = {"KA": (g_ka, upper), "BR": (g_br, upper_eq), "KR": (g_kr, upper_eq)}[name]
                    masked(reader[name][1], out, mask)
                elif name in sums:
                    plus(reader[name][1], *sums[name])
                elif name == "S":
                    dve.wait_ge(products.sem, products.value(ci, "S"))
                    dve.tensor_tensor(st_new[:, :, :], ps("S"), st[:, :, :], ALU.add).then_inc(vectors.at("s_sum"), 1)
                elif name == "O":
                    dve.wait_ge(products.sem, products.value(ci, "O"))
                    dve.wait_ge(vectors.sem, vectors.value(ci, "s_sum"))
                    dve.tensor_tensor(st[:, :, :], st_new[:, :, :], t.p_end[:, :, bass.ds(ci, 1)].broadcast_to([P, PAIRS, CHUNK]),
                                      ALU.mult).then_inc(vectors.at("s"), 1)

            def front_step(nb, name, ins):
                ins.then_inc(front_dve.at(name), 1)
                dve.wait_ge(front_dve.sem, front_dve.value(nb, name))
                dve.sem_inc(waited_dve, 1)

            def norm_slot(nb, s, rows):
                def per_pair(n):
                    i = PARAMS.index(n) * PAIRS
                    return t.par[:, i:i + PAIRS].unsqueeze(2).broadcast_to([P, PAIRS, P])

                of, vf, sf = flat(o), flat(vt2), flat(gn_std)
                hr, n = h[0:rows, :], slice(0, rows)
                if s == 0:
                    if rows == P:
                        dve.wait_ge(copies.sem, copies.value(nb * 2 + 2, "o"))
                    front_step(nb, "rk0", dve.tensor_tensor(flat(rk), flat(rh2), flat(ka2), ALU.mult))
                    front_step(nb, "rk", dve.tensor_tensor(rk[:, :, :], rk[:, :, :], per_pair("r_k"), ALU.mult))
                elif s == 1:
                    dve.wait_ge(front_pe.sem, front_pe.value(nb, "mean"))
                    front_step(nb, "centred", dve.scalar_tensor_tensor(out=of, in0=bank[0][:, :], scalar=-1.0 / HD, in1=of, op0=ALU.mult, op1=ALU.add))
                elif s == 2:
                    dve.wait_ge(front_pe.sem, front_pe.value(nb, "bonus"))
                    front_step(nb, "bonus", dve.tensor_tensor(vf, bank[1][:, :], vf, ALU.mult))
                elif s == 3:
                    dve.wait_ge(front_pe.sem, front_pe.value(nb, "var"))
                    front_step(nb, "var", dve.tensor_scalar(sf, bank[3][:, :], 1.0 / HD, GN_EPS, ALU.mult, ALU.add))
                elif s == 5:
                    dve.wait_ge(front_act.sem, front_act.value(nb, "gn_std"))
                    front_step(nb, "inv", dve.reciprocal(sf, sf))
                    front_step(nb, "scaled", dve.tensor_tensor(of, of, sf, ALU.mult))
                elif s == 6:
                    front_step(nb, "gain", dve.tensor_tensor(o[:, :, :], o[:, :, :], per_pair("gn_g"), ALU.mult))
                    front_step(nb, "offset", dve.tensor_tensor(o[:, :, :], o[:, :, :], per_pair("gn_b"), ALU.add))
                elif s == 7:
                    front_step(nb, "plus", dve.tensor_tensor(of, of, vf, ALU.add))
                    dve.wait_ge(front_pe.sem, front_pe.value(nb, "gate"))
                    front_step(nb, "y", dve.tensor_tensor(of, bank[2][:, :], of, ALU.mult))
                elif s == 12:
                    dve.wait_ge(h_loaded, nb * 16 + 16)
                    dve.wait_ge(front_pe.sem, front_pe.value(nb, "mix"))
                    front_step(nb, "sum", dve.scalar_tensor_tensor(out=hr, in0=hr, scalar=ALPHA, in1=flat(wide_ps[n, :, :]), op0=ALU.mult, op1=ALU.add))
                elif s == 13:
                    front_step(nb, "bn0", dve.bn_stats(st1[n, 0:6], hr[:, 0:512]))
                    front_step(nb, "bn1", dve.bn_stats(st1[n, 6:12], hr[:, 512:1024]))
                    front_step(nb, "aggr", dve.bn_aggr(mo1[n, :], st1[n, :]))
                    front_step(nb, "ln_var", dve.tensor_scalar(rs1[n, :], mo1[n, 1:2], LN_EPS, None, ALU.add))
                elif s == 14:
                    dve.wait_ge(front_act.sem, front_act.value(nb, "ln_std"))
                    front_step(nb, "ln_inv", dve.reciprocal(rs1[n, :], rs1[n, :]))
                    front_step(nb, "ln_x", dve.tensor_scalar(hr, hr, mo1[n, 0:1], rs1[n, :], ALU.subtract, ALU.mult))
                elif s == 15:
                    front_step(nb, "ln_g", dve.tensor_tensor(hr, hr, ln1_gb[n, 0, :], ALU.mult))
                    front_step(nb, "h1", dve.tensor_tensor(hr, hr, ln1_gb[n, 1, :], ALU.add))

            def top16(nb, j, rows):
                sc, rest = score_ps(j)[0:rows, 0:N_KEYS], others[0:rows, :]
                val, place = t.top_val[0:rows, j // 2, j % 2, :], places[0:rows, :]
                dve.wait_ge(front_pe.sem, front_pe.value(nb, f"s{j}"))
                dve.sem_inc(waited_dve, 1)
                front_step(nb, f"max{j}", dve.max(val[:, 0:8], sc))
                front_step(nb, f"place{j}", dve.max_index(place[:, 0:8], val[:, 0:8], sc))
                front_step(nb, f"others{j}", dve.match_replace(rest, val[:, 0:8], sc, NEG))
                front_step(nb, f"max2_{j}", dve.max(val[:, 8:16], rest))
                front_step(nb, f"place2_{j}", dve.max_index(place[:, 8:16], val[:, 8:16], rest))
                front_step(nb, f"top{j}", dve.tensor_copy(t.top_idx[0:rows, j // 2, j % 2, :], place))

            def front_slot(nb, n, s):
                rows = NS if isinstance(nb, int) and nb == TBLOCKS else P
                if n <= 4 and rows == P:
                    chunk_step(*chunk_slot(nb, n, s))
                elif (n, s) == (1, 0):
                    for dst, src in ((rh2, t.samp[:, 0]), (ka2, t.samp[:, 1]), (vt2, t.samp[:, 2])):
                        done(dve.tensor_copy(dst[:, :, 0:NS], src.rearrange("p b c -> p c b")), sample_ready)
                    done(dve.tensor_copy(o[:, :, 0:NS], t.samp_o[:, :, :]), sample_ready)
                elif n == 5:
                    norm_slot(nb, s, rows)
                elif n >= 6:
                    for j in queries(n, s, 1):
                        top16(nb, j, rows)

            def pick(turn, par, head, step):
                step(pick_experts(dve, step, P, t.top_val[:, head], t.top_idx[:, head], k, best[:, par, :], idx[:, head % 4, :]))
                step(dve.tensor_scalar(neg_max[:, par, :], best[:, par, 0:1], -1.0, None, ALU.mult))
                dve.sem_inc(picked, 1)

            def counted(sem, base):
                n = [0]

                def step(ins):
                    n[0] += 1
                    ins.then_inc(sem, 1)
                    dve.wait_ge(sem, base + n[0])
                    dve.sem_inc(waited_dve, 1)
                return step, n

            def a_turn(turn, n, nb, sums=True, dots_left=True, new_block=None):
                par = n % 2
                if new_block is not None:
                    step, _ = counted(block_chain, (new_block - 1) * BLOCK_STEPS)
                    step(dve.tensor_scalar(res[:, :], x[:, :], ALPHA, None, ALU.mult))
                    take_rows(new_block)
                if not dots_left:
                    return
                for s in range(TOPK):
                    dve.wait_ge(u_landed[s % RING], (turn * 2 + s // RING + 1) * 16)
                    dve.tensor_tensor_reduce(u[:, s % RING, :], u[:, s % RING, :], x[:, :], 1.0, 0.0, ALU.mult, ALU.add,
                                             hu[:, par, s:s + 1]).then_inc(dots, 1)
                    if nb is not None:
                        front_slot(nb, n, s)
                step, steps = counted(turn_chain, turn * TURN_STEPS)
                dve.wait_ge(exp_ready, turn + 1)
                step(dve.reciprocal(total[:, par, :], total[:, par, :]))
                dve.wait_ge(gelu_ready, turn + 1)
                dve.scalar_tensor_tensor(out=act_v[:, par, :], in0=act_v[:, par, :], scalar=total[:, par, :], in1=ex[:, par, :],
                                         op0=ALU.mult, op1=ALU.mult).then_inc(act_ready, 1)
                if not (isinstance(turn, int) and n >= H - 2):
                    if sums:
                        dve.wait_ge(v_used, turn * TOPK - TOPK + RING)
                        dve.sem_inc(waited_dve, 1)
                    pick(turn + 2, par, (n + 2) % H, step)
                    assert steps[0] == TURN_STEPS, steps
                else:
                    dve.sem_inc(turn_chain, TURN_STEPS - steps[0])

            def take_rows(b):
                dve.wait_ge(front_pe.sem, front_pe.value(b, "turned"))
                dve.tensor_copy(x[:, :], h[:, :]).then_inc(x_taken, 1)
                dve.wait_ge(x_taken, b + 1)

            def finish(b):
                last = isinstance(b, int)
                step, n = counted(block_chain, b * BLOCK_STEPS + 1)
                if last:
                    dve.tensor_scalar(res[:, :], x[:, :], ALPHA, None, ALU.mult).then_inc(block_chain, 1)
                    dve.wait_ge(block_chain, b * BLOCK_STEPS + 1)
                dve.wait_ge(v_used, (b + 1) * (H * TOPK) + RING)
                dve.wait_ge(y_free, b + 1)
                dve.tensor_tensor(y[:, :], flat(out_ps[:, :, :]), res[:, :], ALU.add).then_inc(sum_read, 1)
                dve.wait_ge(sum_read, b + 2)
                step(dve.bn_stats(stats[:, 0:6], y[:, 0:512]))
                step(dve.bn_stats(stats[:, 6:12], y[:, 512:1024]))
                step(dve.bn_aggr(moments[:, :], stats[:, :]))
                dve.tensor_scalar(rstd[:, :], moments[:, 1:2], LN_EPS, None, ALU.add).then_inc(var_ready, 1)
                dve.wait_ge(std_ready, b + 1)
                step(dve.reciprocal(rstd[:, :], rstd[:, :]))
                step(dve.tensor_scalar(y[:, :], y[:, :], moments[:, 0:1], rstd[:, :], ALU.subtract, ALU.mult))
                step(dve.tensor_tensor(y[:, :], y[:, :], ln2_gb[:, 0, :], ALU.mult))
                dve.tensor_tensor(y[:, :], y[:, :], ln2_gb[:, 1, :], ALU.add).then_inc(y_ready, 1)
                if not last:
                    dve.sem_inc(block_chain, BLOCK_STEPS - 1 - n[0])

            done(dve.memset(st[:, :, :], 0.0), start_chain)
            vectors.start(dve)
            front_dve.start(dve)
            dve.wait_ge(consts, N_CONSTS)
            dve.sem_inc(y_free, 1)
            for name in PRODUCTS:
                chunk_step(0, name, CHUNK)
            front(front_slot, 0)
            for turn in range(2):
                pick(turn, turn, turn, lambda ins: done(ins, start_chain))
            take_rows(0)
            over_turns(dve, a_turn, finish)


PARAMS = ["w0", "a0", "k_k", "k_a", "r_k", "gn_g", "gn_b", "mu_r", "mu_k", "mu_v", "cw0", "cw1", "cw2"]

PAR_COLS = len(PARAMS) * PAIRS + 2


class Tiles:
    pass


def clear_semaphores(nc):
    used = sorted(nc.released_uncleared_semaphores)
    while used:
        n = 1
        while n < len(used) and used[n] == used[0] + n:
            n += 1
        nc.gpsimd.sem_clear(range(used[0], used[0] + n))
        used = used[n:]
    nc.all_engine_barrier()


def build(nc, d):
    t = Tiles()
    outer, upto2 = ExitStack(), ExitStack()
    with outer:
        sb = lambda n, s, c=outer: c.enter_context(nc.sbuf_tensor(n, s, F32))
        t.h_stored, t.spilled, t.y_spilled, t.sp_landed = (
            [outer.enter_context(nc.semaphore(f"{n}{i}")) for i in range(c)]
            for n, c in (("h_stored", 3), ("spilled", 2), ("y_spilled", 2), ("sp_landed", 2)))
        t.ident, t.head_ones = sb("ident", [P, P]), sb("head_ones", [P, P])
        t.par = sb("par", [P, PAR_COLS])
        t.mu_lora = t.par[:, PAR_COLS - 2:]
        t.samp = sb("samp", [P, 6, NS, PAIRS])
        t.samp_o = sb("samp_o", [P, PAIRS, NS])
        t.p_end = sb("p_end", [P, PAIRS, CHUNKS])
        t.z_out = sb("z_out", [P, PAIRS, NS + 2])
        t.conv_state = sb("conv_state", [P, PAIRS, 2 * NS])
        t.keysT = sb("keysT", [P, HP, N_KEYS])
        t.top_val, t.top_idx = sb("top_val", [P, PEER_HEADS, 2, TOPK]), sb("top_idx", [P, PEER_HEADS, 2, TOPK])
        with upto2:
            t.hT = sb("hT", [P, KT, PROJ_COLS], upto2)
            input_phase(nc, t, d)
            project_phase(nc, t, d)
        sample_phase(nc, t, d)
        clear_semaphores(nc)
        steady_phase(nc, t, d)
        sample_experts_phase(nc, t, d)


_INS = ['x_prompt', 'x_sample', 'state_conv', 'state_shift', 'state_wkv', 'meta_tokens', 'ln_in_g', 'ln_in_b',
        'w_in', 'conv_w', 'mu', 'w0', 'w_up', 'a0', 'a_up', 'g_up', 'k_k', 'k_a', 'r_k', 'gn_g', 'gn_b', 'w_o',
        'ln1_g', 'ln1_b', 'w_q', 'sub_keys', 'peer_u', 'peer_v', 'ln2_g', 'ln2_b']
_OUTS = [("y_prompt", (1, SEQ, D)), ("y_sample", (NS, 1, D)), ("new_conv_prompt", (1, 1, 2, CONVW)),
         ("new_shift_prompt", (1, 1, D)), ("new_wkv_prompt", (1, 1, HEADS, HD, HD)),
         ("new_conv_sample", (1, NS, 2, CONVW)), ("new_shift_sample", (1, NS, D)),
         ("new_wkv_sample", (1, NS, HEADS, HD, HD))]
_SCRATCH = [("h_rows", (PROJ_COLS, D), F32), ("samp_rows", (NS * PAIRS, 2, 6, HD), F32), ("h1_rows", (NS, D), F32),
            ("operands", (5, P, PAIRS, WKV_COLS), F32), ("y_conv", (P, PAIRS, PROJ_COLS), F32), ("lora_g", (G_LORA, PROJ_COLS), F32),
            ("sp_idx", (NS, SLOTS), U32), ("sp_gate", (NS, SLOTS), F32)]


def kernel(**inputs):
    import numpy as _np
    import concourse.bacc as _bacc
    from concourse import mybir as _mybir
    from concourse.bass_utils import run_bass_kernel_spmd as _run

    nc = _bacc.Bacc("TRN2", target_bir_lowering=False, num_devices=1)
    arrays, tensors = {}, {}
    for name in _INS:
        a = _np.ascontiguousarray(inputs[name])
        arrays[f"in_{name}_dram"] = a
        tensors[name] = nc.dram_tensor(f"in_{name}_dram", a.shape, _mybir.dt.from_np(a.dtype), kind="ExternalInput").ap()
    for i, (name, shape) in enumerate(_OUTS):
        tensors[name] = nc.dram_tensor(f"out_{i}_dram", shape, _mybir.dt.float32, kind="ExternalOutput").ap()
    for name, shape, dt in _SCRATCH:
        tensors[name] = nc.dram_tensor(f"scratch_{name}", shape, dt, kind="Internal").ap()
    build(nc, tensors)
    r = _run(nc, [arrays], core_ids=[0])
    return tuple(r.results[0][f"out_{i}_dram"] for i in range(len(_OUTS)))
```

```python
from contextlib import ExitStack
import math

import concourse.bass as bass
from concourse import mybir

F32 = mybir.dt.float32
U32 = mybir.dt.uint32
ALU = mybir.AluOpType
ACT = mybir.ActivationFunctionType
AX_X = mybir.AxisListType.X

P = 128
D = 1024
KT = D // P
SEQ = 1024
NS = 8
N_META = 16
CONVW = 512
RW = 512
PAIRS = RW // P
HD = 64
HEADS = 8
W_LORA = A_LORA = 32
G_LORA = 96
RW0 = 3 * CONVW
LORA0 = RW0 + 3 * RW
C_META = 2 * NS
C_PROMPT = C_META + N_META
PROJ_COLS = C_PROMPT + SEQ
COLS3 = PROJ_COLS // 3
CHUNK = 64
WKV_OFF = 32
WKV_COLS = PROJ_COLS + WKV_OFF
CHUNKS = WKV_COLS // CHUNK
LN_EPS = 1e-5
GN_EPS = HD * 1e-5
ALPHA = 2.0 ** 0.25
LOG_DECAY = math.exp(-0.5)
PEER_HEADS = 8
N_KEYS = 128
TOPK = 16
SLOTS = PEER_HEADS * TOPK
TBLOCKS = SEQ // P
HP = 2 * PEER_HEADS
RING = 8
NEG = -3.0e38


def signals(eng):
    count = {}

    def done(ins, sem):
        count[sem.name] = count.get(sem.name, 0) + 1
        ins.then_inc(sem, 1)
        eng.wait_ge(sem, count[sem.name])
    return done


def chained(eng, sem):
    count = [0]

    def step(ins):
        count[0] += 1
        ins.then_inc(sem, 1)
        eng.wait_ge(sem, count[0])
    return step


def input_phase(nc, t, d):
    ctx = ExitStack()
    with ctx:
        NX = 3
        xrow = ctx.enter_context(nc.sbuf_tensor("xrow", [P, NX, D], F32))
        ln_gb = ctx.enter_context(nc.sbuf_tensor("ln_gb", [P, 2, D], F32))
        stats = ctx.enter_context(nc.sbuf_tensor("stats", [P, NX, 12], F32))
        moments = ctx.enter_context(nc.sbuf_tensor("moments", [P, NX, 2], F32))
        rstd = ctx.enter_context(nc.sbuf_tensor("rstd", [P, NX, 1], F32))
        conv_rows = ctx.enter_context(nc.sbuf_tensor("conv_rows", [2 * NS, CONVW], F32))
        key_rows = ctx.enter_context(nc.sbuf_tensor("key_rows", [N_KEYS, HP, P], F32))
        par_rows = ctx.enter_context(nc.sbuf_tensor("par_rows", [PAR_COLS, P], F32))
        turned = ctx.enter_context(nc.psum_tensor("turned", [P, 2, 512], F32))
        keys_ps = ctx.enter_context(nc.psum_tensor("keys_ps", [P, 2, 4, N_KEYS], F32))
        turned2 = ctx.enter_context(nc.psum_tensor("turned2", [P, 2, 512], F32))
        sem = lambda n: ctx.enter_context(nc.semaphore(n))
        const_loaded, conv_loaded = sem("const_loaded"), sem("conv_loaded")
        x_loaded = [sem(f"x_loaded{i}") for i in range(NX)]
        shift_loaded, ident_done, var_ready, std_ready = sem("shift_loaded"), sem("ident_done"), sem("var_ready"), sem("std_ready")
        vec_chain, norm_ready, turned_ready, turned_read = sem("vec_chain"), sem("norm_ready"), sem("turned_ready"), sem("turned_read")
        h_stored = t.h_stored
        rows_cleared, keys_loaded, keys_turned, keys_read = sem("rows_cleared"), sem("keys_loaded"), sem("keys_turned"), sem("keys_read")
        block = ctx.enter_context(nc.Block())
        TILES = 1 + TBLOCKS
        rows = [C_PROMPT] + [P] * TBLOCKS

        @block.sync
        def _(sp):
            sp.dma_start(ln_gb[:, 0, :], d["ln_in_g"][None, :].broadcast_to([P, D])).then_inc(const_loaded, 16)
            sp.dma_start(ln_gb[:, 1, :], d["ln_in_b"][None, :].broadcast_to([P, D])).then_inc(const_loaded, 16)
            def load_tile(i):
                s = i % NX
                if i >= NX:
                    sp.wait_ge(turned_ready, 2 * (i - NX + 1))
                    sp.wait_ge(h_stored[s], 16 * (i // NX))
                if i == 0:
                    sp.dma_start(xrow[0:NS, s, :], d["x_sample"][:, 0, :]).then_inc(x_loaded[s], 16)
                    sp.dma_start(xrow[NS:2 * NS, s, :], d["state_shift"][0]).then_inc(x_loaded[s], 16)
                    sp.dma_start(xrow[C_META:C_PROMPT, s, :], d["meta_tokens"]).then_inc(x_loaded[s], 16)
                else:
                    sp.dma_start(xrow[:, s, :], d["x_prompt"][0, (i - 1) * P:i * P, :]).then_inc(x_loaded[s], 16)
            for i in range(NX):
                load_tile(i)
            sp.dma_start(conv_rows[:, :], d["state_conv"][0].rearrange("b j c -> (b j) c")).then_inc(conv_loaded, 16)
            sp.wait_ge(rows_cleared, 1)
            for n in PARAMS:
                src = {"mu_r": d["mu"][0, 0:RW], "mu_k": d["mu"][0, RW:2 * RW], "mu_v": d["mu"][0, 2 * RW:3 * RW],
                       "r_k": d["r_k"][0].rearrange("h k -> (h k)"),
                       "cw0": d["conv_w"][0, 0], "cw1": d["conv_w"][0, 1], "cw2": d["conv_w"][0, 2]}.get(n)
                src = d[n][0] if src is None else src
                r0 = PARAMS.index(n) * PAIRS
                sp.dma_start(par_rows[r0:r0 + PAIRS, :], src.rearrange("(c p) -> c p", p=P)).then_inc(conv_loaded, 16)
            mu1 = d["mu"][0:1, 3 * RW:]
            sp.dma_start(par_rows[PAR_COLS - 2:PAR_COLS - 1, 0:2 * W_LORA], mu1[:, 0:2 * W_LORA]).then_inc(conv_loaded, 16)
            sp.dma_start(par_rows[PAR_COLS - 1:PAR_COLS, 0:G_LORA], mu1[:, 2 * W_LORA:]).then_inc(conv_loaded, 16)
            sp.dma_start(key_rows[:, :, :], d["sub_keys"][0].rearrange("h s n k -> n (h s) k")).then_inc(keys_loaded, 16)
            sp.wait_ge(norm_ready, 1)
            sp.dma_start(xrow[NS:2 * NS, 0, :], d["state_shift"][0]).then_inc(shift_loaded, 16)
            for i in range(NX, TILES):
                load_tile(i)

        @block.gpsimd
        def _(pool):
            done = signals(pool)
            done(pool.memset(t.ident[:, :], 0.0), ident_done)
            done(pool.affine_select(out=t.ident[:, :], in_=t.ident[:, :], compare_op=ALU.not_equal, fill=1.0,
                                    base=0, pattern=[[-1, P]], channel_multiplier=1), ident_done)
            done(pool.memset(t.head_ones[:, :], 0.0), ident_done)
            done(pool.memset(t.head_ones[0:HD, 0:HD], 1.0), ident_done)
            done(pool.memset(t.head_ones[HD:P, HD:P], 1.0), ident_done)
            for i in range(TILES):
                pool.wait_ge(norm_ready, i + 1)
                n = rows[i]
                c0 = 0 if i == 0 else C_PROMPT + (i - 1) * P
                if i == 0:
                    pool.dma_start(d["h_rows"][0:NS, :], xrow[0:NS, 0, :]).then_inc(h_stored[0], 16)
                else:
                    pool.dma_start(d["h_rows"][c0:c0 + n, :], xrow[:, i % NX, :]).then_inc(h_stored[i % NX], 16)
            for s in range(NX):
                pool.wait_ge(h_stored[s], 16 * len(range(s, TILES, NX)))

        @block.vector
        def _(dve):
            step = chained(dve, vec_chain)
            dve.memset(par_rows[32:PAR_COLS, :], 0.0).then_inc(rows_cleared, 1)
            dve.wait_ge(const_loaded, 32)

            def statistics(i):
                s, n = i % NX, rows[i]
                dve.wait_ge(x_loaded[s], 48 + 16 * (i // NX) if s == 0 else 16 * (i // NX + 1))
                x = xrow[0:n, s, :]
                dve.bn_stats(stats[0:n, s, 0:6], x[:, 0:512])
                step(dve.bn_stats(stats[0:n, s, 6:12], x[:, 512:1024]))
                step(dve.bn_aggr(moments[0:n, s, :], stats[0:n, s, :]))
                dve.tensor_scalar(rstd[0:n, s, :], moments[0:n, s, 1:2], LN_EPS, None, ALU.add).then_inc(var_ready, 1)

            statistics(0)
            for i in range(TILES):
                if i + 1 < TILES:
                    statistics(i + 1)
                s, n = i % NX, rows[i]
                x = xrow[0:n, s, :]
                dve.wait_ge(std_ready, i + 1)
                step(dve.reciprocal(rstd[0:n, s, :], rstd[0:n, s, :]))
                step(dve.tensor_scalar(x, x, moments[0:n, s, 0:1], rstd[0:n, s, :], ALU.subtract, ALU.mult))
                step(dve.tensor_tensor(x, x, ln_gb[0:n, 0, :], ALU.mult))
                dve.tensor_tensor(x, x, ln_gb[0:n, 1, :], ALU.add).then_inc(norm_ready, 1)

        @block.tensor
        def _(pe):
            pe.wait_ge(ident_done, 5)
            for i in range(TILES):
                s, n = i % NX, rows[i]
                pe.wait_ge(norm_ready, i + 1)
                if i == 0:
                    pe.wait_ge(shift_loaded, 16)
                for half in range(2):
                    if i >= 1:
                        pe.wait_ge(turned_read, 2 * i - 1 + half)
                    buf = (turned, turned2)[half]
                    for k in range(4):
                        kt = half * 4 + k
                        last = pe.transpose(buf[:, 0, k * P:k * P + n], xrow[0:n, s, kt * P:(kt + 1) * P], t.ident[0:n, 0:n])
                    last.then_inc(turned_ready, 1)
            pe.wait_ge(conv_loaded, 16 * (len(PARAMS) + 3))
            for c in range(4):
                last = pe.transpose(turned[:, 1, c * 16:c * 16 + 16], conv_rows[:, c * P:(c + 1) * P], t.ident[0:16, 0:16])
            pe.transpose(turned[:, 1, 64:64 + PAR_COLS], par_rows[:, :], t.ident[0:PAR_COLS, 0:PAR_COLS]).then_inc(turned_ready, 1)
            pe.wait_ge(keys_loaded, 16)
            for g in range(HP // 4):
                if g >= 2:
                    pe.wait_ge(keys_read, g - 1)
                for n in range(4):
                    last = pe.transpose(keys_ps[:, g % 2, n, :], key_rows[:, 4 * g + n, :], t.ident[:, :])
                last.then_inc(keys_turned, 1)

        @block.scalar
        def _(act):
            act_chain = ctx.enter_context(nc.semaphore("in_act_chain"))

            def root(i):
                s, n = i % NX, rows[i]
                act.wait_ge(var_ready, i + 1)
                act.activation(rstd[0:n, s, :], rstd[0:n, s, :], ACT.Sqrt).then_inc(std_ready, 1)

            root(0)
            for i in range(TILES):
                n = rows[i]
                c0 = 0 if i == 0 else C_PROMPT + (i - 1) * P
                if i + 1 < TILES:
                    root(i + 1)
                for half in range(2):
                    buf = (turned, turned2)[half]
                    act.wait_ge(turned_ready, 2 * i + 1 + half)
                    act.activation(t.hT[:, half * 4:half * 4 + 4, c0:c0 + n],
                                   buf[:, 0, :].rearrange("p (k n) -> p k n", k=4)[:, :, 0:n], ACT.Copy).then_inc(turned_read, 1)
            act.wait_ge(turned_ready, 2 * TILES + 1)
            act.activation(t.par[:, :], turned[:, 1, 64:64 + PAR_COLS], ACT.Copy).then_inc(act_chain, 1)
            act.activation(t.conv_state[:, :, :], turned[:, 1, 0:64].rearrange("p (c n) -> p c n", c=4), ACT.Copy).then_inc(act_chain, 1)
            act.wait_ge(act_chain, 2)
            for g in range(HP // 4):
                act.wait_ge(keys_turned, g + 1)
                act.activation(t.keysT[:, 4 * g:4 * g + 4, :], keys_ps[:, g % 2, :, :], ACT.Copy).then_inc(keys_read, 1)


def project_phase(nc, t, d):
    ctx = ExitStack()
    with ctx:
        sb = lambda n, s: ctx.enter_context(nc.sbuf_tensor(n, s, F32))
        sem = lambda n: ctx.enter_context(nc.semaphore(n))
        NW = 3
        OPERANDS = ("alpha", "beta", "kappa", "rho", "vT")
        alpha, beta, kappa, rho, vT = (sb(n, [P, 2, WKV_COLS]) for n in OPERANDS)
        lora_g = sb("lora_g", [G_LORA, PROJ_COLS])
        pair_ready = sem("pair_ready")
        w_ring = sb("w_ring", [P, NW, KT, P])
        lora_up = sb("lora_up", [2 * W_LORA, RW])
        lora_wa = sb("lora_wa", [2 * W_LORA, PROJ_COLS])
        raw = sb("raw", [P, 2, PROJ_COLS])
        diff = sb("diff", [P, PROJ_COLS])
        sig = sb("sig", [P, PROJ_COLS])
        csig = sb("csig", [P, PROJ_COLS])
        p_inv = sb("p_inv", [P, PROJ_COLS])
        aa = sb("aa", [P, PROJ_COLS])
        keep = sb("keep", [P, PROJ_COLS])
        jobs_ps = [ctx.enter_context(nc.psum_tensor(f"job_ps{i}", [P, 3, 512], F32)) for i in range(2)]
        w_loaded = [sem(f"w_loaded{i}") for i in range(NW)]
        par_loaded = sem("par_loaded")
        job_done = sem("job_done")
        job_read = [sem("job_read0"), sem("job_read1")]
        raw_ready, raw_used, vec_chain, act_chain = sem("raw_ready"), sem("raw_used"), sem("vec_chain2"), sem("act_chain2")
        lora_mixed, lora_ready, kk_ready, square_ready = sem("lora_mixed"), sem("lora_ready"), sem("kk_ready"), sem("square_ready")
        sig_ready, sig_used, aa_ready, aa_used = sem("sig_ready"), sem("sig_used"), sem("aa_ready"), sem("aa_used")
        csig_ready, p_inv_ready, p_inv_used = sem("csig_ready"), sem("p_inv_ready"), sem("p_inv_used")
        p_prev_ready, p_cum_ready, p_cum_used = sem("p_prev_ready"), sem("p_cum_ready"), sem("p_cum_used")

        jobs = [("wa", 0, LORA0, 2 * W_LORA), ("gd", 0, LORA0 + 2 * W_LORA, G_LORA)]
        for c in range(PAIRS):
            jobs += [("k", c, RW0 + RW + c * P, P), ("w", c, None, P), ("a", c, None, P), ("r", c, RW0 + c * P, P),
                     ("norm", c, None, P), ("v", c, RW0 + 2 * RW + c * P, P)]
        streamed = [i for i, job in enumerate(jobs) if job[2] is not None]
        in_raw = [i for i, job in enumerate(jobs) if job[0] not in ("w", "a")]

        def param(n, c):
            return t.par[:, PARAMS.index(n) * PAIRS + c:PARAMS.index(n) * PAIRS + c + 1]

        def ps(i, n=P):
            return jobs_ps[i % 2][0:n, :, 0:COLS3]

        def three(x):
            return x.rearrange("p (a b) -> p a b", a=3)

        block = ctx.enter_context(nc.Block())

        @block.sync
        def _(sp):
            for n, i in enumerate(streamed):
                _, _, c0, m = jobs[i]
                if n >= NW:
                    sp.wait_ge(job_done, streamed[n - NW] + 1)
                sp.dma_start(w_ring[:, n % NW, :, 0:m],
                             d["w_in"][0, :, c0:c0 + m].rearrange("(k p) c -> p k c", p=P)).then_inc(w_loaded[n % NW], 16)
                if n == 0:
                    sp.dma_start(lora_up[0:W_LORA, :], d["w_up"][0]).then_inc(par_loaded, 16)
                    sp.dma_start(lora_up[W_LORA:2 * W_LORA, :], d["a_up"][0]).then_inc(par_loaded, 16)

        @block.gpsimd
        def _(pool):
            pool.wait_ge(lora_ready, 2)
            pool.dma_start(d["lora_g"], lora_g[:, :]).then_inc(t.lora_spilled, 16)
            for c in range(PAIRS):
                pool.wait_ge(pair_ready, c + 1)
                for j, x in enumerate((alpha, beta, kappa, rho, vT)):
                    pool.dma_start(d["operands"][j, :, c, :], x[:, c % 2, :]).then_inc(t.spilled[c % 2], 16)
            for s in range(2):
                pool.wait_ge(t.spilled[s], 160)
            pool.wait_ge(t.lora_spilled, 16)

        @block.tensor
        def _(pe):
            for i, (kind, c, c0, m) in enumerate(jobs):
                if i >= 2:
                    pe.wait_ge(job_read[i % 2], i // 2)
                if c0 is not None:
                    n = streamed.index(i)
                    pe.wait_ge(w_loaded[n % NW], 16 * (n // NW + 1))
                    for k in range(KT):
                        for a in range(3):
                            last = pe.matmul(jobs_ps[i % 2][0:m, a, 0:COLS3], w_ring[:, n % NW, k, 0:m],
                                             t.hT[:, k, a * COLS3:(a + 1) * COLS3], start=(k == 0), stop=(k == KT - 1))
                else:
                    if kind == "norm":
                        pe.wait_ge(square_ready, c + 1)
                        lhsT, rhs = t.head_ones[:, :], p_inv[:, :]
                    else:
                        if i == 3:
                            pe.wait_ge(lora_ready, 1)
                            pe.wait_ge(lora_mixed, 1)
                            pe.wait_ge(par_loaded, 32)
                        rows = slice(0, W_LORA) if kind == "w" else slice(W_LORA, 2 * W_LORA)
                        lhsT, rhs = lora_up[rows, c * P:(c + 1) * P], lora_wa[rows, :]
                    for a in range(3):
                        last = pe.matmul(jobs_ps[i % 2][:, a, 0:COLS3], lhsT, rhs[:, a * COLS3:(a + 1) * COLS3],
                                         start=True, stop=True)
                last.then_inc(job_done, 1)

        @block.scalar
        def _(act):
            done = signals(act)
            done(act.activation(t.samp[:, 5, 0:1, 0], t.ident[:, 0:1], ACT.Copy), act_chain)
            for i, (kind, c, _, m) in enumerate(jobs):
                if i in in_raw:
                    n = in_raw.index(i)
                    if n >= 2:
                        act.wait_ge(raw_used, n - 1)
                    act.wait_ge(job_done, i + 1)
                    done(act.activation(three(raw[0:m, n % 2, :]), ps(i, m), ACT.Sqrt if kind == "norm" else ACT.Copy), raw_ready)
                    act.sem_inc(job_read[i % 2], 1)
                if kind == "wa":
                    act.wait_ge(lora_mixed, 1)
                    act.activation(lora_wa[0:W_LORA, :], lora_wa[0:W_LORA, :], ACT.Tanh).then_inc(lora_ready, 1)
                elif kind == "gd":
                    act.wait_ge(lora_mixed, 2)
                    act.activation(lora_g[0:G_LORA, :], lora_g[0:G_LORA, :], ACT.Sigmoid).then_inc(lora_ready, 1)
                elif kind == "w":
                    if c:
                        act.wait_ge(sig_used, c)
                    act.wait_ge(job_done, i + 1)
                    done(act.activation(three(sig[:, :]), ps(i), ACT.Sigmoid, bias=param("w0", c)), sig_ready)
                    act.sem_inc(job_read[i % 2], 1)
                    act.wait_ge(sig_ready, c + 1)
                    act.activation(t.samp[:, 5, :, c], sig[:, 0:NS], ACT.Exp, scale=-LOG_DECAY).then_inc(act_chain, 1)
                elif kind == "a":
                    if c:
                        act.wait_ge(aa_used, c)
                    act.wait_ge(job_done, i + 1)
                    done(act.activation(three(aa[:, :]), ps(i), ACT.Sigmoid, bias=param("a0", c)), aa_ready)
                    act.sem_inc(job_read[i % 2], 1)
                    act.wait_ge(kk_ready, c + 1)
                    if c:
                        act.wait_ge(p_inv_used, c)
                    act.activation(p_inv[:, :], alpha[:, c % 2, WKV_OFF:], ACT.Square).then_inc(square_ready, 1)
                elif kind == "norm":
                    act.wait_ge(csig_ready, c + 1)
                    act.activation(p_inv[:, :], csig[:, :], ACT.Exp, scale=LOG_DECAY).then_inc(p_inv_ready, 1)
                    act.activation(sig[:, :], sig[:, :], ACT.Exp, scale=-LOG_DECAY).then_inc(p_prev_ready, 1)
                    act.wait_ge(p_inv_ready, c + 1)
                    act.activation(csig[:, :], csig[:, :], ACT.Exp, scale=-LOG_DECAY).then_inc(p_cum_ready, 1)

        @block.vector
        def _(dve):
            done = signals(dve)
            step = lambda ins: done(ins, vec_chain)
            step(dve.memset(keep[:, :], 1.0))
            step(dve.memset(keep[:, C_META:C_META + 1], 0.0))
            step(dve.memset(keep[:, C_PROMPT:].rearrange("p (a b) -> p a b", b=CHUNK)[:, :, 0:1], 0.0))
            step(dve.memset(diff[:, NS:2 * NS], 0.0))
            for x in (alpha, beta, kappa, rho, vT):
                step(dve.memset(x[:, :, 0:WKV_OFF], 0.0))

            def shift_mix(i, p, m, mu, out):
                dve.wait_ge(raw_ready, in_raw.index(i) + 1)
                step(dve.tensor_tensor(diff[0:m, 0:NS], p[0:m, NS:2 * NS], p[0:m, 0:NS], ALU.subtract))
                step(dve.memset(p[0:m, C_META - 1:C_META], 0.0))
                step(dve.tensor_tensor(diff[0:m, C_META:], p[0:m, C_META - 1:PROJ_COLS - 1], p[0:m, C_META:], ALU.subtract))
                done(dve.scalar_tensor_tensor(out=out, in0=diff[0:m, :], scalar=mu, in1=p[0:m, :], op0=ALU.mult, op1=ALU.add), raw_used)

            for i, (kind, c, _, m) in enumerate(jobs):
                al, be, ka, rh, vt = (x[:, c % 2, WKV_OFF:] for x in (alpha, beta, kappa, rho, vT))
                p = raw[:, in_raw.index(i) % 2, :] if i in in_raw else None
                if kind == "wa":
                    shift_mix(i, p, m, t.mu_lora[0:m, 0:1], lora_wa[:, :])
                    dve.sem_inc(lora_mixed, 1)
                elif kind == "gd":
                    shift_mix(i, p, m, t.mu_lora[0:m, 1:2], lora_g[0:m, :])
                    dve.sem_inc(lora_mixed, 1)
                elif kind == "k":
                    if c >= 2:
                        dve.wait_ge(t.spilled[c % 2], 16 * 5)
                    shift_mix(i, p, P, param("mu_k", c), ka)
                    done(dve.tensor_scalar(al, ka, param("k_k", c), None, ALU.mult), kk_ready)
                elif kind == "w":
                    dve.wait_ge(sig_ready, c + 1)
                    dve.wait_ge(act_chain, c + 2)
                    if c:
                        dve.wait_ge(p_cum_used, c)
                    step(dve.tensor_tensor_scan(csig[:, :], keep[:, :], sig[:, :], 0.0, ALU.mult, ALU.add))
                    done(dve.tensor_tensor(sig[:, :], csig[:, :], sig[:, :], ALU.subtract), csig_ready)
                elif kind == "a":
                    dve.wait_ge(aa_ready, c + 1)
                    step(dve.tensor_scalar(diff[:, :], aa[:, :], 1.0, param("k_a", c), ALU.subtract, ALU.mult))
                    step(dve.scalar_tensor_tensor(out=ka, in0=diff[:, :], scalar=1.0, in1=ka, op0=ALU.add, op1=ALU.mult))
                    step(dve.memset(diff[:, NS:2 * NS], 0.0))
                elif kind == "r":
                    shift_mix(i, p, P, param("mu_r", c), rh)
                    step(dve.tensor_copy(t.samp[:, 0, :, c], rh[:, 0:NS]))
                elif kind == "norm":
                    dve.wait_ge(raw_ready, in_raw.index(i) + 1)
                    step(dve.tensor_scalar(p, p, 1e-12, None, ALU.max))
                    step(dve.reciprocal(p, p))
                    done(dve.tensor_tensor(al, al, p, ALU.mult), raw_used)
                    done(dve.tensor_tensor(be, al, aa[:, :], ALU.mult), aa_used)
                    step(dve.tensor_copy(t.samp[:, 1, :, c], ka[:, 0:NS]))
                    step(dve.tensor_copy(t.samp[:, 3, :, c], al[:, 0:NS]))
                    step(dve.tensor_copy(t.samp[:, 4, :, c], be[:, 0:NS]))
                    dve.wait_ge(p_inv_ready, c + 1)
                    step(dve.tensor_tensor(ka, ka, p_inv[:, :], ALU.mult))
                    done(dve.tensor_tensor(be, be, p_inv[:, :], ALU.mult), p_inv_used)
                    dve.wait_ge(p_prev_ready, c + 1)
                    done(dve.scalar_tensor_tensor(out=al, in0=al, scalar=-1.0, in1=sig[:, :], op0=ALU.mult, op1=ALU.mult), sig_used)
                    dve.wait_ge(p_cum_ready, c + 1)
                    step(dve.tensor_tensor(rh, rh, csig[:, :], ALU.mult))
                    done(dve.tensor_copy(t.p_end[:, c, :], csig[:, C_PROMPT - 1:PROJ_COLS:CHUNK]), p_cum_used)
                elif kind == "v":
                    shift_mix(i, p, P, param("mu_v", c), vt)
                    step(dve.tensor_copy(t.samp[:, 2, :, c], vt[:, 0:NS]))
                    for x in (al, be, ka, rh, vt):
                        step(dve.memset(x[:, 0:C_META], 0.0))
                    dve.sem_inc(pair_ready, 1)


class Stages:

    def __init__(self, sem, names):
        self.sem, self.names = sem, names
        self.emitted = 0

    def start(self, eng):
        eng.sem_inc(self.sem, len(self.names))

    def done_by(self, ins, name):
        assert self.names[self.emitted % len(self.names)] == name, name
        self.emitted += 1
        ins.then_inc(self.sem, 1)

    def wait(self, eng, turn, *steps):
        steps = [(x, 0) if isinstance(x, str) else x for x in steps]
        eng.wait_ge(self.sem, turn * len(self.names) + max((1 - back) * len(self.names) + self.names.index(name) + 1
                                                         for name, back in steps))


def pick_experts(dve, step, rows, val, idx, k, best, expert):
    n = slice(0, rows)
    sq = [rows, TOPK, TOPK]
    step(dve.tensor_tensor(k.sums[n], val[n, 0, :].unsqueeze(2).broadcast_to(sq), val[n, 1, :].unsqueeze(1).broadcast_to(sq), ALU.add))
    flat, flat2 = k.sums[n].rearrange("p a b -> p (a b)"), k.sums2[n].rearrange("p a b -> p (a b)")
    step(dve.max(best[n, 0:8], flat))
    step(dve.max_index(k.place[n, 0:8], best[n, 0:8], flat))
    step(dve.match_replace(flat2, best[n, 0:8], flat, NEG))
    step(dve.max(best[n, 8:16], flat2))
    step(dve.max_index(k.place[n, 8:16], best[n, 8:16], flat2))
    step(dve.tensor_single_scalar(k.half[n, 0, :], k.place[n, :], 4, ALU.logical_shift_right))
    step(dve.tensor_single_scalar(k.half[n, 1, :], k.place[n, :], TOPK - 1, ALU.bitwise_and))
    for j in range(2):
        step(dve.tensor_tensor(k.sums[n], k.half[n, j, :].unsqueeze(2).broadcast_to(sq), k.iota[n, :].unsqueeze(1).broadcast_to(sq), ALU.is_equal))
        step(dve.tensor_tensor(k.sums[n], k.sums[n], idx[n, j, :].unsqueeze(1).broadcast_to(sq), ALU.mult))
        step(dve.tensor_reduce(k.number[n, j, :], k.sums[n], AX_X, ALU.add))
    return dve.scalar_tensor_tensor(out=expert[n, :], in0=k.number[n, 0, :], scalar=float(N_KEYS), in1=k.number[n, 1, :],
                                    op0=ALU.mult, op1=ALU.add)


def pick_tiles(nc, ctx, name):
    k = Tiles()
    k.sums = ctx.enter_context(nc.sbuf_tensor(name + "_sums", [P, TOPK, TOPK], F32))
    k.sums2 = ctx.enter_context(nc.sbuf_tensor(name + "_sums2", [P, TOPK, TOPK], F32))
    k.place = ctx.enter_context(nc.sbuf_tensor(name + "_place", [P, TOPK], U32))
    k.half = ctx.enter_context(nc.sbuf_tensor(name + "_half", [P, 2, TOPK], U32))
    k.number = ctx.enter_context(nc.sbuf_tensor(name + "_number", [P, 2, TOPK], F32))
    k.iota = ctx.enter_context(nc.sbuf_tensor(name + "_iota", [P, TOPK], F32))
    return k


def gather(pool, ring, table, index):
    return pool.indirect_dma_start(out=ring, out_offset=None, in_=table, in_offset=bass.IndirectOffsetOnAxis(ap=index, axis=0))


class Stages:

    def __init__(self, sem, names):
        self.sem, self.names = sem, names
        self.emitted = 0

    def start(self, eng):
        eng.sem_inc(self.sem, len(self.names))

    def at(self, name):
        assert self.names[self.emitted % len(self.names)] == name, name
        self.emitted += 1
        return self.sem

    def value(self, turn, *steps):
        steps = [(x, 0) if isinstance(x, str) else x for x in steps]
        return turn * len(self.names) + max((1 - back) * len(self.names) + self.names.index(name) + 1 for name, back in steps)


def steady_phase(nc, t, d):
    ctx = ExitStack()
    with ctx:
        sb = lambda n, s, dt=F32: ctx.enter_context(nc.sbuf_tensor(n, s, dt))
        sem = lambda n: ctx.enter_context(nc.semaphore(n))
        H = PEER_HEADS
        flat = lambda x: x.rearrange("p a b -> p (a b)")
        N_CONSTS = 28
        NW = 4
        k = pick_tiles(nc, ctx, "ep")
        u, v = t.rings[:, 0:RING, :], t.rings[:, RING:2 * RING, :]
        diag = sb("diag", [P, RING, P])
        idx = sb("idx", [P, 4, TOPK], U32)
        best, neg_max = sb("head_best", [P, 2, TOPK]), sb("neg_max", [P, 2, 1])
        ex, total = sb("head_ex", [P, 2, TOPK]), sb("head_total", [P, 2, 1])
        hu, act_v = sb("hu", [P, 2, TOPK]), sb("act_v", [P, 2, TOPK])
        x, res, y = sb("x_rows", [P, D]), sb("res", [P, D]), sb("y_rows", [P, D])
        ln2_gb, ln1_gb = sb("ln2_gb", [P, 2, D]), sb("ln1_gb", [P, 2, D])
        stats, moments, rstd = sb("ep_stats", [P, 12]), sb("ep_moments", [P, 2]), sb("ep_rstd", [P, 1])
        ops = sb("ops", [P, 5, PAIRS, P])
        al2, be2, ka2, rh2, vt2 = (ops[:, j] for j in range(5))
        o = sb("wkv_o", [P, PAIRS, P])
        yc, lora = sb("yc_block", [P, PAIRS, P]), sb("lora_block", [G_LORA, P])
        tile = lambda n: sb(n, [P, PAIRS, CHUNK])
        ud, ue, nd, r_, q_ = (tile(n) for n in ("ud", "ue", "nd", "r_", "q_"))
        shared = sb("front_shared", [P, 6, PAIRS, CHUNK])
        g_ka, g_br, g_kr, be_t, ka_t, v_t = (shared[:, i] for i in range(6))
        rk, square, gn_std = (shared[:, 2 * i:2 * i + 2].rearrange("p a c n -> p (a c n)").rearrange("p (c n) -> p c n", c=PAIRS) for i in range(3))
        u2, n2, u4, n4, u8, n8 = (tile(n) for n in ("u2", "n2", "u4", "n4", "u8", "n8"))
        mt, m_, m2, xx, sa = u2, n2, u4, n4, u8
        st, st_new, s_out = tile("st"), ud, ue
        eye, upper, upper_eq = sb("eye", [P, CHUNK]), sb("upper", [P, CHUNK]), sb("upper_eq", [P, CHUNK])
        upper_in, upper_out, lower_in = sb("upper_in", [P, CHUNK]), sb("upper_out", [P, CHUNK]), sb("lower_in", [P, CHUNK])
        g_up, w_o = sb("g_up", [G_LORA, RW]), sb("w_o", [P, KT, D])
        h, h1T = sb("h_block", [P, D]), sb("h1T", [P, KT, P])
        st1, mo1, rs1 = sb("ln1_stats", [P, 12]), sb("ln1_moments", [P, 2]), sb("ln1_rstd", [P, 1])
        w_q, q = sb("wq_ring", [P, NW, KT, P]), sb("q_T", [P, 2, P])
        others = sb("others", [P, N_KEYS])
        places = sb("top_places", [P, TOPK], U32)
        UNITS, N_CONV_W = 9 * PAIRS, 5
        CONV_STEPS = (3 * 4 + 5) * PAIRS
        KINDS = ("cg", "hv", "bg")
        CONV_SLOTS = 92
        conv_room = t.rings[:, :, :].rearrange("p a b -> p (a b)")[:, KT * PROJ_COLS:]
        conv_w = conv_room[:, 0:N_CONV_W * KT * P].rearrange("p (n k c) -> p n k c", n=N_CONV_W, k=KT)
        conv_cg, conv_y = (conv_room[:, N_CONV_W * KT * P + 2 * i * COLS3:N_CONV_W * KT * P + 2 * (i + 1) * COLS3]
                           .rearrange("p (n c) -> p n c", n=2) for i in range(2))
        conv_z = conv_room[:, N_CONV_W * KT * P + 4 * COLS3:N_CONV_W * KT * P + 4 * COLS3 + PROJ_COLS]
        BH, R = NS * HEADS, 3 * NS * PAIRS
        per_head = lambda x: x.rearrange("p a b -> p (a b)").rearrange("p (j k) -> p j k", k=HD)
        samp_state, samp_term = per_head(w_o[0:BH, 0:KT // 2, :]), per_head(w_o[0:BH, KT // 2:, :])
        samp_rows, samp_vecs, samp_sa = diag[0:R, 0:2, :], per_head(diag[0:BH, 2:5, :]), diag[0:BH, 5, 0:HD]
        samp_o, z_rows = sb("samp_o", [BH, 2, HD]), y[0:NS + 2, 0:CONVW]
        PER = P // NS
        EACH = SLOTS // PER
        assert EACH == RING
        samp_top = flat(ops[:, 0]).rearrange("p (j h a k) -> p j h a k", j=2, h=H, a=2)
        samp_val, samp_place = samp_top[:, 0], samp_top[:, 1]
        samp_best, samp_ex, samp_total = (ops[0:NS, 1, i, :].rearrange("p (h k) -> p h k", h=H) for i in range(3))
        samp_total = samp_total[:, :, 0:1]
        samp_expert = sb("samp_expert", [NS, H, TOPK], U32)
        samp_idx, samp_gate, samp_hu = sb("samp_idx", [P, EACH], U32), sb("samp_gate", [P, EACH]), sb("samp_hu", [P, EACH])
        by_token = sb("by_token", [P, NS])
        y_samp, x_samp = w_o[0:NS, 0, :], w_o[:, 1, :]
        SAMPLE_HEADS = {(8, 2): 0, (8, 7): 1, (8, 12): 2, (9, 2): 3, (9, 7): 4, (9, 12): 5, (10, 1): 6, (10, 3): 7}
        out_ps = ctx.enter_context(nc.psum_tensor("ep_ps", [P, 2, 512], F32))
        bank = [ctx.enter_context(nc.psum_tensor(f"front_ps{i}", [P, 512], F32)) for i in range(4)]
        wide_ps = ctx.enter_context(nc.psum_tensor("front_wide", [P, 2, 512], F32))

        u_landed = [sem(f"u_landed{s}") for s in range(RING)]
        v_landed = [sem(f"v_landed{s}") for s in range(RING)]
        wq_loaded = [sem(f"wq_loaded{s}") for s in range(NW)]
        consts, const_loaded, ops_loaded, h_loaded = sem("st_consts"), sem("st_const_loaded"), sem("ops_loaded"), sem("h_loaded")
        x_taken, turn_chain, block_chain, start_chain = sem("x_taken"), sem("turn_chain"), sem("block_chain"), sem("start_chain")
        picked, dots, gelu_ready, act_ready, diag_ready, v_used = (
            sem("picked"), sem("dots"), sem("gelu_ready"), sem("act_ready"), sem("diag_ready"), sem("v_used"))
        exp_ready, sum_read, var_ready, std_ready, y_ready, y_stored, y_free = (
            sem("exp_ready"), sem("sum_read"), sem("ep_var"), sem("ep_std"), sem("ep_y"), sem("ep_y_stored"), sem("y_free"))
        waited_pool, waited_dve, waited_pe, waited_sp = (sem(f"waited_{e}") for e in ("pool", "dve", "pe", "sp"))
        state_turned, state_out, state_stored, h1_stored = sem("state_turned"), sem("state_out"), sem("state_stored"), sem("h1_stored")
        sample_ready = sem("sample_ready")
        state_loaded, vecs_loaded, rows_stored, samp_stored = (
            sem("samp_state_loaded"), sem("samp_vecs_loaded"), sem("samp_rows_stored"), sem("samp_stored"))
        samp_turned, samp_copied, samp_chain = sem("samp_turned"), sem("samp_copied"), sem("samp_chain")
        SAMP_STEPS = 20
        conv_w_loaded = [sem(f"conv_w_loaded{i}") for i in range(N_CONV_W)]
        conv_done, conv_read, cg_ready, conv_chain, conv_y_ready = (
            sem("conv_done"), sem("conv_read"), sem("cg_ready"), sem("conv_chain"), sem("conv_y_ready"))
        conv_stored = [sem("conv_stored0"), sem("conv_stored1")]
        samp_diff, samp_exp, samp_picked, samp_idx_stored, samp_idx_loaded, x_samp_loaded = (
            sem("samp_diff"), sem("samp_exp"), sem("samp_picked"), sem("samp_idx_stored"), sem("samp_idx_loaded"), sem("x_samp_loaded"))
        samp_gelu, samp_var, samp_std, y_samp_ready, y_samp_stored, samp_end = (
            sem("samp_gelu"), sem("samp_var"), sem("samp_std"), sem("y_samp_ready"), sem("y_samp_stored"), sem("samp_end"))

        HALVES = [["U", "N", "BT", "U2", "N2", "KA", "R1", "U4", "Q1", "N4", "KT", "R2", "U8", "Q2", "N8"],
                  ["VT", "R3", "Q3", "BR", "MT", "M", "KR", "M2", "Z1", "X", "Z", "SA", "S", "O"]]
        PRODUCTS = HALVES[0] + HALVES[1]
        products = Stages(sem("wkv_products"), PRODUCTS)
        copies = Stages(sem("wkv_copies"), ["be_t", "u2", "n2", "u4", "n4", "ka_t", "u8", "n8", "v_t", "mt", "m", "m2", "xx", "sa", "o"])
        vectors = Stages(sem("wkv_vectors"), ["ud", "r", "nd", "q", "ue", "g_ka", "r1", "q1", "r2", "q2", "r3", "q3", "g_br", "g_kr",
                                              "z1", "z", "s_sum", "s"])
        reader = {"U": (vectors, "ue"), "N": (vectors, "nd"), "BT": (copies, "be_t"), "U2": (copies, "u2"), "N2": (copies, "n2"),
                  "KA": (vectors, "g_ka"), "R1": (vectors, "r1"), "U4": (copies, "u4"), "Q1": (vectors, "q1"), "N4": (copies, "n4"),
                  "KT": (copies, "ka_t"), "R2": (vectors, "r2"), "U8": (copies, "u8"), "Q2": (vectors, "q2"), "N8": (copies, "n8"),
                  "VT": (copies, "v_t"), "R3": (vectors, "r3"), "Q3": (vectors, "q3"), "BR": (vectors, "g_br"), "MT": (copies, "mt"),
                  "M": (copies, "m"), "KR": (vectors, "g_kr"), "M2": (copies, "m2"), "Z1": (vectors, "z1"), "Z": (vectors, "z"),
                  "X": (copies, "xx"), "SA": (copies, "sa"), "S": (vectors, "s_sum"), "O": (copies, "o")}
        front_pe = Stages(sem("front_pe"), ["mean", "bonus", "gate", "var", "mix", "turned"]
                          + [n for j in range(HP) for n in (f"q{j}", f"s{j}")])
        front_act = Stages(sem("front_act"), ["square", "gn_std", "ln_std", "h1T"] + [f"q{j}" for j in range(HP)])
        front_dve = Stages(sem("front_dve"), ["rk0", "rk", "centred", "bonus", "var", "inv", "scaled", "gain", "offset", "plus", "y",
                                              "sum", "bn0", "bn1", "aggr", "ln_var", "ln_inv", "ln_x", "ln_g", "h1"]
                           + [f"{n}{j}" for j in range(HP) for n in ("max", "place", "others", "max2_", "place2_", "top")])

        def ps(name):
            i = PRODUCTS.index(name) % 6
            return (bank[i] if i < 4 else wide_ps[:, i - 4])[:, 0:PAIRS * CHUNK].rearrange("p (c n) -> p c n", c=PAIRS)

        def score_ps(j):
            return (wide_ps[:, 0], wide_ps[:, 1], bank[0], bank[1])[j % 4]

        SCORE_SLOTS = [1 + (2 * TOPK - 4) * j // (HP - 1) for j in range(HP)]
        assert SCORE_SLOTS[-1] + 1 < 2 * TOPK

        def queries(n, s, back=0):
            return [j for j in range(HP) if SCORE_SLOTS[j] == (n - 6) * TOPK + s - back]

        def over_turns(eng, a_turn, finish):
            a_turn(0, 0, None, sums=False)
            with eng.Fori(0, TBLOCKS - 1) as b:
                for n in range(1, H):
                    a_turn(b * H + n, n, b + 1)
                a_turn(b * H + H, 0, None, new_block=b + 1)
                finish(b)
            for n in range(1, H):
                a_turn((TBLOCKS - 1) * H + n, n, TBLOCKS)
            a_turn(TBLOCKS * H, 0, None, dots_left=False)
            finish(TBLOCKS - 1)

        def unit_of(u):
            return u // 9, u % 9 // 3, KINDS[u % 3]

        def conv_tile(u):
            return u // 9 * 3 + u % 3

        def before_turns(chunk_step, conv_slot, slot):
            n = 0
            for name in PRODUCTS:
                chunk_step(0, name, CHUNK)
                conv_slot(n)
                n += 1
            for turn in range(1, 5):
                for s in range(TOPK):
                    slot(0, turn, s)
                    conv_slot(n)
                    n += 1
            assert n > CONV_SLOTS

        def conv_first(n):
            return min(n, CONV_SLOTS) * UNITS * KT // CONV_SLOTS

        def finished_unit(n):
            unit = conv_first(n + 1) // KT - 1
            return unit if (unit + 1) * KT > conv_first(n) else None

        HEAD_SCORED = [SCORE_SLOTS[1] + 2, SCORE_SLOTS[3] + 2]

        def front_to_head_0(slot):
            for s in range(TOPK):
                slot(0, 5, s)
            for s in range(HEAD_SCORED[0]):
                slot(0, 6, s)

        def front_to_head_1(slot):
            for s in range(*HEAD_SCORED):
                slot(0, 6, s)

        def front_rest(slot, s):
            left = 2 * TOPK - HEAD_SCORED[1]
            for i in range(s * left // TOPK, (s + 1) * left // TOPK):
                i += HEAD_SCORED[1]
                slot(0, 6 + i // TOPK, i % TOPK)

        def rows_and_stage(nb, n):
            if isinstance(nb, int) and nb == TBLOCKS:
                return NS, n if n == 1 else n + 3
            return P, n

        def chunk_slot(nb, n, s):
            names = HALVES[(n - 1) % 2]
            return nb * 2 + 1 + (n - 1) // 2, names[s] if s < len(names) else None, (n - 1) // 2 * CHUNK

        block = ctx.enter_context(nc.Block())

        @block.sync
        def _(sp):
            def load_ops(c0, dst, n):
                for j in range(5):
                    sp.dma_start(ops[:, j, :, dst:dst + n], d["operands"][j][:, :, bass.ds(c0, n)]).then_inc(ops_loaded, 16)

            def load_yc(nb):
                sp.dma_start(yc[:, :, :], d["y_conv"][:, :, bass.ds(nb * P + C_PROMPT, P)]).then_inc(ops_loaded, 16)

            def load_lora(nb):
                sp.dma_start(lora[:, :], d["lora_g"][:, bass.ds(nb * P + C_PROMPT, P)]).then_inc(ops_loaded, 16)

            def load_block(nb):
                load_ops(nb * P + 2 * WKV_OFF, 0, P)
                load_lora(nb)
                load_yc(nb)

            def load_conv_w(n):
                if n >= N_CONV_W:
                    old = n - N_CONV_W
                    sp.wait_ge(conv_done, old // 3 * 9 + 6 + old % 3 + 1)
                c0 = (1, 2, 0)[n % 3] * CONVW + n // 3 * P
                sp.dma_start(conv_w[:, n % N_CONV_W, :, :],
                             d["w_in"][0, :, c0:c0 + P].rearrange("(k p) c -> p k c", p=P)).then_inc(conv_w_loaded[n % N_CONV_W], 16)

            def load_wq(nb):
                for j in range(HP):
                    sp.wait_ge(front_pe.sem, front_pe.value(nb, f"q{j - NW}" if j >= NW else (f"q{j + HP - NW}", 1)))
                    sp.sem_inc(waited_sp, 1)
                    sp.dma_start(w_q[:, j % NW, :, :], d["w_q"][0, :, j * P:(j + 1) * P].rearrange("(k p) c -> p k c", p=P)).then_inc(wq_loaded[j % NW], 16)

            def load_h(nb):
                sp.dma_start(h[:, :], d["h_rows"][bass.ds(nb * P + C_PROMPT, P), :]).then_inc(h_loaded, 16)

            load_ops(0, CHUNK, CHUNK)
            load_ops(2 * WKV_OFF, 0, CHUNK)
            load_lora(0)
            for n in range(N_CONV_W):
                load_conv_w(n)
            load_h(0)
            sp.dma_start(samp_state, d["state_wkv"][0].rearrange("b h v k -> (b h) v k")).then_inc(state_loaded, 16)
            sp.wait_ge(samp_copied, 2)
            for j in range(6):
                sp.dma_start(d["samp_rows"][:, :, j, :],
                             samp_rows[(j % 3) * 32:(j % 3) * 32 + 32, j // 3, :].rearrange("p (h k) -> p h k", h=2)).then_inc(rows_stored, 16)
            sp.dma_start(g_up[:, :], d["g_up"][0]).then_inc(const_loaded, 16)
            for j, n in enumerate(("ln1_g", "ln1_b")):
                sp.dma_start(ln1_gb[:, j, :], d[n][0:1, :].broadcast_to([P, D])).then_inc(const_loaded, 16)
            for j, n in enumerate(("ln2_g", "ln2_b")):
                sp.dma_start(ln2_gb[:, j, :], d[n][0:1, :].broadcast_to([P, D])).then_inc(const_loaded, 16)
            sp.wait_ge(rows_stored, 96)
            sp.dma_start(samp_vecs, d["samp_rows"].rearrange("a h j k -> (a h) j k")).then_inc(vecs_loaded, 16)
            sp.dma_start(d["new_shift_prompt"][0], d["h_rows"][PROJ_COLS - 1:PROJ_COLS, :]).then_inc(samp_stored, 16)
            sp.dma_start(d["new_shift_sample"][0], d["h_rows"][0:NS, :]).then_inc(samp_stored, 16)
            sp.dma_start(d["new_conv_sample"][0, :, 0, :], d["state_conv"][0, :, 1, :]).then_inc(samp_stored, 16)
            for n in range(N_CONV_W, 8):
                load_conv_w(n)
            sp.wait_ge(products.sem, products.value(0, "O"))
            sp.wait_ge(ops_loaded, 176)
            load_ops(2 * WKV_OFF + CHUNK, CHUNK, CHUNK)
            sp.wait_ge(samp_chain, SAMP_STEPS)
            sp.wait_ge(t.samp_state_stored, 16)
            for kt in range(KT):
                sp.dma_start(w_o[:, kt, :], d["w_o"][0, kt * P:(kt + 1) * P, :]).then_inc(const_loaded, 16)
            for n in range(8, 3 * PAIRS):
                load_conv_w(n)
            for stored in conv_stored:
                sp.wait_ge(stored, 16 * 3 * PAIRS // 2)
            load_yc(0)
            sp.wait_ge(samp_copied, 3)
            sp.dma_start(d["new_conv_sample"][0, :, 1, :], z_rows[0:NS, :]).then_inc(samp_stored, 16)
            sp.dma_start(d["new_conv_prompt"][0, 0], z_rows[NS:NS + 2, :]).then_inc(samp_stored, 16)
            load_wq(0)
            sp.wait_ge(samp_stored, 80)
            sp.sem_inc(y_free, 1)

            def after_norm(nb):
                sp.wait_ge(front_dve.sem, front_dve.value(nb, "y"))
                sp.sem_inc(waited_sp, 1)
                sp.wait_ge(front_pe.sem, front_pe.value(nb, "mix"))
                sp.sem_inc(waited_sp, 1)

            def store_y(b):
                sp.wait_ge(y_ready, b + 1)
                sp.sem_inc(waited_sp, 1)
                sp.dma_start(d["y_prompt"][0, bass.ds(b * P, P), :], y[:, :]).then_inc(y_stored, 16)
                sp.wait_ge(y_stored, b * 16 + 16)
                sp.sem_inc(waited_sp, 1)
                sp.sem_inc(y_free, 1)

            after_norm(0)
            load_block(1)
            sp.wait_ge(x_taken, 1)
            load_h(1)
            with sp.Fori(0, TBLOCKS - 2) as b:
                load_wq(b + 1)
                after_norm(b + 1)
                load_block(b + 2)
                sp.wait_ge(x_taken, b + 2)
                sp.sem_inc(waited_sp, 1)
                load_h(b + 2)
                store_y(b)
            load_wq(TBLOCKS - 1)
            after_norm(TBLOCKS - 1)
            sp.dma_start(yc[:, :, 0:NS], d["y_conv"][:, :, 0:NS]).then_inc(ops_loaded, 16)
            sp.dma_start(lora[:, 0:NS], d["lora_g"][:, 0:NS]).then_inc(ops_loaded, 16)
            sp.wait_ge(x_taken, TBLOCKS)
            sp.dma_start(h[0:NS, :], d["h_rows"][0:NS, :]).then_inc(h_loaded, 16)
            store_y(TBLOCKS - 2)
            sp.wait_ge(state_out, 1)
            for c in range(PAIRS):
                sp.dma_start(d["new_wkv_prompt"][0, 0, 2 * c:2 * c + 2].rearrange("h v k -> (h v) k"), s_out[:, c, :]).then_inc(state_stored, 16)
            load_wq(TBLOCKS)
            sp.wait_ge(front_dve.sem, front_dve.value(TBLOCKS, "h1"))
            sp.dma_start(d["h1_rows"], h[0:NS, :]).then_inc(h1_stored, 16)
            sp.wait_ge(h1_stored, 16)
            for b in range(NS):
                sp.dma_start(x_samp[b * PER:(b + 1) * PER, :], d["h1_rows"][b:b + 1, :].broadcast_to([PER, D])).then_inc(x_samp_loaded, 16)
            sp.wait_ge(samp_picked, 2)
            sp.dma_start(d["sp_idx"], samp_expert[:, :, :].rearrange("p a b -> p (a b)")).then_inc(samp_idx_stored, 16)
            sp.dma_start(d["sp_gate"], ops[0:NS, 1, 1, :]).then_inc(samp_idx_stored, 16)
            sp.wait_ge(samp_idx_stored, 32)
            sp.dma_start(samp_idx[:, :], d["sp_idx"].rearrange("b (s e) -> (b s) e", e=EACH)).then_inc(samp_idx_loaded, 16)
            sp.dma_start(samp_gate[:, :], d["sp_gate"].rearrange("b (s e) -> (b s) e", e=EACH)).then_inc(samp_idx_loaded, 16)
            store_y(TBLOCKS - 1)
            sp.wait_ge(y_samp_ready, 1)
            sp.dma_start(d["y_sample"][:, 0, :], y_samp).then_inc(y_samp_stored, 16)
            sp.wait_ge(y_samp_stored, 16)
            sp.wait_ge(state_stored, 16 * PAIRS)

        @block.gpsimd
        def _(pool):
            done = signals(pool)
            n_consts = [0]

            def const(ins):
                n_consts[0] += 1
                done(ins, consts)

            def select(m, op, base, pattern, fill, row=1):
                for head in range(2):
                    const(pool.affine_select(out=m[head * HD:(head + 1) * HD], in_=m[head * HD:(head + 1) * HD], compare_op=op,
                                             fill=fill, base=base, pattern=pattern, channel_multiplier=row))

            const(pool.memset(eye[:, :], 0.0))
            select(eye[:, :], ALU.not_equal, 0, [[-1, CHUNK]], 1.0)
            for m in (upper, upper_eq, upper_in, lower_in):
                const(pool.memset(m[:, :], 1.0))
            select(upper[:, :], ALU.is_gt, 0, [[1, CHUNK]], 0.0, -1)
            select(upper_eq[:, :], ALU.is_ge, 0, [[1, CHUNK]], 0.0, -1)
            for m in (upper_in, lower_in):
                select(m[:, :].rearrange("p (a b) -> p a b", b=16), ALU.is_ge, 0, [[-16, 4], [0, 16]], 0.0)
                select(m[:, :].rearrange("p (a b) -> p a b", b=16), ALU.is_gt, 16, [[16, 4], [0, 16]], 0.0, -1)
            select(lower_in[:, :], ALU.is_gt, 0, [[-1, CHUNK]], 0.0)
            select(upper_in[:, :], ALU.is_gt, 0, [[1, CHUNK]], 0.0, -1)
            const(pool.tensor_tensor(upper_out[:, :], upper[:, :], upper_in[:, :], ALU.subtract))
            const(pool.iota(k.iota[:, :], [[1, TOPK]], base=0, channel_multiplier=0, allow_small_or_imprecise_dtypes=True))
            const(pool.memset(by_token[:, :], 1.0))
            const(pool.affine_select(out=by_token[:, :], in_=by_token[:, :], compare_op=ALU.is_ge, fill=0.0, base=0,
                                     pattern=[[-PER, NS]], channel_multiplier=1))
            const(pool.affine_select(out=by_token[:, :], in_=by_token[:, :], compare_op=ALU.is_gt, fill=0.0, base=PER,
                                     pattern=[[PER, NS]], channel_multiplier=-1))
            assert n_consts[0] == N_CONSTS, n_consts

            step = lambda ins: done(ins, samp_chain)
            state, term = samp_state, samp_term
            along_k = lambda x: x.unsqueeze(1).broadcast_to([BH, HD, HD])
            along_v = lambda x: x.unsqueeze(2).broadcast_to([BH, HD, HD])

            def sum_over_keys(out):
                width = HD // 2
                while width > 1:
                    step(pool.tensor_tensor(term[:, :, 0:width], term[:, :, 0:width], term[:, :, width:2 * width], ALU.add))
                    width //= 2
                step(pool.tensor_tensor(out.unsqueeze(2), term[:, :, 0:1], term[:, :, 1:2], ALU.add))

            pool.wait_ge(state_loaded, 16)
            pool.wait_ge(vecs_loaded, 16)
            r, k_, v_, kk, kka, w = (samp_vecs[:, j, :] for j in range(6))
            step(pool.tensor_tensor(term, state, along_k(kk), ALU.mult))
            sum_over_keys(samp_sa)
            step(pool.tensor_tensor(state, state, along_k(w), ALU.mult))
            step(pool.tensor_tensor(term, along_v(samp_sa), along_k(kka), ALU.mult))
            step(pool.tensor_tensor(state, state, term, ALU.subtract))
            step(pool.tensor_tensor(term, along_v(v_), along_k(k_), ALU.mult))
            step(pool.tensor_tensor(state, state, term, ALU.add))
            pool.dma_start(d["new_wkv_sample"][0].rearrange("b h v k -> (b h) v k"), state).then_inc(t.samp_state_stored, 16)
            step(pool.tensor_tensor(term, state, along_k(r), ALU.mult))
            sum_over_keys(samp_o[:, 0, :])
            step(pool.tensor_copy(samp_o[:, 1, :], samp_o[:, 0, :]))
            pool.wait_ge(t.samp_state_stored, 16)
            pool.wait_ge(picked, 1)
            for s in range(RING):
                gather(pool, u[:, s, :], d["peer_u"][0], idx[:, 0, s:s + 1]).then_inc(u_landed[s], 16)

            def a_turn(turn, n, nb, sums=True, dots_left=True, new_block=None):
                last = n == H - 1 and isinstance(turn, int)
                for s in range(TOPK):
                    own = s + RING < TOPK
                    row = (s + RING) % TOPK
                    if dots_left:
                        if row == 0 and not last:
                            pool.wait_ge(picked, turn + 2)
                        elif row == 0:
                            pool.wait_ge(samp_idx_loaded, 32)
                        pool.wait_ge(dots, turn * TOPK + s + 1)
                        pool.sem_inc(waited_pool, 1)
                        index = samp_idx[:, row:row + 1] if last and not own else idx[:, (n if own else n + 1) % 4, row:row + 1]
                        gather(pool, u[:, s % RING, :], d["peer_u"][0], index).then_inc(u_landed[s % RING], 16)
                    if sums or not own:
                        pool.wait_ge(v_used, turn * TOPK + s - RING + 1)
                        pool.sem_inc(waited_pool, 1)
                        index = idx[:, (n - 1 if own else n) % 4, row:row + 1] if own or dots_left else samp_idx[:, row:row + 1]
                        gather(pool, v[:, s % RING, :], d["peer_v"][0], index).then_inc(v_landed[s % RING], 16)
            over_turns(pool, a_turn, lambda b: None)

        @block.tensor
        def _(pe):
            def chunk_step(ci, name, dst):
                al, be, ka, rh, vt = (x[:, :, dst:dst + CHUNK] for x in (al2, be2, ka2, rh2, vt2))

                def product(name, pairs, V=(), A=()):
                    i = PRODUCTS.index(name)
                    stages, step = reader[PRODUCTS[i - 6] if i >= 6 else PRODUCTS[i + 6 * ((len(PRODUCTS) - 1 - i) // 6)]]
                    bank_read = (step, 0 if i >= 6 else 1)
                    V = list(V) + ([bank_read] if stages is vectors else [])
                    A = list(A) + ([bank_read] if stages is copies else [])
                    if V:
                        pe.wait_ge(vectors.sem, vectors.value(ci, *V))
                    if A:
                        pe.wait_ge(copies.sem, copies.value(ci, *A))
                    pe.sem_inc(waited_pe, 1)
                    for c in range(PAIRS):
                        for head in range(2):
                            rows = slice(head * HD, (head + 1) * HD)
                            for n, (a, b) in enumerate(pairs):
                                last = pe.matmul(ps(name)[rows, c, :], a[rows, c, :], b[rows, :] if b is eye else b[rows, c, :],
                                                 start=(n == 0), stop=(n == len(pairs) - 1))
                    last.then_inc(products.at(name), 1)

                operands, V, A = {
                    "U": ([(be, al)], [], []), "N": ([(al, be)], [], []), "BT": ([(be, eye)], [], []),
                    "U2": ([(nd, ud)], ["nd"], []), "N2": ([(ud, nd)], [], []), "KA": ([(ka, al)], [], []),
                    "R1": ([(n2, r_)], ["q"], ["n2"]), "U4": ([(n2, u2)], [], []), "Q1": ([(u2, q_)], [], []),
                    "N4": ([(u2, n2)], [], []), "KT": ([(ka, eye)], [], []), "R2": ([(n4, r_)], ["r1"], ["n4"]),
                    "U8": ([(n4, u4)], [], []), "Q2": ([(u4, q_)], ["q1"], []), "N8": ([(u4, n4)], [], []),
                    "VT": ([(vt, eye)], [], []), "R3": ([(n8, r_)], ["r2"], ["n8"]), "Q3": ([(u8, q_)], ["q2"], []),
                    "BR": ([(be, rh)], [], []), "MT": ([(q_, ue)], ["q3"], []), "M": ([(ue, q_)], [], []),
                    "KR": ([(ka, rh)], [], []), "M2": ([(mt, m_)], [], ["m"]), "Z1": ([(m_, r_)], [], []),
                    "X": ([(al, st), (g_ka, v_t)], [("s", 1)], []), "Z": ([(m2, r_)], ["z1"], ["m2"]),
                    "SA": ([(r_, xx)], ["z"], ["xx"]), "S": ([(be_t, sa), (ka_t, v_t)], [], ["sa"]),
                    "O": ([(st, rh), (sa, g_br), (v_t, g_kr)], [], [])}[name]
                product(name, operands, V, A)

            def norm_slot(nb, s, rows):
                if s == 0:
                    if rows == P:
                        pe.wait_ge(copies.sem, copies.value(nb * 2 + 2, "o"))
                        pe.wait_ge(vectors.sem, vectors.value(nb * 2 + 2, "s"))
                    pe.wait_ge(front_dve.sem, front_dve.value(nb, "rk"))
                    pe.sem_inc(waited_pe, 1)
                    pe.matmul(bank[0][:, :], t.head_ones[:, :], flat(o), start=True, stop=True).then_inc(front_pe.at("mean"), 1)
                elif s == 1:
                    pe.matmul(bank[1][:, :], t.head_ones[:, :], flat(rk), start=True, stop=True).then_inc(front_pe.at("bonus"), 1)
                elif s == 2:
                    if isinstance(nb, int) and nb == 0:
                        pe.wait_ge(const_loaded, 16 * (KT + 5))
                        pe.wait_ge(ops_loaded, 160 + 112)
                        pe.wait_ge(samp_copied, 3)
                    for c in range(PAIRS):
                        last = pe.matmul(bank[2][:, c * P:(c + 1) * P], g_up[:, c * P:(c + 1) * P], lora[:, :], start=True, stop=True)
                    last.then_inc(front_pe.at("gate"), 1)
                elif s == 3:
                    pe.wait_ge(front_act.sem, front_act.value(nb, "square"))
                    pe.sem_inc(waited_pe, 1)
                    pe.matmul(bank[3][:, :], t.head_ones[:, :], flat(square), start=True, stop=True).then_inc(front_pe.at("var"), 1)
                elif s - 4 < KT:
                    kt = s - 4
                    if kt == PAIRS:
                        pe.wait_ge(front_dve.sem, front_dve.value(nb, "y"))
                        pe.sem_inc(waited_pe, 1)
                    y_in = yc[:, kt, :] if kt < PAIRS else o[:, kt - PAIRS, :]
                    for half in range(2):
                        last = pe.matmul(wide_ps[0:rows, half, :], y_in[:, 0:rows], w_o[:, kt, half * 512:(half + 1) * 512],
                                         start=(kt == 0), stop=(kt == KT - 1))
                    if kt == KT - 1:
                        last.then_inc(front_pe.at("mix"), 1)

            def turn_h1(nb, rows):
                pe.wait_ge(front_dve.sem, front_dve.value(nb, "h1"))
                pe.sem_inc(waited_pe, 1)
                for kt in range(KT):
                    last = pe.transpose(bank[kt // 4][:, (kt % 4) * P:(kt % 4) * P + rows], h[0:rows, kt * P:(kt + 1) * P],
                                        t.ident[0:rows, 0:rows])
                last.then_inc(front_pe.at("turned"), 1)

            def query(nb, j, rows):
                pe.wait_ge(wq_loaded[j % NW], (nb * (HP // NW) + j // NW + 1) * 16)
                pe.wait_ge(front_act.sem, front_act.value(nb, f"q{j - 2}" if j >= 2 else "h1T"))
                pe.sem_inc(waited_pe, 1)
                for kt in range(KT):
                    last = pe.matmul(bank[2 + j % 2][:, 0:rows], w_q[:, j % NW, kt, :], h1T[:, kt, 0:rows],
                                     start=(kt == 0), stop=(kt == KT - 1))
                last.then_inc(front_pe.at(f"q{j}"), 1)

            def key_scores(nb, j, rows):
                pe.wait_ge(front_act.sem, front_act.value(nb, f"q{j}"))
                if j >= 4:
                    pe.wait_ge(front_dve.sem, front_dve.value(nb, f"others{j - 4}"))
                pe.sem_inc(waited_pe, 1)
                pe.matmul(score_ps(j)[0:rows, 0:N_KEYS], q[:, j % 2, 0:rows], t.keysT[:, j, :],
                          start=True, stop=True).then_inc(front_pe.at(f"s{j}"), 1)

            def front_slot(nb, n, s):
                rows, n = rows_and_stage(nb, n)
                if n <= 4 and rows == P:
                    if n == 1 and s == 0:
                        if not (isinstance(nb, int) and nb == 0):
                            pe.wait_ge(ops_loaded, nb * 112 + 160 + 112)
                        pe.wait_ge(front_dve.sem, front_dve.value(nb, (f"top{HP - 1}", 1)))
                        pe.sem_inc(waited_pe, 1)
                    if n == 3 and s == 0 and isinstance(nb, int) and nb == 0:
                        pe.wait_ge(ops_loaded, 176 + 80)
                    ci, name, dst = chunk_slot(nb, n, s)
                    if name:
                        chunk_step(ci, name, dst)
                elif (n, s) == (1, 0):
                    pe.wait_ge(front_dve.sem, front_dve.value(nb, (f"top{HP - 1}", 1)))
                    for c in range(PAIRS):
                        for head in range(2):
                            r = slice(head * HD, (head + 1) * HD)
                            last = pe.matmul(bank[0][r, c * HD:(c + 1) * HD], st[r, c, :], eye[r, :], start=True, stop=True)
                    last.then_inc(state_turned, 1)
                    pe.wait_ge(samp_chain, SAMP_STEPS)
                    pe.matmul(bank[1][:, 0:BH], samp_o[:, :, :].rearrange("p a b -> p (a b)"), t.ident[0:BH, 0:BH],
                              start=True, stop=True).then_inc(samp_turned, 1)
                elif n == 5:
                    if rows == NS and s == 0:
                        pe.wait_ge(ops_loaded, TBLOCKS * 112 + 160 + 32)
                        pe.wait_ge(state_out, 1)
                        pe.wait_ge(samp_copied, 5)
                    norm_slot(nb, s, rows)
                elif n in (6, 7):
                    if (n, s) == (6, 0):
                        turn_h1(nb, rows)
                    for j in queries(n, s, 1):
                        key_scores(nb, j, rows)
                    for j in queries(n, s):
                        query(nb, j, rows)

            def a_turn(turn, n, nb, sums=True, dots_left=True, new_block=None):
                head = (n - 1) % H
                for s in range(TOPK):
                    if sums:
                        if n == 1 and s == 0:
                            pe.wait_ge(sum_read, nb)
                        pe.wait_ge(v_landed[s % RING], (turn * 2 + s // RING - 1) * 16)
                        pe.wait_ge(diag_ready, (turn - 1) * TOPK + s + 1)
                        for half in range(2):
                            mm = pe.matmul(out_ps[:, half, :], diag[:, s % RING, :], v[:, s % RING, half * 512:(half + 1) * 512],
                                           start=head == 0 and s == 0, stop=head == H - 1 and s == TOPK - 1)
                        mm.then_inc(v_used, 1)
                    if nb is not None:
                        front_slot(nb, n, s)
                    elif n == 0 and isinstance(turn, int) and turn == 0:
                        front_rest(front_slot, s)
                if not dots_left:
                    pe.wait_ge(front_dve.sem, front_dve.value(TBLOCKS, f"top{HP - 1}"))
                    for e in range(EACH):
                        pe.wait_ge(v_landed[e], (turn * 2 + 1) * 16)
                        pe.wait_ge(diag_ready, turn * TOPK + e + 1)
                        for half in range(2):
                            mm = pe.matmul(wide_ps[0:NS, half, :], diag[:, e, 0:NS], v[:, e, half * 512:(half + 1) * 512],
                                           start=e == 0, stop=e == EACH - 1)
                        mm.then_inc(v_used, 1)

            front_pe.start(pe)
            products.start(pe)
            samp = t.samp[:, :, :, :].rearrange("p j b c -> p (j b c)")
            for half in range(2):
                pe.transpose(bank[half][0:R, 0:P], samp[:, half * R:(half + 1) * R], t.ident[:, :]).then_inc(samp_turned, 1)
            pe.sem_inc(v_used, RING)
            pe.sem_inc(sum_read, 1)
            pe.wait_ge(consts, N_CONSTS)
            pe.wait_ge(ops_loaded, 176)
            pe.wait_ge(samp_copied, 2)

            def conv_slot(n):
                for m in range(conv_first(n), conv_first(n + 1)):
                    unit, kt = m // KT, m % KT
                    _, third, _ = unit_of(unit)
                    w = conv_tile(unit)
                    if kt == 0:
                        if third == 0:
                            pe.wait_ge(conv_w_loaded[w % N_CONV_W], 16 * (w // N_CONV_W + 1))
                        if unit >= 2:
                            i, kind = (unit - 2) // 3, (unit - 2) % 3
                            if kind == 0:
                                pe.wait_ge(cg_ready, i + 1)
                            else:
                                pe.wait_ge(conv_read, 2 * i + kind)
                    mm = pe.matmul(out_ps[:, unit % 2, 0:COLS3], conv_w[:, w % N_CONV_W, kt, :],
                                   t.hT[:, kt, third * COLS3:(third + 1) * COLS3], start=kt == 0, stop=kt == KT - 1)
                    if kt == KT - 1:
                        mm.then_inc(conv_done, 1)

            before_turns(chunk_step, conv_slot, front_slot)
            pe.wait_ge(conv_chain, CONV_STEPS)
            pe.wait_ge(copies.sem, copies.value(2, "o"))
            pe.wait_ge(vectors.sem, vectors.value(2, "s"))
            for c in range(PAIRS):
                last = pe.transpose(bank[2][0:NS + 2, c * P:(c + 1) * P], t.z_out[:, c, :], t.ident[:, :])
            last.then_inc(samp_turned, 1)
            front_to_head_0(front_slot)
            front_to_head_1(front_slot)
            over_turns(pe, a_turn, lambda b: None)

        @block.scalar
        def _(act):
            def chunk_step(ci, name, dst):
                copied = {"BT": be_t, "U2": u2, "N2": n2, "U4": u4, "N4": n4, "KT": ka_t, "U8": u8, "N8": n8, "VT": v_t, "MT": mt,
                          "M": m_, "M2": m2, "X": xx, "SA": sa, "O": o[:, :, dst:dst + CHUNK]}
                if name in copied:
                    act.wait_ge(products.sem, products.value(ci, name))
                    act.activation(copied[name][:, :, :], ps(name), ACT.Copy).then_inc(copies.at(reader[name][1]), 1)

            def front_slot(nb, n, s):
                rows, n = rows_and_stage(nb, n)
                if n <= 4 and rows == P:
                    chunk_step(*chunk_slot(nb, n, s))
                elif (n, s) == (1, 0):
                    act.wait_ge(state_turned, 1)
                    act.activation(flat(s_out), bank[0][:, 0:PAIRS * HD], ACT.Copy).then_inc(state_out, 1)
                    act.wait_ge(samp_turned, 4)
                    for hd in range(2):
                        r = slice(hd * HD, (hd + 1) * HD)
                        src = bank[1][r, 0:BH].rearrange("p (b c h) -> p h c b", b=NS, c=PAIRS)[:, hd]
                        act.activation(o[r, :, 0:NS], src, ACT.Copy).then_inc(samp_copied, 1)
                elif (n, s) == (5, 2):
                    act.wait_ge(front_dve.sem, front_dve.value(nb, "centred"))
                    act.activation(flat(square), flat(o), ACT.Square).then_inc(front_act.at("square"), 1)
                elif (n, s) == (5, 4):
                    act.wait_ge(front_dve.sem, front_dve.value(nb, "var"))
                    act.activation(flat(gn_std), flat(gn_std), ACT.Sqrt).then_inc(front_act.at("gn_std"), 1)
                elif (n, s) == (5, 14):
                    act.wait_ge(front_dve.sem, front_dve.value(nb, "ln_var"))
                    act.activation(rs1[0:rows, :], rs1[0:rows, :], ACT.Sqrt).then_inc(front_act.at("ln_std"), 1)
                elif (n, s) == (6, 0):
                    act.wait_ge(front_pe.sem, front_pe.value(nb, "turned"))
                    for half in range(2):
                        ins = act.activation(h1T[:, 4 * half:4 * half + 4, 0:rows],
                                             bank[half][:, :].rearrange("p (k n) -> p k n", k=4)[:, :, 0:rows], ACT.Copy)
                    ins.then_inc(front_act.at("h1T"), 1)
                elif n in (6, 7):
                    for j in queries(n, s):
                        act.wait_ge(front_pe.sem, front_pe.value(nb, f"q{j}"))
                        act.activation(q[:, j % 2, 0:rows], bank[2 + j % 2][:, 0:rows], ACT.Copy).then_inc(front_act.at(f"q{j}"), 1)
                elif (n, s) == (10, 4):
                    act.wait_ge(samp_diff, 1)
                    act.activation(samp_ex, samp_ex, ACT.Exp).then_inc(samp_exp, 1)

            def exp_of(turn, par):
                act.wait_ge(picked, turn + 1)
                act.activation(ex[:, par, :], best[:, par, :], ACT.Exp, bias=neg_max[:, par, :], accum_out=total[:, par, :]).then_inc(exp_ready, 1)

            def a_turn(turn, n, nb, sums=True, dots_left=True, new_block=None):
                par = n % 2
                last = n == H - 1 and isinstance(turn, int)
                for s in range(TOPK):
                    if sums:
                        if s == 0:
                            act.wait_ge(act_ready, turn)
                        act.wait_ge(v_used, (turn - 1) * TOPK + s + 1)
                        act.activation(diag[:, s % RING, :], t.ident[:, :], ACT.Copy, scale=act_v[:, 1 - par, s:s + 1]).then_inc(diag_ready, 1)
                    if s == 12 and not dots_left:
                        act.wait_ge(dots, turn * TOPK + EACH)
                        act.activation(samp_hu[:, :], samp_hu[:, :], ACT.Gelu).then_inc(samp_gelu, 1)
                    if s == 4 and dots_left and not last:
                        exp_of(turn + 1, 1 - par)
                    if nb is not None:
                        front_slot(nb, n, s)
                    elif n == 0 and isinstance(turn, int) and turn == 0:
                        front_rest(front_slot, s)
                if dots_left:
                    act.wait_ge(dots, (turn + 1) * TOPK)
                    act.activation(act_v[:, par, :], hu[:, par, :], ACT.Gelu).then_inc(gelu_ready, 1)
                else:
                    act.wait_ge(act_ready, turn + 1)
                    for e in range(EACH):
                        act.wait_ge(v_used, turn * TOPK + e + 1)
                        act.activation(diag[:, e, 0:NS], by_token[:, :], ACT.Copy, scale=samp_hu[:, e:e + 1]).then_inc(diag_ready, 1)

            def finish(b):
                act.wait_ge(var_ready, b + 1)
                act.activation(rstd[:, :], rstd[:, :], ACT.Sqrt).then_inc(std_ready, 1)

            copies.start(act)
            front_act.start(act)
            for half in range(2):
                act.wait_ge(samp_turned, half + 1)
                act.activation(samp_rows[:, half, :], bank[half][0:R, 0:P], ACT.Copy).then_inc(samp_copied, 1)

            def conv_slot(n):
                unit = finished_unit(n)
                if unit is not None:
                    c, third, kind = unit_of(unit)
                    i = unit // 3
                    if kind == "cg":
                        if i >= 2:
                            act.wait_ge(conv_read, 2 * i - 3)
                        act.wait_ge(conv_done, unit + 1)
                        act.activation(conv_cg[:, i % 2, :], out_ps[:, unit % 2, 0:COLS3], ACT.Copy).then_inc(cg_ready, 1)
                before = finished_unit(n - 1) if n else None
                if before is not None and before % 3 == 2:
                    c, third, _ = unit_of(before)
                    i = before // 3
                    act.wait_ge(conv_y_ready, i + 1)
                    act.dma_start(d["y_conv"][:, c, third * COLS3:(third + 1) * COLS3], conv_y[:, i % 2, :]).then_inc(conv_stored[i % 2], 16)

            before_turns(chunk_step, conv_slot, front_slot)
            act.wait_ge(samp_turned, 3)
            act.activation(z_rows, bank[2][0:NS + 2, :], ACT.Copy).then_inc(samp_copied, 1)
            front_to_head_0(front_slot)
            front_to_head_1(front_slot)
            exp_of(0, 0)
            over_turns(act, a_turn, finish)
            act.wait_ge(samp_var, 1)
            act.activation(rs1[0:NS, :], rs1[0:NS, :], ACT.Sqrt).then_inc(samp_std, 1)

        @block.vector
        def _(dve):
            done = signals(dve)
            TURN_STEPS = 17
            BLOCK_STEPS = 8
            step = lambda ins: done(ins, start_chain)

            def wide(mask):
                return mask[:, :].unsqueeze(1).broadcast_to([P, PAIRS, CHUNK])

            def chunk_step(ci, name, dst):
                def masked(step, out, mask):
                    dve.wait_ge(products.sem, products.value(ci, name))
                    dve.tensor_tensor(out[:, :, :], ps(name), wide(mask), ALU.mult).then_inc(vectors.at(step), 1)

                def plus_eye(step, out, x, x_step):
                    dve.wait_ge(vectors.sem, vectors.value(ci, x_step))
                    dve.tensor_tensor(out[:, :, :], x[:, :, :], wide(eye), ALU.add).then_inc(vectors.at(step), 1)

                def plus(step, out, own):
                    dve.wait_ge(products.sem, products.value(ci, name))
                    dve.wait_ge(vectors.sem, vectors.value(ci, own))
                    dve.tensor_tensor(out[:, :, :], ps(name), out[:, :, :], ALU.add).then_inc(vectors.at(step), 1)

                sums = {"R1": (r_, "r"), "Q1": (q_, "q"), "R2": (r_, "r1"), "Q2": (q_, "q1"), "R3": (r_, "r2"), "Q3": (q_, "q2"),
                        "Z1": (r_, "r3"), "Z": (r_, "z1")}
                if name == "U":
                    dve.wait_ge(vectors.sem, vectors.value(ci, ("s", 1)))
                    masked("ud", ud, upper_in)
                    plus_eye("r", r_, ud, "ud")
                elif name == "N":
                    masked("nd", nd, lower_in)
                    plus_eye("q", q_, nd, "nd")
                elif name == "BT":
                    dve.tensor_tensor(ue[:, :, :], ps("U"), wide(upper_out), ALU.mult).then_inc(vectors.at("ue"), 1)
                elif name in ("KA", "BR", "KR"):
                    out, mask = {"KA": (g_ka, upper), "BR": (g_br, upper_eq), "KR": (g_kr, upper_eq)}[name]
                    masked(reader[name][1], out, mask)
                elif name in sums:
                    plus(reader[name][1], *sums[name])
                elif name == "S":
                    dve.wait_ge(products.sem, products.value(ci, "S"))
                    dve.tensor_tensor(st_new[:, :, :], ps("S"), st[:, :, :], ALU.add).then_inc(vectors.at("s_sum"), 1)
                elif name == "O":
                    dve.wait_ge(products.sem, products.value(ci, "O"))
                    dve.wait_ge(vectors.sem, vectors.value(ci, "s_sum"))
                    dve.tensor_tensor(st[:, :, :], st_new[:, :, :], t.p_end[:, :, bass.ds(ci, 1)].broadcast_to([P, PAIRS, CHUNK]),
                                      ALU.mult).then_inc(vectors.at("s"), 1)

            def front_step(nb, name, ins):
                ins.then_inc(front_dve.at(name), 1)
                dve.wait_ge(front_dve.sem, front_dve.value(nb, name))
                dve.sem_inc(waited_dve, 1)

            def norm_slot(nb, s, rows):
                def per_pair(n):
                    i = PARAMS.index(n) * PAIRS
                    return t.par[:, i:i + PAIRS].unsqueeze(2).broadcast_to([P, PAIRS, P])

                of, vf, sf = flat(o), flat(vt2), flat(gn_std)
                hr, n = h[0:rows, :], slice(0, rows)
                if s == 0:
                    if rows == P:
                        dve.wait_ge(copies.sem, copies.value(nb * 2 + 2, "o"))
                    front_step(nb, "rk0", dve.tensor_tensor(flat(rk), flat(rh2), flat(ka2), ALU.mult))
                    front_step(nb, "rk", dve.tensor_tensor(rk[:, :, :], rk[:, :, :], per_pair("r_k"), ALU.mult))
                elif s == 1:
                    dve.wait_ge(front_pe.sem, front_pe.value(nb, "mean"))
                    front_step(nb, "centred", dve.scalar_tensor_tensor(out=of, in0=bank[0][:, :], scalar=-1.0 / HD, in1=of, op0=ALU.mult, op1=ALU.add))
                elif s == 2:
                    dve.wait_ge(front_pe.sem, front_pe.value(nb, "bonus"))
                    front_step(nb, "bonus", dve.tensor_tensor(vf, bank[1][:, :], vf, ALU.mult))
                elif s == 3:
                    dve.wait_ge(front_pe.sem, front_pe.value(nb, "var"))
                    front_step(nb, "var", dve.tensor_scalar(sf, bank[3][:, :], 1.0 / HD, GN_EPS, ALU.mult, ALU.add))
                elif s == 5:
                    dve.wait_ge(front_act.sem, front_act.value(nb, "gn_std"))
                    front_step(nb, "inv", dve.reciprocal(sf, sf))
                    front_step(nb, "scaled", dve.tensor_tensor(of, of, sf, ALU.mult))
                elif s == 6:
                    front_step(nb, "gain", dve.tensor_tensor(o[:, :, :], o[:, :, :], per_pair("gn_g"), ALU.mult))
                    front_step(nb, "offset", dve.tensor_tensor(o[:, :, :], o[:, :, :], per_pair("gn_b"), ALU.add))
                elif s == 7:
                    front_step(nb, "plus", dve.tensor_tensor(of, of, vf, ALU.add))
                    dve.wait_ge(front_pe.sem, front_pe.value(nb, "gate"))
                    front_step(nb, "y", dve.tensor_tensor(of, bank[2][:, :], of, ALU.mult))
                elif s == 12:
                    dve.wait_ge(h_loaded, nb * 16 + 16)
                    dve.wait_ge(front_pe.sem, front_pe.value(nb, "mix"))
                    front_step(nb, "sum", dve.scalar_tensor_tensor(out=hr, in0=hr, scalar=ALPHA, in1=flat(wide_ps[n, :, :]), op0=ALU.mult, op1=ALU.add))
                elif s == 13:
                    front_step(nb, "bn0", dve.bn_stats(st1[n, 0:6], hr[:, 0:512]))
                    front_step(nb, "bn1", dve.bn_stats(st1[n, 6:12], hr[:, 512:1024]))
                    front_step(nb, "aggr", dve.bn_aggr(mo1[n, :], st1[n, :]))
                    front_step(nb, "ln_var", dve.tensor_scalar(rs1[n, :], mo1[n, 1:2], LN_EPS, None, ALU.add))
                elif s == 14:
                    dve.wait_ge(front_act.sem, front_act.value(nb, "ln_std"))
                    front_step(nb, "ln_inv", dve.reciprocal(rs1[n, :], rs1[n, :]))
                    front_step(nb, "ln_x", dve.tensor_scalar(hr, hr, mo1[n, 0:1], rs1[n, :], ALU.subtract, ALU.mult))
                elif s == 15:
                    front_step(nb, "ln_g", dve.tensor_tensor(hr, hr, ln1_gb[n, 0, :], ALU.mult))
                    front_step(nb, "h1", dve.tensor_tensor(hr, hr, ln1_gb[n, 1, :], ALU.add))

            def top16(nb, j, rows):
                sc, rest = score_ps(j)[0:rows, 0:N_KEYS], others[0:rows, :]
                top_val, top_idx = (samp_val, samp_place) if rows == NS else (t.top_val, t.top_idx)
                val, place = top_val[0:rows, j // 2, j % 2, :], places[0:rows, :]
                dve.wait_ge(front_pe.sem, front_pe.value(nb, f"s{j}"))
                dve.sem_inc(waited_dve, 1)
                front_step(nb, f"max{j}", dve.max(val[:, 0:8], sc))
                front_step(nb, f"place{j}", dve.max_index(place[:, 0:8], val[:, 0:8], sc))
                front_step(nb, f"others{j}", dve.match_replace(rest, val[:, 0:8], sc, NEG))
                front_step(nb, f"max2_{j}", dve.max(val[:, 8:16], rest))
                front_step(nb, f"place2_{j}", dve.max_index(place[:, 8:16], val[:, 8:16], rest))
                front_step(nb, f"top{j}", dve.tensor_copy(top_idx[0:rows, j // 2, j % 2, :], place))

            def front_slot(nb, n, s):
                rows, n = rows_and_stage(nb, n)
                if n <= 4 and rows == P:
                    chunk_step(*chunk_slot(nb, n, s))
                elif (n, s) == (1, 0):
                    for dst, src in ((rh2, t.samp[:, 0]), (ka2, t.samp[:, 1]), (vt2, t.samp[:, 2])):
                        done(dve.tensor_copy(dst[:, :, 0:NS], src.rearrange("p b c -> p c b")), sample_ready)
                elif n == 5:
                    norm_slot(nb, s, rows)
                elif n in (6, 7):
                    for j in queries(n, s, 1):
                        top16(nb, j, rows)
                elif (n, s) in SAMPLE_HEADS:
                    hd = SAMPLE_HEADS[n, s]
                    step(pick_experts(dve, step, NS, samp_val[:, hd], samp_place[:, hd], k, samp_best[:, hd, :], samp_expert[:, hd, :]))
                elif (n, s) == (10, 4):
                    dve.sem_inc(samp_picked, 1)
                    done(dve.tensor_tensor(samp_ex, samp_best, samp_best[:, :, 0:1].broadcast_to([NS, H, TOPK]), ALU.subtract), samp_diff)
                elif (n, s) == (10, 5):
                    dve.wait_ge(samp_exp, 1)
                    step(dve.tensor_reduce(samp_total, samp_ex, AX_X, ALU.add))
                    step(dve.reciprocal(samp_total, samp_total))
                    done(dve.tensor_tensor(samp_ex, samp_ex, samp_total.broadcast_to([NS, H, TOPK]), ALU.mult), samp_picked)

            def pick(turn, par, head, step):
                step(pick_experts(dve, step, P, t.top_val[:, head], t.top_idx[:, head], k, best[:, par, :], idx[:, head % 4, :]))
                step(dve.tensor_scalar(neg_max[:, par, :], best[:, par, 0:1], -1.0, None, ALU.mult))
                dve.sem_inc(picked, 1)

            def counted(sem, base):
                n = [0]

                def step(ins):
                    n[0] += 1
                    ins.then_inc(sem, 1)
                    dve.wait_ge(sem, base + n[0])
                    dve.sem_inc(waited_dve, 1)
                return step, n

            def a_turn(turn, n, nb, sums=True, dots_left=True, new_block=None):
                par = n % 2
                if new_block is not None:
                    step, _ = counted(block_chain, (new_block - 1) * BLOCK_STEPS)
                    step(dve.tensor_scalar(res[:, :], x[:, :], ALPHA, None, ALU.mult))
                    take_rows(new_block)
                if not dots_left:
                    dve.wait_ge(x_samp_loaded, 16 * NS)
                    for e in range(EACH):
                        dve.wait_ge(u_landed[e], (turn * 2 + 1) * 16)
                        dve.tensor_tensor_reduce(u[:, e, :], u[:, e, :], x_samp, 1.0, 0.0, ALU.mult, ALU.add,
                                                 samp_hu[:, e:e + 1]).then_inc(dots, 1)
                    dve.wait_ge(samp_gelu, 1)
                    dve.wait_ge(samp_idx_loaded, 32)
                    dve.tensor_tensor(samp_hu[:, :], samp_hu[:, :], samp_gate[:, :], ALU.mult).then_inc(act_ready, 1)
                    return
                for s in range(TOPK):
                    dve.wait_ge(u_landed[s % RING], (turn * 2 + s // RING + 1) * 16)
                    dve.tensor_tensor_reduce(u[:, s % RING, :], u[:, s % RING, :], x[:, :], 1.0, 0.0, ALU.mult, ALU.add,
                                             hu[:, par, s:s + 1]).then_inc(dots, 1)
                    if nb is not None:
                        front_slot(nb, n, s)
                    elif n == 0 and isinstance(turn, int) and turn == 0:
                        front_rest(front_slot, s)
                step, steps = counted(turn_chain, turn * TURN_STEPS)
                dve.wait_ge(exp_ready, turn + 1)
                step(dve.reciprocal(total[:, par, :], total[:, par, :]))
                dve.wait_ge(gelu_ready, turn + 1)
                dve.scalar_tensor_tensor(out=act_v[:, par, :], in0=act_v[:, par, :], scalar=total[:, par, :], in1=ex[:, par, :],
                                         op0=ALU.mult, op1=ALU.mult).then_inc(act_ready, 1)
                if not (isinstance(turn, int) and n >= H - 2):
                    if sums:
                        dve.wait_ge(v_used, turn * TOPK - TOPK + RING)
                        dve.sem_inc(waited_dve, 1)
                    pick(turn + 2, par, (n + 2) % H, step)
                    assert steps[0] == TURN_STEPS, steps
                else:
                    dve.sem_inc(turn_chain, TURN_STEPS - steps[0])

            def take_rows(b):
                dve.wait_ge(front_pe.sem, front_pe.value(b, "turned"))
                dve.tensor_copy(x[:, :], h[:, :]).then_inc(x_taken, 1)
                dve.wait_ge(x_taken, b + 1)

            def finish(b):
                last = isinstance(b, int)
                step, n = counted(block_chain, b * BLOCK_STEPS + 1)
                if last:
                    dve.tensor_scalar(res[:, :], x[:, :], ALPHA, None, ALU.mult).then_inc(block_chain, 1)
                    dve.wait_ge(block_chain, b * BLOCK_STEPS + 1)
                dve.wait_ge(v_used, (b + 1) * (H * TOPK) + RING)
                dve.wait_ge(y_free, b + 1)
                dve.tensor_tensor(y[:, :], flat(out_ps[:, :, :]), res[:, :], ALU.add).then_inc(sum_read, 1)
                dve.wait_ge(sum_read, b + 2)
                step(dve.bn_stats(stats[:, 0:6], y[:, 0:512]))
                step(dve.bn_stats(stats[:, 6:12], y[:, 512:1024]))
                step(dve.bn_aggr(moments[:, :], stats[:, :]))
                dve.tensor_scalar(rstd[:, :], moments[:, 1:2], LN_EPS, None, ALU.add).then_inc(var_ready, 1)
                dve.wait_ge(std_ready, b + 1)
                step(dve.reciprocal(rstd[:, :], rstd[:, :]))
                step(dve.tensor_scalar(y[:, :], y[:, :], moments[:, 0:1], rstd[:, :], ALU.subtract, ALU.mult))
                step(dve.tensor_tensor(y[:, :], y[:, :], ln2_gb[:, 0, :], ALU.mult))
                dve.tensor_tensor(y[:, :], y[:, :], ln2_gb[:, 1, :], ALU.add).then_inc(y_ready, 1)
                if not last:
                    dve.sem_inc(block_chain, BLOCK_STEPS - 1 - n[0])

            done(dve.memset(st[:, :, :], 0.0), start_chain)
            vectors.start(dve)
            front_dve.start(dve)
            dve.wait_ge(consts, N_CONSTS)
            conv_step = lambda ins: done(ins, conv_chain)

            def param(n, c):
                return t.par[:, PARAMS.index(n) * PAIRS + c:PARAMS.index(n) * PAIRS + c + 1]

            def conv_slot(n):
                unit, taps = finished_unit(n), False
                if unit is None and n:
                    unit, taps = finished_unit(n - 1), True
                if unit is None:
                    return
                c, third, kind = unit_of(unit)
                i = unit // 3
                cols = slice(third * COLS3, (third + 1) * COLS3)
                y_out = conv_y[:, i % 2, :]
                product_ps = out_ps[:, unit % 2, 0:COLS3]
                lo = C_META if third == 0 else 0
                if kind == "hv" and not taps:
                    dve.wait_ge(cg_ready, i + 1)
                    dve.wait_ge(conv_done, unit + 1)
                    conv_step(dve.tensor_tensor(conv_z[:, cols], product_ps, conv_cg[:, i % 2, :], ALU.mult))
                    dve.sem_inc(conv_read, 1)
                    if third == 0:
                        conv_step(dve.memset(conv_z[:, NS:2 * NS], 0.0))
                        conv_step(dve.tensor_copy(t.z_out[:, c, 0:NS], conv_z[:, 0:NS]))
                    if third == 2:
                        conv_step(dve.tensor_copy(t.z_out[:, c, NS:NS + 2], conv_z[:, PROJ_COLS - 2:]))
                    if i >= 2:
                        dve.wait_ge(conv_stored[i % 2], 16 * (i // 2))
                    conv_step(dve.tensor_scalar(y_out, conv_z[:, cols], param("cw2", c), None, ALU.mult))
                elif kind == "hv":
                    for back, w in ((1, "cw1"), (2, "cw0")):
                        conv_step(dve.scalar_tensor_tensor(out=y_out[:, lo:], in0=conv_z[:, third * COLS3 + lo - back:(third + 1) * COLS3 - back],
                                                           scalar=param(w, c), in1=y_out[:, lo:], op0=ALU.mult, op1=ALU.add))
                    if third == 0:
                        old = t.conv_state[:, c, :].rearrange("p (b j) -> p j b", j=2)
                        for j, w in ((0, "cw0"), (1, "cw1")):
                            conv_step(dve.scalar_tensor_tensor(out=y_out[:, 0:NS], in0=old[:, j, :], scalar=param(w, c),
                                                               in1=y_out[:, 0:NS], op0=ALU.mult, op1=ALU.add))
                elif kind == "bg" and not taps:
                    dve.wait_ge(conv_done, unit + 1)
                    done(dve.tensor_tensor(y_out, product_ps, y_out, ALU.mult), conv_y_ready)
                    dve.sem_inc(conv_read, 1)

            before_turns(chunk_step, conv_slot, front_slot)
            front_to_head_0(front_slot)
            pick(0, 0, 0, step)
            front_to_head_1(front_slot)
            pick(1, 1, 1, step)
            take_rows(0)
            over_turns(dve, a_turn, finish)
            dve.wait_ge(v_used, TBLOCKS * H * TOPK + EACH + RING)
            last_step = lambda ins: done(ins, samp_end)
            last_step(dve.scalar_tensor_tensor(out=y_samp, in0=h[0:NS, :], scalar=ALPHA, in1=flat(wide_ps[0:NS, :, :]), op0=ALU.mult, op1=ALU.add))
            last_step(dve.bn_stats(st1[0:NS, 0:6], y_samp[:, 0:512]))
            last_step(dve.bn_stats(st1[0:NS, 6:12], y_samp[:, 512:1024]))
            last_step(dve.bn_aggr(mo1[0:NS, :], st1[0:NS, :]))
            done(dve.tensor_scalar(rs1[0:NS, :], mo1[0:NS, 1:2], LN_EPS, None, ALU.add), samp_var)
            dve.wait_ge(samp_std, 1)
            last_step(dve.reciprocal(rs1[0:NS, :], rs1[0:NS, :]))
            last_step(dve.tensor_scalar(y_samp, y_samp, mo1[0:NS, 0:1], rs1[0:NS, :], ALU.subtract, ALU.mult))
            last_step(dve.tensor_tensor(y_samp, y_samp, ln2_gb[0:NS, 0, :], ALU.mult))
            done(dve.tensor_tensor(y_samp, y_samp, ln2_gb[0:NS, 1, :], ALU.add), y_samp_ready)


PARAMS = ["w0", "a0", "k_k", "k_a", "r_k", "gn_g", "gn_b", "mu_r", "mu_k", "mu_v", "cw0", "cw1", "cw2"]

PAR_COLS = len(PARAMS) * PAIRS + 2


class Tiles:
    pass


def clear_semaphores(nc):
    used = sorted(nc.released_uncleared_semaphores)
    while used:
        n = 1
        while n < len(used) and used[n] == used[0] + n:
            n += 1
        nc.gpsimd.sem_clear(range(used[0], used[0] + n))
        used = used[n:]
    nc.all_engine_barrier()


def build(nc, d):
    t = Tiles()
    outer = ExitStack()
    with outer:
        sb = lambda n, s: outer.enter_context(nc.sbuf_tensor(n, s, F32))
        t.h_stored, t.spilled = (
            [outer.enter_context(nc.semaphore(f"{n}{i}")) for i in range(c)]
            for n, c in (("h_stored", 3), ("spilled", 2)))
        t.lora_spilled = outer.enter_context(nc.semaphore("lora_spilled"))
        t.samp_state_stored = outer.enter_context(nc.semaphore("samp_state_stored"))
        t.ident, t.head_ones = sb("ident", [P, P]), sb("head_ones", [P, P])
        t.par = sb("par", [P, PAR_COLS])
        t.mu_lora = t.par[:, PAR_COLS - 2:]
        t.samp = sb("samp", [P, 6, NS, PAIRS])
        t.p_end = sb("p_end", [P, PAIRS, CHUNKS])
        t.z_out = sb("z_out", [P, PAIRS, NS + 2])
        t.conv_state = sb("conv_state", [P, PAIRS, 2 * NS])
        t.rings = sb("rings", [P, 2 * RING, D])
        t.hT = t.rings[:, :, :].rearrange("p a b -> p (a b)")[:, 0:KT * PROJ_COLS].rearrange("p (k c) -> p k c", k=KT)
        t.keysT = sb("keysT", [P, HP, N_KEYS])
        t.top_val, t.top_idx = sb("top_val", [P, PEER_HEADS, 2, TOPK]), sb("top_idx", [P, PEER_HEADS, 2, TOPK])
        input_phase(nc, t, d)
        project_phase(nc, t, d)
        clear_semaphores(nc)
        steady_phase(nc, t, d)


_INS = ['x_prompt', 'x_sample', 'state_conv', 'state_shift', 'state_wkv', 'meta_tokens', 'ln_in_g', 'ln_in_b',
        'w_in', 'conv_w', 'mu', 'w0', 'w_up', 'a0', 'a_up', 'g_up', 'k_k', 'k_a', 'r_k', 'gn_g', 'gn_b', 'w_o',
        'ln1_g', 'ln1_b', 'w_q', 'sub_keys', 'peer_u', 'peer_v', 'ln2_g', 'ln2_b']
_OUTS = [("y_prompt", (1, SEQ, D)), ("y_sample", (NS, 1, D)), ("new_conv_prompt", (1, 1, 2, CONVW)),
         ("new_shift_prompt", (1, 1, D)), ("new_wkv_prompt", (1, 1, HEADS, HD, HD)),
         ("new_conv_sample", (1, NS, 2, CONVW)), ("new_shift_sample", (1, NS, D)),
         ("new_wkv_sample", (1, NS, HEADS, HD, HD))]
_SCRATCH = [("h_rows", (PROJ_COLS, D), F32), ("samp_rows", (NS * PAIRS, 2, 6, HD), F32), ("h1_rows", (NS, D), F32),
            ("operands", (5, P, PAIRS, WKV_COLS), F32), ("y_conv", (P, PAIRS, PROJ_COLS), F32), ("lora_g", (G_LORA, PROJ_COLS), F32),
            ("sp_idx", (NS, SLOTS), U32), ("sp_gate", (NS, SLOTS), F32)]


def kernel(**inputs):
    import numpy as _np
    import concourse.bacc as _bacc
    from concourse import mybir as _mybir
    from concourse.bass_utils import run_bass_kernel_spmd as _run

    nc = _bacc.Bacc("TRN2", target_bir_lowering=False, num_devices=1)
    arrays, tensors = {}, {}
    for name in _INS:
        a = _np.ascontiguousarray(inputs[name])
        arrays[f"in_{name}_dram"] = a
        tensors[name] = nc.dram_tensor(f"in_{name}_dram", a.shape, _mybir.dt.from_np(a.dtype), kind="ExternalInput").ap()
    for i, (name, shape) in enumerate(_OUTS):
        tensors[name] = nc.dram_tensor(f"out_{i}_dram", shape, _mybir.dt.float32, kind="ExternalOutput").ap()
    for name, shape, dt in _SCRATCH:
        tensors[name] = nc.dram_tensor(f"scratch_{name}", shape, dt, kind="Internal").ap()
    build(nc, tensors)
    r = _run(nc, [arrays], core_ids=[0])
    return tuple(r.results[0][f"out_{i}_dram"] for i in range(len(_OUTS)))
```
